# Optimizing a Trainium2 kernel written in Bass

```python
import jax, jax.numpy as jnp
from jax import lax
import numpy as np
import math
import jax
import jax.numpy as jnp

D_MODEL = 1024
BATCH = 1
SEQ = 256
DEPTH = 2

N_META = 16
N_A_LAYERS = DEPTH // 2
N_B_LAYERS = DEPTH - N_A_LAYERS
POOL_WINDOWS = (2, 4, 8, 16)
POOL_GROUP = D_MODEL // len(POOL_WINDOWS)
SB_HEADS = 16
SB_HEAD_DIM = D_MODEL // SB_HEADS
Q_BLOCK = 128
PEER_HEADS = 8
PEER_N_KEYS = 128
PEER_N_EXPERTS = PEER_N_KEYS * PEER_N_KEYS
PEER_TOPK = 16
PEER_QUERY_DIM = 256
PEER_HALF = PEER_QUERY_DIM // 2
PEER_CHUNK = 16
EPS = 1e-6


def rmsnorm(x, g):
    xf = x.astype(jnp.float32)
    y = xf * lax.rsqrt(jnp.mean(xf * xf, axis=-1, keepdims=True) + EPS)
    return (y * g.astype(jnp.float32)).astype(x.dtype)

def pool_mixer(h, w_pool, scale):
    L = h.shape[1]
    hf = h.astype(jnp.float32)
    pos = jnp.arange(L)
    outs = []
    for g, w in enumerate(POOL_WINDOWS):
        hg = hf[..., g * POOL_GROUP:(g + 1) * POOL_GROUP]
        c = jnp.cumsum(hg, axis=1)
        c_prev = jnp.pad(c, ((0, 0), (w, 0), (0, 0)))[:, :L]
        cnt = jnp.minimum(pos + 1, w).astype(jnp.float32)[None, :, None]
        pooled = ((c - c_prev) / cnt - hg).astype(h.dtype)
        outs.append(jnp.einsum('bsc,cd->bsd', pooled, w_pool[g]))
    return jnp.concatenate(outs, axis=-1) * scale

def stick_breaking(q, k, v):
    B, L, H, dh = q.shape
    pad = (-L) % Q_BLOCK
    Lp = L + pad
    nblk = Lp // Q_BLOCK
    pw = ((0, 0), (pad, 0), (0, 0), (0, 0))
    qb = jnp.pad(q, pw).reshape(B, nblk, Q_BLOCK, H, dh).transpose(1, 0, 3, 2, 4)
    kp = jnp.pad(k, pw).transpose(0, 2, 1, 3)
    vp = jnp.pad(v, pw).transpose(0, 2, 1, 3)
    key_pos = jnp.arange(Lp)
    key_real = key_pos >= pad
    scale = SB_HEAD_DIM ** -0.5

    def block(args):
        q_blk, i = args
        q_pos = i * Q_BLOCK + jnp.arange(Q_BLOCK)
        z = jnp.einsum('bhqd,bhkd->bhqk', q_blk, kp,
                       preferred_element_type=jnp.float32) * scale
        valid = (key_pos[None, :] < q_pos[:, None]) & key_real[None, :]
        log_keep = jnp.where(valid, jax.nn.log_sigmoid(-z), 0.0)
        after = lax.cumsum(log_keep, axis=3, reverse=True) - log_keep
        log_w = jax.nn.log_sigmoid(z) + after
        wgt = jnp.where(valid, jnp.exp(log_w), 0.0)
        return jnp.einsum('bhqk,bhkd->bqhd', wgt.astype(v.dtype), vp)

    out = lax.map(block, (qb, jnp.arange(nblk)))
    out = out.transpose(1, 0, 2, 3, 4).reshape(B, Lp, H * dh)
    return out[:, pad:]

def peer(h, w_query, sub_keys, u, v):
    B, L, D = h.shape
    nchunk = L // PEER_CHUNK
    hc = h.reshape(B, nchunk, PEER_CHUNK, D).transpose(1, 0, 2, 3)

    def chunk(hx):
        q = jnp.einsum('btd,dq->btq', hx, w_query).reshape(
            B, PEER_CHUNK, PEER_HEADS, 2, PEER_HALF)
        s = jnp.einsum('bthpc,hpnc->bthpn', q, sub_keys,
                       preferred_element_type=jnp.float32)
        top_s, top_i = lax.top_k(s, PEER_TOPK)
        cand_s = (top_s[..., 0, :, None] + top_s[..., 1, None, :]).reshape(
            B, PEER_CHUNK, PEER_HEADS, PEER_TOPK * PEER_TOPK)
        cand_i = (top_i[..., 0, :, None] * PEER_N_KEYS + top_i[..., 1, None, :]).reshape(
            B, PEER_CHUNK, PEER_HEADS, PEER_TOPK * PEER_TOPK)
        best_s, best_pos = lax.top_k(cand_s, PEER_TOPK)
        expert = jnp.take_along_axis(cand_i, best_pos, axis=-1)
        gate = jax.nn.softmax(best_s, axis=-1)
        u_sel = jnp.take(u, expert, axis=0)
        v_sel = jnp.take(v, expert, axis=0)
        act = jax.nn.gelu(jnp.einsum('btd,bthkd->bthk', hx, u_sel,
                                     preferred_element_type=jnp.float32), approximate=False)
        return jnp.einsum('bthk,bthkd->btd', (gate * act).astype(h.dtype), v_sel)

    y = lax.map(chunk, hc)
    return y.transpose(1, 0, 2, 3).reshape(B, L, D)

def first_inputs(seed: int = 0) -> dict:
    key = jax.random.key(seed)
    ks = jax.random.split(key, 16)
    f = jnp.float32
    D = D_MODEL
    nrm = lambda k, shape, s: jax.random.normal(k, shape, f) * s
    return {
        "x": jax.random.normal(ks[0], (BATCH, SEQ, D), f),
        "meta_tokens": nrm(ks[1], (N_META, D), 1.0),
        "norm_mix": 1.0 + nrm(ks[2], (DEPTH, D), 0.02),
        "norm_ffn": 1.0 + nrm(ks[3], (DEPTH, D), 0.02),
        "pool_w": nrm(ks[4], (N_A_LAYERS, len(POOL_WINDOWS), POOL_GROUP, POOL_GROUP), POOL_GROUP ** -0.5),
        "pool_scale": 0.5 + nrm(ks[5], (N_A_LAYERS, D), 0.05),
        "kv_norm": 1.0 + nrm(ks[6], (D,), 0.02),
        "w_kv": nrm(ks[7], (D, 2 * D), D ** -0.5),
        "k_norm": 1.0 + nrm(ks[8], (SB_HEAD_DIM,), 0.02),
        "w_q": nrm(ks[9], (N_B_LAYERS, D, D), D ** -0.5),
        "q_norm": 1.0 + nrm(ks[10], (N_B_LAYERS, SB_HEAD_DIM), 0.02),
        "w_o": nrm(ks[11], (N_B_LAYERS, D, D), D ** -0.5),
        "peer_wq": nrm(ks[12], (DEPTH, D, PEER_HEADS * PEER_QUERY_DIM), D ** -0.5),
        "peer_keys": nrm(ks[13], (DEPTH, PEER_HEADS, 2, PEER_N_KEYS, PEER_HALF), PEER_HALF ** -0.5),
        "peer_u": nrm(ks[14], (DEPTH, PEER_N_EXPERTS, D), D ** -0.5),
        "peer_v": nrm(ks[15], (DEPTH, PEER_N_EXPERTS, D), 0.25),
    }

def first_block(x, meta_tokens, norm_mix, norm_ffn, pool_w, pool_scale, kv_norm, w_kv, k_norm,
              w_q, q_norm, w_o, peer_wq, peer_keys, peer_u, peer_v):
    B = x.shape[0]
    meta = jnp.broadcast_to(meta_tokens[None].astype(x.dtype), (B, N_META, D_MODEL))
    h = jnp.concatenate([meta, x], axis=1)
    L = h.shape[1]
    k_sh = None
    v_sh = None
    for layer in range(DEPTH):
        hn = rmsnorm(h, norm_mix[layer])
        if layer < N_A_LAYERS:
            mix = pool_mixer(hn, pool_w[layer], pool_scale[layer])
        else:
            j = layer - N_A_LAYERS
            q = jnp.einsum('bld,de->ble', hn, w_q[j]).reshape(B, L, SB_HEADS, SB_HEAD_DIM)
            q = rmsnorm(q, q_norm[j])
            mix = jnp.einsum('ble,ed->bld', stick_breaking(q, k_sh, v_sh), w_o[j])
        h = h + mix
        h = h + peer(rmsnorm(h, norm_ffn[layer]), peer_wq[layer], peer_keys[layer],
                     peer_u[layer], peer_v[layer])
        if layer == N_A_LAYERS - 1:
            kv = jnp.einsum('bld,de->ble', rmsnorm(h, kv_norm), w_kv)
            k_sh = rmsnorm(kv[..., :D_MODEL].reshape(B, L, SB_HEADS, SB_HEAD_DIM), k_norm)
            v_sh = kv[..., D_MODEL:].reshape(B, L, SB_HEADS, SB_HEAD_DIM)
    return h[:, N_META:]


DEPTH_2 = 1

MEM_LEN = 256
MOBA_HEADS = 8
MOBA_HEAD_DIM = 64
MOBA_BLOCK = 256
MOBA_TOPK = 3
MOBA_Q_CHUNK = 32
RET_HEADS = 4
RET_QK_DIM = 128
RET_V_DIM = 128
RET_CHUNK = 128
ROPE_BASE = 10000.0
MEM_HEADS = 4
MEM_HEAD_DIM = 128
REL_BUCKETS = 32
REL_MAX_DIST = 2048
D_FF = 2816
CONV_WIDTH = 3
NEG_INF = -1e30

MOBA_W = MOBA_HEADS * MOBA_HEAD_DIM
RET_QK_W = RET_HEADS * RET_QK_DIM
RET_V_W = RET_HEADS * RET_V_DIM
MEM_W = MEM_HEADS * MEM_HEAD_DIM
IN_SIZES = (MOBA_W, MOBA_W, MOBA_W, RET_QK_W, RET_QK_W, RET_V_W, RET_V_W, MEM_W, D_MODEL, D_MODEL, D_MODEL)
IN_SPLIT_AT = tuple(int(s) for s in np.cumsum(IN_SIZES)[:-1])
D_IN = int(sum(IN_SIZES))


def rmsnorm_2(x, g):
    xf = x.astype(jnp.float32)
    y = xf * lax.rsqrt(jnp.mean(xf * xf, axis=-1, keepdims=True) + EPS)
    return (y * g.astype(jnp.float32)).astype(x.dtype)

def rel_bucket(dist):
    max_exact = REL_BUCKETS // 2
    d = jnp.maximum(dist, 0)
    df = jnp.maximum(d, 1).astype(jnp.float32)
    large = max_exact + (jnp.log(df / max_exact) / math.log(REL_MAX_DIST / max_exact)
                         * (REL_BUCKETS - max_exact)).astype(jnp.int32)
    large = jnp.minimum(large, REL_BUCKETS - 1)
    return jnp.where(d < max_exact, d, large)

def rotary(x, pos):
    half = x.shape[-1] // 2
    inv = ROPE_BASE ** (-jnp.arange(half, dtype=jnp.float32) / half)
    ang = pos.astype(jnp.float32)[:, None] * inv
    cos = jnp.cos(ang)[None, :, None, :]
    sin = jnp.sin(ang)[None, :, None, :]
    x1, x2 = x[..., :half], x[..., half:]
    return jnp.concatenate([x1 * cos - x2 * sin, x1 * sin + x2 * cos], axis=-1).astype(x.dtype)

def moba_attention(q, k, v, rel_bias):
    B, S, H, dh = q.shape
    nb = -(-S // MOBA_BLOCK)
    s_pad = nb * MOBA_BLOCK
    n_sel = min(MOBA_TOPK, nb)
    qc_len = MOBA_Q_CHUNK
    scale = dh ** -0.5
    q = q.transpose(0, 2, 1, 3)
    pad = ((0, 0), (0, 0), (0, s_pad - S), (0, 0))
    k = jnp.pad(k.transpose(0, 2, 1, 3), pad)
    v = jnp.pad(v.transpose(0, 2, 1, 3), pad)
    kb = k.reshape(B, H, nb, MOBA_BLOCK, dh)
    vb = v.reshape(B, H, nb, MOBA_BLOCK, dh)
    k_mean = jnp.mean(kb.astype(jnp.float32), axis=3)

    pos = jnp.arange(S)
    fully_past = jnp.arange(nb)[None, :] < (pos // MOBA_BLOCK)[:, None]
    gate = jnp.einsum('bhsd,bhnd->bhsn', q.astype(jnp.float32), k_mean)
    gate = jnp.where(fully_past, gate, NEG_INF)
    _, sel = lax.top_k(gate, n_sel)

    table = rel_bias.T.astype(jnp.float32)
    b_idx = jnp.arange(B)[:, None, None, None]
    h_idx = jnp.arange(H)[None, :, None, None]
    blk_off = jnp.arange(MOBA_BLOCK)

    def query_chunk(ci):
        c0 = ci * qc_len
        q_pos = c0 + jnp.arange(qc_len)
        blk = c0 // MOBA_BLOCK
        q_c = lax.dynamic_slice_in_dim(q, c0, qc_len, axis=2)
        sel_c = lax.dynamic_slice_in_dim(sel, c0, qc_len, axis=2)
        k_sel = kb[b_idx, h_idx, sel_c]
        v_sel = vb[b_idx, h_idx, sel_c]
        sel_pos = sel_c[..., None] * MOBA_BLOCK + blk_off
        s_sel = jnp.einsum('bhqd,bhqknd->bhqkn', q_c, k_sel).astype(jnp.float32) * scale
        s_sel = s_sel + table[h_idx[..., None], rel_bucket(q_pos[:, None, None] - sel_pos)]
        s_sel = jnp.where((sel_c < blk)[..., None], s_sel, NEG_INF)
        own_start = blk * MOBA_BLOCK
        k_own = lax.dynamic_slice_in_dim(k, own_start, MOBA_BLOCK, axis=2)
        v_own = lax.dynamic_slice_in_dim(v, own_start, MOBA_BLOCK, axis=2)
        d_own = q_pos[:, None] - (own_start + blk_off)[None, :]
        s_own = (jnp.einsum('bhqd,bhnd->bhqn', q_c, k_own).astype(jnp.float32) * scale
                 + table[:, rel_bucket(d_own)])
        s_own = jnp.where(d_own >= 0, s_own, NEG_INF)
        logits = jnp.concatenate([s_sel.reshape(B, H, qc_len, n_sel * MOBA_BLOCK), s_own], axis=-1)
        p = jax.nn.softmax(logits, axis=-1).astype(v.dtype)
        p_sel = p[..., :n_sel * MOBA_BLOCK].reshape(B, H, qc_len, n_sel, MOBA_BLOCK)
        p_own = p[..., n_sel * MOBA_BLOCK:]
        return (jnp.einsum('bhqkn,bhqkne->bhqe', p_sel, v_sel)
                + jnp.einsum('bhqn,bhne->bhqe', p_own, v_own))

    out = lax.map(query_chunk, jnp.arange(S // qc_len))
    return out.transpose(1, 0, 3, 2, 4).reshape(B, S, H * dh)

def retention(q, k, v, g, gn_gain):
    B, S, H, dk = q.shape
    dv = v.shape[-1]
    C = RET_CHUNK
    N = S // C
    pos = jnp.arange(S)
    q = rotary(q, pos)
    k = rotary(k, pos) * (dk ** -0.5)
    log_gamma = jnp.log1p(-jnp.power(2.0, -5.0 - jnp.arange(H, dtype=jnp.float32)))
    i = jnp.arange(C, dtype=jnp.float32)
    diff = i[:, None] - i[None, :]
    decay = jnp.where(diff >= 0, jnp.exp(log_gamma[:, None, None] * jnp.maximum(diff, 0.0)), 0.0)
    q_in = jnp.exp(log_gamma[:, None] * (i + 1.0))
    k_out = jnp.exp(log_gamma[:, None] * (C - 1.0 - i))
    chunk_decay = jnp.exp(log_gamma * C)

    def to_chunks(t):
        return t.reshape(B, N, C, H, t.shape[-1]).transpose(0, 3, 1, 2, 4)
    qc, kc, vc = to_chunks(q), to_chunks(k), to_chunks(v)
    scores = jnp.einsum('bhncd,bhnjd->bhncj', qc, kc) * decay[None, :, None]
    inner = jnp.einsum('bhncj,bhnje->bhnce', scores, vc)
    kv = jnp.einsum('bhnjd,bhnje->nbhde', kc * k_out[None, :, None, :, None], vc).astype(jnp.float32)

    def step(state, kv_n):
        return chunk_decay[None, :, None, None] * state + kv_n, state
    _, prev = lax.scan(step, jnp.zeros((B, H, dk, dv), jnp.float32), kv)
    cross = jnp.einsum('bhncd,nbhde->bhnce', qc * q_in[None, :, None, :, None], prev)
    y = (inner + cross).astype(jnp.float32).transpose(0, 2, 3, 1, 4).reshape(B, S, H, dv)
    mu = jnp.mean(y, axis=-1, keepdims=True)
    var = jnp.mean(jnp.square(y - mu), axis=-1, keepdims=True)
    yn = ((y - mu) * lax.rsqrt(var + EPS)).reshape(B, S, H * dv) * gn_gain.astype(jnp.float32)
    return (yn * jax.nn.silu(g.astype(jnp.float32))).astype(v.dtype)

def memory_attention(q, mem_n, w_mem_kv):
    B, S, H, dh = q.shape
    M = mem_n.shape[1]
    k, v = jnp.split(mem_n @ w_mem_kv, 2, axis=-1)
    k = k.reshape(B, M, H, dh)
    v = v.reshape(B, M, H, dh)
    s = jnp.einsum('bshd,bmhd->bhsm', q, k).astype(jnp.float32) * (dh ** -0.5)
    p = jax.nn.softmax(s, axis=-1).astype(v.dtype)
    return jnp.einsum('bhsm,bmhd->bshd', p, v).reshape(B, S, H * dh)

def conv_ffn(x, w_up, conv_w, conv_b, w_down):
    h = x @ w_up
    c = h.shape[-1]
    h = lax.conv_general_dilated(
        h, conv_w.reshape(CONV_WIDTH, 1, c).astype(h.dtype), window_strides=(1,),
        padding=[(CONV_WIDTH - 1, 0)], dimension_numbers=('NWC', 'WIO', 'NWC'),
        feature_group_count=c) + conv_b
    gate, up = jnp.split(h, 2, axis=-1)
    return (jax.nn.gelu(gate, approximate=False) * up) @ w_down

def second_inputs(seed: int = 0) -> dict:
    key = jax.random.key(seed)
    ks = jax.random.split(key, 18)
    f32 = jnp.float32
    L = DEPTH_2

    def dense(k, shape, fan_in):
        return jax.random.normal(k, shape, f32) * fan_in ** -0.5

    def gain(k, shape):
        return 1.0 + 0.02 * jax.random.normal(k, shape, f32)

    return {
        "x": jax.random.normal(ks[0], (BATCH, SEQ, D_MODEL), f32),
        "mem": jax.random.normal(ks[1], (BATCH, MEM_LEN, D_MODEL), f32),
        "g_mix": gain(ks[2], (L, D_MODEL)),
        "w_in": dense(ks[3], (L, D_MODEL, D_IN), D_MODEL),
        "rel_bias": 0.5 * jax.random.normal(ks[4], (REL_BUCKETS, MOBA_HEADS), f32),
        "ret_gn_gain": gain(ks[5], (L, RET_V_W)),
        "g_mem": gain(ks[6], (L, D_MODEL)),
        "w_mem_kv": dense(ks[7], (L, D_MODEL, 2 * MEM_W), D_MODEL),
        "w_br_attn": dense(ks[8], (L, MOBA_W, D_MODEL), MOBA_W),
        "w_br_ret": dense(ks[9], (L, RET_V_W, D_MODEL), RET_V_W),
        "w_br_mem": dense(ks[10], (L, MEM_W, D_MODEL), MEM_W),
        "w_out": dense(ks[11], (L, D_MODEL, D_MODEL), D_MODEL),
        "g_ffn": gain(ks[12], (L, D_MODEL)),
        "w_up": dense(ks[13], (L, D_MODEL, 2 * D_FF), D_MODEL),
        "conv_w": dense(ks[14], (L, CONV_WIDTH, 2 * D_FF), CONV_WIDTH),
        "conv_b": 0.02 * jax.random.normal(ks[15], (L, 2 * D_FF), f32),
        "w_down": dense(ks[16], (L, D_FF, D_MODEL), D_FF),
        "g_final": gain(ks[17], (D_MODEL,)),
    }

def second_block(x, mem, g_mix, w_in, rel_bias, ret_gn_gain, g_mem, w_mem_kv, w_br_attn, w_br_ret,
              w_br_mem, w_out, g_ffn, w_up, conv_w, conv_b, w_down, g_final):
    B, S, _ = x.shape
    h = x
    for l in range(DEPTH_2):
        n = rmsnorm_2(h, g_mix[l])
        (q_a, k_a, v_a, q_r, k_r, v_r, g_r, q_m, z_a, z_r, z_m) = jnp.split(n @ w_in[l], IN_SPLIT_AT, axis=-1)
        y_a = moba_attention(q_a.reshape(B, S, MOBA_HEADS, MOBA_HEAD_DIM),
                             k_a.reshape(B, S, MOBA_HEADS, MOBA_HEAD_DIM),
                             v_a.reshape(B, S, MOBA_HEADS, MOBA_HEAD_DIM), rel_bias)
        y_r = retention(q_r.reshape(B, S, RET_HEADS, RET_QK_DIM),
                        k_r.reshape(B, S, RET_HEADS, RET_QK_DIM),
                        v_r.reshape(B, S, RET_HEADS, RET_V_DIM), g_r, ret_gn_gain[l])
        y_m = memory_attention(q_m.reshape(B, S, MEM_HEADS, MEM_HEAD_DIM),
                               rmsnorm_2(mem, g_mem[l]), w_mem_kv[l])
        merged = (jax.nn.sigmoid(z_a) * (y_a @ w_br_attn[l])
                  + jax.nn.sigmoid(z_r) * (y_r @ w_br_ret[l])
                  + jax.nn.sigmoid(z_m) * (y_m @ w_br_mem[l]))
        h = h + merged @ w_out[l]
        h = h + conv_ffn(rmsnorm_2(h, g_ffn[l]), w_up[l], conv_w[l], conv_b[l], w_down[l])
    return rmsnorm_2(h, g_final)


def setup_inputs(seed=0):
    out = dict(first_inputs(seed))
    for name, value in second_inputs(seed + 1).items():
        if name != "x":
            out[name + "_2"] = value
    return out


def reference(
    x, meta_tokens, norm_mix, norm_ffn, pool_w, pool_scale, kv_norm, w_kv, k_norm, w_q, q_norm,
    w_o, peer_wq, peer_keys, peer_u, peer_v, mem_2, g_mix_2, w_in_2, rel_bias_2, ret_gn_gain_2,
    g_mem_2, w_mem_kv_2, w_br_attn_2, w_br_ret_2, w_br_mem_2, w_out_2, g_ffn_2, w_up_2,
    conv_w_2, conv_b_2, w_down_2, g_final_2,
):
    x = first_block(
        x, meta_tokens, norm_mix, norm_ffn, pool_w, pool_scale, kv_norm, w_kv, k_norm, w_q,
        q_norm, w_o, peer_wq, peer_keys, peer_u, peer_v,
    )
    return second_block(
        x, mem_2, g_mix_2, w_in_2, rel_bias_2, ret_gn_gain_2, g_mem_2, w_mem_kv_2, w_br_attn_2,
        w_br_ret_2, w_br_mem_2, w_out_2, g_ffn_2, w_up_2, conv_w_2, conv_b_2, w_down_2,
        g_final_2,
    )


_drawn_inputs = setup_inputs


def setup_inputs(seed=0):
    import zlib

    import numpy as np

    out = dict(_drawn_inputs(seed))
    spreads = {}
    factors = {'kv_norm': 2.816,
     'k_norm': 5.648,
     'q_norm': 5.212,
     'g_mix_2': 4.879,
     'ret_gn_gain_2': 8.0,
     'g_mem_2': 8.0,
     'g_ffn_2': 14.77,
     'conv_b_2': 15.024,
     'g_final_2': 8.096,
     'rel_bias_2': 3.389}
    for name, (base, spread) in spreads.items():
        noise = np.random.default_rng([zlib.crc32(name.encode()), seed]).standard_normal(out[name].shape)
        drawn = base * np.exp(spread * noise) if base else spread * noise
        out[name] = jnp.asarray(drawn.astype(out[name].dtype))
    for name, factor in factors.items():
        out[name] = (out[name] * factor).astype(out[name].dtype)
    return out
```

```python
from contextlib import ExitStack

import numpy as np

import concourse.bass as bass
from concourse import mybir

D = 1024
SEQ = 256
META = 16
LTOK = SEQ + META
DC = D // 128
EPS = 1e-6
NEG = -1e30
EXPERTS = 128 * 128
PEER_H = 8
TOPK = 16
DFF = 2816
FFC = DFF // 128
RET_DK = 128

R = 8
NU = 4
NV = 8
GB = 32
SLOTS = PEER_H * TOPK

TILES = [(0, 128), (128, 128), (256, META)]

UNITS = [("pool", 2), ("wq0", 16), ("keys0", 2), ("kv_k", 8), ("kv_v", 8), ("w_q", 8), ("w_o", 8),
         ("wq1", 16), ("keys1", 2), ("mem_k", 4), ("mem_v", 4), ("in_T", 20), ("in_v", 12), ("in_z", 24),
         ("br", 12), ("out", 8), ("up", 44), ("down", 22)]
N_UNITS = sum(n for _, n in UNITS)

COL = {}
_at = 0
for _name, _n in [("mix0", 8), ("mix1", 8), ("kvn", 8), ("gmix", 8), ("gmem", 8), ("gffn", 8),
                  ("knorm", 1), ("qnorm", 1), ("convb", 44), ("convw", 132)]:
    COL[_name] = _at
    _at += _n
NCOL = _at

CST = {}
_at = 0
for _name, _n in [("ident", 128), ("tri", 128), ("ones", 128), ("iota", 16), ("sel", 16), ("strict", 384)]:
    CST[_name] = _at
    _at += _n
NCST = _at
CS2 = {}
_at = 0
for _name, _n in [("swap", 128), ("flip", 128), ("cosq", 256), ("sinq", 256), ("cosk", 256), ("sink", 256),
                  ("decay", 4 * 384), ("bucket", 384), ("future", 384)]:
    CS2[_name] = _at
    _at += _n
NCS2 = _at


def program(nc, xin, metain, units, cols, cst, cs2, poolm, bc_rows, peer_u, peer_v, mem, rel, out):
    fp32 = mybir.dt.float32
    bf16 = mybir.dt.bfloat16
    u32 = mybir.dt.uint32
    ALU = mybir.AluOpType
    ACT = mybir.ActivationFunctionType
    AX = mybir.AxisListType.X
    ds = bass.ds

    ctx = ExitStack()
    with ctx:
        def sb(name, shape, dt=fp32):
            return ctx.enter_context(nc.sbuf_tensor(name, shape, dt))

        sems = {}

        def S(name):
            if name not in sems:
                sems[name] = ctx.enter_context(nc.semaphore(name))
            return sems[name]

        h = sb("h", [128, 3, D])
        hn = sb("hn", [128, 3, D])
        xT = sb("xT", [128, DC, LTOK])
        wring = sb("wring", [128, R, 1024])
        colc = sb("colc", [128, NCOL])
        cstc = sb("cstc", [128, NCST])
        ss = sb("ss", [128, 32])
        rs = sb("rs", [128, 32])
        zb = sb("zb", [128, 512], bf16)
        bcF = sb("bcF", [128, 2, D])
        hsum = sb("hsum", [128, 48])
        nmx = sb("nmx", [128, 16])

        def cc(name, n, p=128):
            return cstc[0:p, CST[name]:CST[name] + n]

        ident = cc("ident", 128)

        def gcol(name, i=0):
            return colc[:, COL[name] + i:COL[name] + i + 1]

        def gains(name, n):
            return colc[:, COL[name]:COL[name] + DC].unsqueeze(2).to_broadcast([128, DC, n])

        A1W = (NU + NV) * 1024
        a1 = sb("a1", [128, A1W])
        ug = a1[:, 0:NU * 1024].rearrange("p (n d) -> p n d", d=1024)
        vg = a1[:, NU * 1024:A1W].rearrange("p (n d) -> p n d", d=1024)
        A2W = 13500
        a2 = sb("a2", [128, A2W])
        free2 = [0]

        def take2(n, at=None):
            if at is None:
                at = free2[0]
                free2[0] += n
            assert at + n <= A2W, (at, n)
            return a2[:, at:at + n]

        qT = take2(16 * LTOK).rearrange("p (j t) -> p j t", t=LTOK)
        s_sb = [take2(2048), take2(2048)]
        oh = take2(2048)
        s_m = take2(256)
        hnm = take2(1024)
        tv = take2(256)
        tif = take2(256)
        bv = take2(128)
        sel_a = take2(128)
        sel_b = take2(128)
        ia = take2(128)
        ib = take2(128)
        gates = [take2(128) for _ in range(3)]
        gm = take2(8)
        gs = take2(8)
        ti = sb("ti", [128, 256], u32)
        bp = sb("bp", [128, 128], u32)
        pab = sb("pab", [128, 2, 128], u32)
        eidx = sb("eidx", [128, 3, 128], u32)
        ixc = sb("ixc", [128, 2, 16], u32)
        dots = sb("dots", [128, 8])
        gel = sb("gel", [128, 8])
        diag = sb("diag", [128, 4, 128])

        poolP = a1[:, 0:4 * 3 * LTOK].rearrange("p (g s t) -> p g s t", g=4, s=3)
        bcP = a1[:, 4096:5120]
        free2[0] = 0
        kT = take2(DC * LTOK).rearrange("p (c t) -> p c t", t=LTOK)
        vk = take2(3 * D).rearrange("p (s d) -> p s d", d=D)
        qhT = take2(DC * SEQ).rearrange("p (c t) -> p c t", t=SEQ)
        oT = take2(DC * SEQ).rearrange("p (c t) -> p c t", t=SEQ)
        sq = take2(D)
        st0 = a1[:, 0:2 * 5 * 640].rearrange("p (b k n) -> p b k n", b=2, k=5)
        free2[0] = 0
        qkT = take2(20 * SEQ).rearrange("p (j t) -> p j t", t=SEQ)
        vtok = take2(3 * 1024).rearrange("p (k t d) -> p k t d", k=3, t=2)
        biasT = take2(8 * 256).rearrange("p (h y) -> p h y", y=256)
        yT = take2(3 * 1024).rearrange("p (k c t) -> p k c t", k=3, c=4)
        zs = a1[:, 0:3 * 2048].rearrange("p (k t d) -> p k t d", k=3, t=2)
        kmT = a1[:, 6144:7168].rearrange("p (j t) -> p j t", t=SEQ)
        vmem = a1[:, 7168:8192].rearrange("p (t d) -> p t d", t=2)
        pw = a1[:, 8192:8192 + 2048].rearrange("p (b n) -> p b n", b=2)
        mrg = a1[:, 10240:12288].rearrange("p (t d) -> p t d", t=2)
        cs2c = sb("cs2c", [128, NCS2])
        bcG = sb("bcG", [128, 512])
        tsb = sb("tsb", [128, 32])
        aT = a2[:, 0:FFC * SEQ].rearrange("p (j t) -> p j t", t=SEQ)
        up_in = a2[:, 5632:5632 + 2 * 2 * 258].rearrange("p (b k t) -> p b k t", b=2, k=2)
        up_cv = a2[:, 6720:6720 + 2 * 2 * 256].rearrange("p (b k t) -> p b k t", b=2, k=2)
        bcL = a1[:, 0:1024]
        oh2 = sb("rot_tmp", [128, 512])

        ps = ctx.enter_context(nc.psum_tensor("ps", [128, 8, 512], fp32))
        trev_d = nc.dram_tensor("trev_scratch", [8, 384], fp32, kind="Internal").ap()

        def ps2(b, p=128):
            return ps[0:p, b:b + 2, :].rearrange("p a n -> p (a n)")

        U0, n_ = {}, 0
        for name, n in UNITS:
            U0[name] = n_
            n_ += n

        AT, n_ = {}, [0, 0, 0, 0]
        for tag, *k in [("n0", 3, 1, 3, 0), ("f0", 3, 1, 3, 3), ("kv", 3, 1, 3, 3), ("kh", 0, 1, 3, 3),
                        ("n1", 2, 1, 2, 2), ("qh", 0, 1, 2, 2), ("f1", 2, 1, 2, 2), ("nm", 2, 1, 2, 2),
                        ("n2", 2, 1, 2, 2), ("ry", 0, 1, 0, 0), ("yr", 0, 0, 2, 2), ("mg", 0, 0, 2, 2),
                        ("n3", 2, 1, 2, 2), ("n4", 2, 1, 0, 0)]:
            AT[tag] = tuple(n_)
            n_ = [a + b for a, b in zip(n_, k)]

        def tk_number(l, t):
            return [(0, 2), (0, 0), (0, 1), (1, 0), (1, 1)].index((l, t)) + 1

        block = ctx.enter_context(nc.Block())

        @block.sync
        def _(sp):
            for t, (c0, P) in enumerate(TILES[:2]):
                sp.dma_start(h[:, t, :], xin[c0:c0 + P, :]).then_inc(S("ld_h"), 16)
            sp.dma_start(h[0:META, 2, :], metain).then_inc(S("ld_h"), 16)
            sp.dma_start(cstc[:, :], cst).then_inc(S("ld_c"), 16)
            sp.dma_start(colc[:, :], cols).then_inc(S("ld_c"), 16)
            sp.dma_start(poolP.rearrange("p g s t -> p (g s t)"), poolm).then_inc(S("ld_c"), 16)
            sp.dma_start(bcP, bc_rows[2:3, :].to_broadcast([128, D])).then_inc(S("ld_c"), 16)
            for l in range(2):
                sp.dma_start(bcF[:, l, :], bc_rows[l:l + 1, :].to_broadcast([128, D])).then_inc(S("ld_c"), 16)
            for n in range(R):
                sp.dma_start(wring[:, n, :], units[n, :, :]).then_inc(S(f"w{n}"), 16)
            with sp.Fori(1, N_UNITS // R) as i:
                for s in range(R):
                    sp.wait_ge(S("w_used"), R * i + (s + 1 - R))
                    sp.dma_start(wring[:, s, :], units[ds(R * i + s, 1), :, :].rearrange("o p n -> (o p) n"))\
                        .then_inc(S(f"w{s}"), 16)
            for n in range(N_UNITS // R * R, N_UNITS):
                sp.wait_ge(S("w_used"), n + 1 - R)
                sp.dma_start(wring[:, n % R, :], units[n, :, :]).then_inc(S(f"w{n % R}"), 16)
            for t in range(2):
                sp.wait_ge(S("fin"), t + 1)
                sp.dma_start(out[t * 128:(t + 1) * 128, :], hn[:, t, :]).then_inc(S("stored"), 16)
            sp.wait_ge(S("stored"), 32)

        def gathers(l):
            base = 0 if l == 0 else 16 + 2 * SLOTS
            if l == 0:
                return [(2, 0), (0, 16), (1, 16 + SLOTS)]
            return [(0, base), (1, base + SLOTS)]

        @block.gpsimd
        def _(g):
            g.memset(zb[:, :], 0.0).then_inc(S("zb"), 1)
            g.memset(ss[:, :], 1.0).then_inc(S("zb"), 1)
            g.memset(hsum[:, :], 1.0).then_inc(S("zb"), 1)
            n_idx = [0]

            def indices(half, src):
                g.tensor_copy(ixc[:, half, :], src).then_inc(S("ixc"), 1)

            def slot(l, k, n, half, col):
                if not isinstance(n, int) or n >= NU:
                    g.wait_ge(S("dot"), n + (1 - NU))
                    g.sem_inc(S("u_go"), 1)
                g.indirect_dma_start(ug[:, k % NU, :], None, peer_u,
                                     bass.IndirectOffsetOnAxis(ap=ixc[:, half, col:col + 1], axis=0))\
                    .then_inc(S(f"u{k % NU}"), 16)
                if not isinstance(n, int) or n >= NV:
                    g.wait_ge(S("vsum"), n + (1 - NV))
                    g.sem_inc(S("v_go"), 1)
                g.indirect_dma_start(vg[:, k % NV, :], None, peer_v,
                                     bass.IndirectOffsetOnAxis(ap=ixc[:, half, col:col + 1], axis=0))\
                    .then_inc(S(f"v{k % NV}"), 16)

            for l in range(2):
                for t, base in gathers(l):
                    g.wait_ge(S("eidx"), tk_number(l, t))
                    if l == 1 and t == 0:
                        g.wait_ge(S("o_ev"), 16)
                    if t == 2:
                        indices(1, eidx[:, t, 0:16])
                        n_idx[0] += 1
                        g.wait_ge(S("ixc"), n_idx[0])
                        for k in range(16):
                            slot(l, k, base + k, 1, k)
                        continue
                    done = n_idx[0]
                    with g.Fori(0, SLOTS // GB) as i:
                        for half in range(2):
                            indices(half, eidx[:, t, ds(i * GB + 16 * half, 16)])
                            g.wait_ge(S("ixc"), 2 * i + (done + half + 1))
                            for kk in range(16):
                                k = 16 * half + kk
                                slot(l, k, GB * i + (base + k), half, kk)
                    n_idx[0] += 2 * (SLOTS // GB)
            g.wait_ge(S("vsum"), 16 + 4 * SLOTS)
            g.wait_ge(S("y1"), 2)
            for t in range(2):
                g.dma_start(mrg[:, t, :], mem[t * 128:(t + 1) * 128, :]).then_inc(S("ld_m"), 16)
            g.dma_start(cs2c[:, :], cs2).then_inc(S("ld_m"), 16)
            g.dma_start(bcG[:, :], bc_rows[3:4, 0:512].to_broadcast([128, 512])).then_inc(S("ld_m"), 16)
            g.dma_start(tsb[0:32, 0:8], rel).then_inc(S("ld_m"), 16)
            g.wait_ge(S("trev_sb"), 1)
            g.dma_start(trev_d, pw[0:8, 0, 0:384]).then_inc(S("trev_d"), 16)
            g.wait_ge(S("trev_d"), 16)
            rows = bass.AP(trev_d.tensor, 0, [[1, 128], [384, 8], [1, 256]])
            g.dma_start(pw.rearrange("p b n -> p (b n)").rearrange("p (h y) -> p h y", y=256), rows)\
                .then_inc(S("ld_b"), 16)
            g.wait_ge(S("out_h"), 2)
            g.dma_start(bcL, bc_rows[4:5, :].to_broadcast([128, D])).then_inc(S("ld_g"), 16)

        @block.tensor
        def _(pe):
            owed = {}

            def claim(*banks):
                for b in banks:
                    if b in owed:
                        pe.wait_ge(*owed.pop(b))

            def owe(sem, val, *banks):
                for b in banks:
                    owed[b] = (S(sem), val)

            unit_n = [0]

            def unit():
                n = unit_n[0]
                unit_n[0] += 1
                pe.wait_ge(S(f"w{n % R}"), 16 * (n // R + 1))
                return wring[:, n % R, :]

            def used(ins):
                ins.then_inc(S("w_used"), 1)

            def transposes(tag, src, tiles, chunks=DC):
                for n, t in enumerate(tiles):
                    P = TILES[t][1]
                    pe.wait_ge(S("x_ready"), AT[tag][2] + n + 1)
                    claim(6, 7)
                    for c in range(chunks):
                        last = nc.tensor.transpose(ps2(6)[:, c * 128:c * 128 + P],
                                                   src(t)[:, c * 128:(c + 1) * 128], ident[0:P, 0:P])
                    last.then_inc(S("turned"), 1)
                    owe("turned_out", AT[tag][3] + n + 1, 6, 7)

            def tokens_out(lhs, tiles, chunks, reader, b0=0):
                for n, t in enumerate(tiles):
                    claim(b0 + 2 * n, b0 + 2 * n + 1)
                for c in range(chunks):
                    w = unit()
                    for n, t in enumerate(tiles):
                        c0, P = TILES[t]
                        for j in range(2):
                            last = nc.tensor.matmul(ps[0:P, b0 + 2 * n + j, :], lhs(c, c0, P),
                                                    w[:, j * 512:(j + 1) * 512], start=c == 0, stop=c == chunks - 1)
                    used(last)
                for n, t in enumerate(tiles):
                    owe(reader, n + 1, b0 + 2 * n, b0 + 2 * n + 1)

            def cols_out(J, N, reader, banks, first=0):
                for j in range(J):
                    w = unit()
                    b = banks[j % len(banks)]
                    claim(b)
                    for c in range(DC):
                        last = nc.tensor.matmul(ps[:, b, 0:N], w[:, c * 128:(c + 1) * 128], xT[:, c, 0:N],
                                                start=c == 0, stop=c == DC - 1)
                    used(last)
                    owe(reader, first + j + 1, b)

            def x_at(c, c0, P):
                return xT[:, c, c0:c0 + P]

            pe.wait_ge(S("ld_c"), 96)
            pe.wait_ge(S("zb"), 3)
            pe.wait_ge(S("x_ready"), AT["n0"][2] + 3)
            for c in range(DC):
                b = c % 6
                claim(b)
                for s, (c0, P) in enumerate(TILES):
                    last = nc.tensor.matmul(ps[:, b, 0:LTOK], hn[0:P, s, c * 128:(c + 1) * 128],
                                            poolP[0:P, c // 2, s, :], start=s == 0, stop=s == 2)
                last.then_inc(S("pool_pe"), 1)
                owe("pool_ev", c + 1, b)
            pe.wait_ge(S("pool_ev"), DC)
            claim(0, 1, 2, 3, 4, 5)
            for u in range(2):
                w = unit()
                for t, (c0, P) in enumerate(TILES):
                    for g in range(2):
                        for c in range(2):
                            last = nc.tensor.matmul(ps[0:P, 2 * t + u, g * 256:(g + 1) * 256],
                                                    xT[:, 4 * u + 2 * g + c, c0:c0 + P],
                                                    w[:, (2 * g + c) * 256:(2 * g + c + 1) * 256],
                                                    start=c == 0, stop=c == 1)
                used(last)
            for t in range(3):
                owe("mix0_ps", t + 1, 2 * t, 2 * t + 1)

            def peer(l):
                tiles = [0, 1, 2] if l == 0 else [0, 1]
                N = LTOK if l == 0 else SEQ
                transposes(f"f{l}", lambda t: hn[0:TILES[t][1], t, :], tiles)
                pe.wait_ge(S("turned_out"), AT[f"f{l}"][3] + len(tiles))
                cols_out(16, N, f"q{l}_ev", range(6))
                pe.wait_ge(S(f"q{l}_ev"), 16)
                ks = [unit(), unit()]
                for n, t in enumerate([2, 0, 1] if l == 0 else [0, 1]):
                    c0, P = TILES[t]
                    claim(0, 1, 2, 3)
                    for j in range(16):
                        last = nc.tensor.matmul(ps[0:P, j // 4, (j % 4) * 128:(j % 4 + 1) * 128],
                                                qT[:, j, c0:c0 + P], ks[j // 8][:, (j % 8) * 128:(j % 8 + 1) * 128],
                                                start=True, stop=True)
                    last.then_inc(S(f"sc{l}_pe"), 1)
                    owe(f"sc{l}_ev", n + 1, 0, 1, 2, 3)
                claim(7)
                for _ in ks:
                    used(nc.tensor.matmul(ps[0:1, 7, 0:2], zb[:, 0:1], zb[:, 0:2], start=True, stop=True))
                for m, (t, base) in enumerate(gathers(l)):
                    P = TILES[t][1]
                    b = 2 * t
                    claim(b, b + 1)
                    for j in range(2):
                        nc.tensor.matmul(ps[0:P, b + j, :], zb[:, 0:P], zb[:, :], start=True, stop=False)

                    def slot(k, n, vfill):
                        pe.wait_ge(S("diag"), n + 1)
                        pe.wait_ge(S(f"v{k % NV}"), vfill)
                        for j in range(2):
                            last = nc.tensor.matmul(ps[0:P, b + j, :], diag[:, k % 4, 0:P],
                                                    vg[:, k % NV, j * 512:(j + 1) * 512], start=False, stop=False)
                        last.then_inc(S("vsum"), 1)

                    if t == 2:
                        for k in range(16):
                            slot(k, base + k, 16 * ((base + k) // NV + 1))
                    else:
                        with pe.Fori(0, SLOTS // GB) as i:
                            for k in range(GB):
                                slot(k, GB * i + (base + k), 16 * (GB // NV) * i + 16 * ((base + k) // NV + 1))
                    for j in range(2):
                        last = nc.tensor.matmul(ps[0:P, b + j, :], ident[0:P, 0:P],
                                                h[0:P, t, j * 512:(j + 1) * 512], start=False, stop=True)
                    last.then_inc(S(f"y{l}_pe"), 1)
                    owe(f"y{l}", m + 1, b, b + 1)

            peer(0)
            transposes("kv", lambda t: hn[0:TILES[t][1], t, :], [0, 1, 2])
            pe.wait_ge(S("turned_out"), AT["kv"][3] + 3)
            tokens_out(x_at, [0, 1, 2], DC, "k_ev")
            tokens_out(x_at, [0, 1, 2], DC, "v_ev")
            transposes("kh", lambda t: hn[0:TILES[t][1], t, :], [0, 1, 2])
            transposes("n1", lambda t: hn[0:128, t, :], [0, 1])
            pe.wait_ge(S("turned_out"), AT["n1"][3] + 2)
            tokens_out(x_at, [0, 1], DC, "q_ev")
            transposes("qh", lambda t: hn[0:128, t, :], [0, 1])
            pe.wait_ge(S("turned_out"), AT["qh"][3] + 2)
            pe.wait_ge(S("turned_out"), AT["kh"][3] + 3)
            pe.wait_ge(S("v_ev"), 3)

            def stick_z(hd):
                c, r = hd // 2, slice(64 * (hd % 2), 64 * (hd % 2) + 64)
                b = 2 * (hd % 2)
                claim(b, b + 1)
                nc.tensor.matmul(ps[:, b, 0:256], kT[r, c, 0:128], qhT[r, c, :], start=True, stop=True)
                nc.tensor.matmul(ps[:, b, 256:384], kT[r, c, 128:256], qhT[r, c, 128:256], start=True, stop=True)
                nc.tensor.matmul(ps[0:META, b + 1, 0:256], kT[r, c, 256:LTOK], qhT[r, c, :], start=True, stop=True)\
                    .then_inc(S("z_pe"), 1)
                owe("zm", hd + 1, b + 1)
                owe("zA", hd + 1, b)

            def stick_c(hd):
                sp_ = st0[:, hd % 2, 2, :]
                pe.wait_ge(S("sp"), hd + 1)
                claim(4, 5)
                ones, tri = cc("ones", 128), cc("tri", 128)
                nc.tensor.matmul(ps[:, 4, 0:256], tri, sp_[:, 0:256], start=True, stop=False)
                nc.tensor.matmul(ps[:, 4, 128:256], ones, sp_[:, 256:384], start=False, stop=True)
                nc.tensor.matmul(ps[:, 4, 256:384], tri, sp_[:, 256:384], start=True, stop=True)
                nc.tensor.matmul(ps[0:META, 5, 0:256], ones[:, 0:META], sp_[:, 0:256], start=True, stop=False)
                nc.tensor.matmul(ps[0:META, 5, 128:256], ones[:, 0:META], sp_[:, 256:384], start=False, stop=False)
                nc.tensor.matmul(ps[0:META, 5, 0:256], tri[0:META, 0:META], sp_[0:META, 384:640],
                                 start=False, stop=True).then_inc(S("c_pe"), 1)
                owe("dd", hd + 1, 4, 5)

            def stick_o(hd):
                c, r = hd // 2, slice(64 * (hd % 2), 64 * (hd % 2) + 64)
                w_ = st0[:, hd % 2, 3, :]
                b = 6 + hd % 2
                v = slice(hd * 64, hd * 64 + 64)
                pe.wait_ge(S("w"), hd + 1)
                claim(b)
                nc.tensor.matmul(ps[r, b, 0:256], vk[:, 0, v], w_[:, 0:256], start=True, stop=False)
                nc.tensor.matmul(ps[r, b, 128:256], vk[:, 1, v], w_[:, 256:384], start=False, stop=False)
                nc.tensor.matmul(ps[r, b, 0:256], vk[0:META, 2, v], w_[0:META, 384:640], start=False, stop=True)\
                    .then_inc(S("o_pe"), 1)
                owe("o_ev", hd + 1, b)

            stick_z(0)
            for i in range(16):
                if i < 15:
                    stick_z(i + 1)
                stick_c(i)
                if i:
                    stick_o(i - 1)
            stick_o(15)
            pe.wait_ge(S("o_ev"), 16)
            tokens_out(lambda c, c0, P: oT[:, c, c0:c0 + P], [0, 1], DC, "wo_h")
            peer(1)

            transposes("nm", lambda t: hn[0:128, t, :], [0, 1])
            pe.wait_ge(S("turned_out"), AT["nm"][3] + 2)
            cols_out(4, SEQ, "m_ev", [0, 1, 2, 3])

            def halves_out(reader, val, b0):
                claim(b0, b0 + 1)
                for u in range(4):
                    w = unit()
                    for c in range(2):
                        for t in range(2):
                            last = nc.tensor.matmul(ps[:, b0 + t, :], xT[:, 2 * u + c, t * 128:t * 128 + 128],
                                                    w[:, c * 512:(c + 1) * 512], start=u + c == 0, stop=u + c == 4)
                    used(last)
                owe(reader, val, b0, b0 + 1)

            halves_out("m_ev", 6, 4)
            pe.wait_ge(S("ld_m"), 80)
            claim(6)
            nc.tensor.matmul(ps[0:8, 6, 0:384], tsb[0:32, 0:8], cs2c[0:32, CS2["bucket"]:CS2["bucket"] + 384],
                             start=True, stop=True).then_inc(S("trev_pe"), 1)
            owe("trev_sb", 1, 6)
            transposes("n2", lambda t: hn[0:128, t, :], [0, 1])
            pe.wait_ge(S("turned_out"), AT["n2"][3] + 2)
            cols_out(20, SEQ, "iT_ev", range(6))
            for k in range(3):
                halves_out("iv_ev", 2 * k + 2, 2 * k)
            for k in range(3):
                tokens_out(x_at, [0, 1], DC, f"z{k}_ev", b0=4 * (k % 2))

            for j in range(8):
                b = j % 2
                pe.wait_ge(S("iT_ev"), 8 + j + 1)
                claim(b)
                nc.tensor.matmul(ps[:, b, 0:256], cs2c[:, 0:128], qkT[:, 8 + j, :], start=True, stop=True)\
                    .then_inc(S("sw_pe"), 1)
                owe("rot_ps", j + 1, b)
            for hd in range(4):
                b = 2 + hd % 2
                pe.wait_ge(S("rot"), 4 + hd + 1)
                claim(b)
                nc.tensor.matmul(ps[:, b, 0:256], qkT[:, 12 + hd, 0:128], qkT[:, 8 + hd, :], start=True, stop=True)
                nc.tensor.matmul(ps[:, b, 256:384], qkT[:, 12 + hd, 128:256], qkT[:, 8 + hd, 128:256],
                                 start=True, stop=True).then_inc(S("rs_pe"), 1)
                owe("rs_sb", hd + 1, b)
            pe.wait_ge(S("iv_ev"), 4)
            claim(6, 7)
            for hd in range(4):
                e = slice(hd * 128, hd * 128 + 128)
                sT = mrg[:, hd // 2, (hd % 2) * 384:(hd % 2) * 384 + 384]
                pe.wait_ge(S("rs_sb"), hd + 1)
                nc.tensor.matmul(ps[:, 6, e], sT[:, 0:128], vtok[:, 1, 0, e], start=True, stop=True)
                nc.tensor.matmul(ps[:, 7, e], sT[:, 128:256], vtok[:, 1, 0, e], start=True, stop=False)
                nc.tensor.matmul(ps[:, 7, e], sT[:, 256:384], vtok[:, 1, 1, e], start=False, stop=True)\
                    .then_inc(S("ry_pe"), 1)
            owe("ry_ps", 1, 6, 7)

            def soft_s(n):
                b = n % 2
                claim(b)
                if n < 8:
                    c, r = n // 2, slice(64 * (n % 2), 64 * (n % 2) + 64)
                    nc.tensor.matmul(ps[:, b, 0:128], qkT[r, c, 0:128], qkT[r, 4 + c, 0:128], start=True, stop=True)
                    nc.tensor.matmul(ps[:, b, 128:384], qkT[r, c, 128:256], qkT[r, 4 + c, :], start=True, stop=True)\
                        .then_inc(S("ss_pe"), 1)
                else:
                    for t in range(2):
                        last = nc.tensor.matmul(ps[:, b, t * 256:(t + 1) * 256],
                                                qkT[:, 16 + n - 8, t * 128:(t + 1) * 128], kmT[:, n - 8, :],
                                                start=True, stop=True)
                    last.then_inc(S("ss_pe"), 1)
                owe("ss_ps", n + 1, b)

            def soft_t(n):
                b = 2 + n % 2
                p_ = pw[:, n % 2, :]
                pe.wait_ge(S("pn"), n + 1)
                claim(b)
                if n < 8:
                    order = [(0, 0), (1, 128), (2, 256)]
                else:
                    order = [(0, 0), (2, 128), (1, 256), (3, 384)]
                for src, dst in order:
                    last = nc.tensor.transpose(ps[:, b, dst:dst + 128], p_[:, src * 128:(src + 1) * 128], ident)
                last.then_inc(S("pt_pe"), 1)
                owe("pt_ev", n + 1, b)

            def soft_o(n):
                b = 4 + n % 2
                pT_ = pw[:, n % 2, 512:1024]
                pe.wait_ge(S("pt_ev"), n + 1)
                claim(b)
                if n < 8:
                    c, r = n // 2, slice(64 * (n % 2), 64 * (n % 2) + 64)
                    v = slice(n * 64, n * 64 + 64)
                    nc.tensor.matmul(ps[r, b, 0:256], vtok[:, 0, 0, v], pT_[:, 0:256], start=True, stop=False)
                    nc.tensor.matmul(ps[r, b, 128:256], vtok[:, 0, 1, v], pT_[:, 256:384], start=False, stop=True)\
                        .then_inc(S("so_pe"), 1)
                else:
                    v = slice((n - 8) * 128, (n - 8) * 128 + 128)
                    nc.tensor.matmul(ps[:, b, 0:256], vmem[:, 0, v], pT_[:, 0:256], start=True, stop=False)
                    nc.tensor.matmul(ps[:, b, 0:256], vmem[:, 1, v], pT_[:, 256:512], start=False, stop=True)\
                        .then_inc(S("so_pe"), 1)
                owe("so_ev", n + 1, b)

            pe.wait_ge(S("ld_b"), 16)
            claim(0, 1, 2, 3)
            for j in range(4):
                last = nc.tensor.matmul(ps[:, j, :], cs2c[:, CS2["flip"]:CS2["flip"] + 128],
                                        pw.rearrange("p b n -> p (b n)")[:, j * 512:(j + 1) * 512],
                                        start=True, stop=True)
            last.then_inc(S("flip_pe"), 1)
            owe("bias", 1, 0, 1, 2, 3)
            soft_s(0)
            for n in range(12):
                if n < 11:
                    soft_s(n + 1)
                soft_t(n)
                if n:
                    soft_o(n - 1)
            soft_o(11)
            transposes("yr", lambda t: hn[:, 0, t * 512:(t + 1) * 512], [0, 1], chunks=4)
            pe.wait_ge(S("so_ev"), 12)
            pe.wait_ge(S("turned_out"), AT["yr"][3] + 2)
            for k in range(3):
                tokens_out(lambda c, c0, P: yT[:, k, c, c0:c0 + P], [0, 1], 4, f"br{k}_ps", b0=0 if k != 1 else 4)
            transposes("mg", lambda t: mrg[:, t, :], [0, 1])
            pe.wait_ge(S("turned_out"), AT["mg"][3] + 2)
            tokens_out(x_at, [0, 1], DC, "out_h")
            transposes("n3", lambda t: hn[0:128, t, :], [0, 1])
            pe.wait_ge(S("turned_out"), AT["n3"][3] + 2)
            cols_out(2 * FFC, SEQ, "up_ev", range(6))
            claim(0, 1, 2, 3)
            for c in range(FFC):
                w = unit()
                pe.wait_ge(S("a_T"), c + 1)
                for t in range(2):
                    for j in range(2):
                        last = nc.tensor.matmul(ps[:, 2 * t + j, :], aT[:, c, t * 128:(t + 1) * 128],
                                                w[:, j * 512:(j + 1) * 512], start=c == 0, stop=c == FFC - 1)
                used(last)

        @block.scalar
        def _(act):
            def squares(tag, src, dst, tiles, col):
                for n, t in enumerate(tiles):
                    P = TILES[t][1]
                    nc.scalar.activation(dst(t), src(t), ACT.Square, accum_out=ss[0:P, col + n:col + n + 1])\
                        .then_inc(S("squared"), 1)

            def root(tag, ap):
                act.wait_ge(S("var_ready"), AT[tag][1] + 1)
                nc.scalar.activation(ap, ap, ACT.Sqrt).then_inc(S("std_ready"), 1)

            def hT(t):
                return hn[0:TILES[t][1], t, :]

            def hh(t):
                return h[0:TILES[t][1], t, :]

            def t_out(tag, tiles, dst, scale=1.0):
                for n, t in enumerate(tiles):
                    c0, P = TILES[t]
                    act.wait_ge(S("turned"), AT[tag][3] + n + 1)
                    nc.scalar.activation(dst(c0, P), ps2(6).rearrange("p (c n) -> p c n", n=128)[:, :, 0:P],
                                         ACT.Copy, scale=scale).then_inc(S("turned_out"), 1)

            def tokens_ev(units_done, tiles, dst, sem, func=ACT.Copy, b0=0):
                act.wait_ge(S("w_used"), units_done)
                for n, t in enumerate(tiles):
                    nc.scalar.activation(dst(t), ps2(b0 + 2 * n, TILES[t][1]), func).then_inc(S(sem), 1)

            act.wait_ge(S("ld_h"), 48)
            act.wait_ge(S("ld_c"), 96)
            act.wait_ge(S("zb"), 3)
            squares("n0", hh, hT, [0, 1, 2], 0)
            root("n0", rs[:, 0:3])
            for c in range(DC):
                act.wait_ge(S("pool_pe"), c + 1)
                nc.scalar.activation(xT[:, c, :], ps[:, c % 6, 0:LTOK], ACT.Copy, scale=gcol("mix0", c))\
                    .then_inc(S("pool_ev"), 1)

            def peer(l):
                tiles = [0, 1, 2] if l == 0 else [0, 1]
                N = LTOK if l == 0 else SEQ
                act.wait_ge(S("mix0_h" if l == 0 else "wo_h"), len(tiles))
                squares(f"f{l}", hh, hT, tiles, 3 + 8 * l)
                root(f"f{l}", rs[:, 3 + 8 * l:3 + 8 * l + len(tiles)])
                t_out(f"f{l}", tiles, lambda c0, P: xT[:, :, c0:c0 + P])
                for j in range(16):
                    act.wait_ge(S("w_used"), U0[f"wq{l}"] + j + 1)
                    nc.scalar.activation(qT[:, j, 0:N], ps[:, j % 6, 0:N], ACT.Copy).then_inc(S(f"q{l}_ev"), 1)
                for n, t in enumerate([2, 0, 1] if l == 0 else [0, 1]):
                    P = TILES[t][1]
                    act.wait_ge(S(f"sc{l}_pe"), n + 1)
                    if l == 0 and t == 1:
                        act.wait_ge(S("md"), 128)
                    nc.scalar.activation(s_sb[0 if t == 0 else 1][0:P, :], ps[0:P, 0:4, :].rearrange("p b n -> p (b n)"),
                                         ACT.Copy).then_inc(S(f"sc{l}_ev"), 1)
                    if t == 2:
                        act.wait_ge(S("sc0_ev"), 1)
                        for hd in range(PEER_H):
                            r = slice(hd * META, (hd + 1) * META)
                            act.dma_start(s_m[r, :], s_sb[1][0:META, hd * 256:(hd + 1) * 256]).then_inc(S("md"), 16)
                        for hd in range(PEER_H):
                            r = slice(hd * META, (hd + 1) * META)
                            act.dma_start(hnm[r, :], hn[0:META, 2, :]).then_inc(S("md2"), 16)
                for n, t in enumerate([2, 0, 1] if l == 0 else [0, 1]):
                    q = tk_number(l, t)
                    act.wait_ge(S("gx"), q)
                    G = gates[t][:, 0:16 if t == 2 else 128]
                    nc.scalar.activation(G, G, ACT.Exp).then_inc(S("ge"), 1)
                for m, (t, base) in enumerate(gathers(l)):
                    P = TILES[t][1]

                    def slot(k, n):
                        act.wait_ge(S("dot"), n + 1)
                        nc.scalar.activation(gel[:, k % 8:k % 8 + 1], dots[:, k % 8:k % 8 + 1], ACT.Gelu)\
                            .then_inc(S("gelu"), 1)

                    if t == 2:
                        for k in range(16):
                            slot(k, base + k)
                    else:
                        with act.Fori(0, SLOTS // GB) as i:
                            for k in range(GB):
                                slot(k, GB * i + (base + k))
                    act.wait_ge(S(f"y{l}_pe"), m + 1)
                    nc.scalar.activation(hh(t), ps2(2 * t, P), ACT.Copy).then_inc(S(f"y{l}"), 1)

            peer(0)
            act.wait_ge(S("y0"), 3)
            squares("kv", hh, hT, [0, 1, 2], 6)
            root("kv", rs[:, 6:9])
            tokens_ev(U0["kv_k"] + 8, [0, 1, 2], hT, "k_ev")
            root("kh", hsum[:, 0:48])
            tokens_ev(U0["kv_v"] + 8, [0, 1, 2], lambda t: vk[0:TILES[t][1], t, :], "v_ev")
            t_out("kh", [0, 1, 2], lambda c0, P: kT[:, :, c0:c0 + P], gcol("knorm"))
            squares("n1", hh, hT, [0, 1], 9)
            root("n1", rs[:, 9:11])
            tokens_ev(U0["w_q"] + 8, [0, 1], hT, "q_ev")
            root("qh", hsum[:, 0:32])
            t_out("qh", [0, 1], lambda c0, P: qhT[:, :, c0:c0 + P], gcol("qnorm"))

            def stick_front(hd):
                s_ = st0[:, hd % 2, :, :]
                act.wait_ge(S("z_pe"), hd + 1)
                if hd >= 2:
                    act.wait_ge(S("w"), hd - 1)
                else:
                    act.wait_ge(S("stz"), 1)
                nc.scalar.activation(s_[0:META, 0, 384:640], ps[0:META, 2 * (hd % 2) + 1, 0:256], ACT.Copy,
                                     scale=0.125).then_inc(S("zm"), 1)
                act.wait_ge(S("tmin"), hd + 1)
                nc.scalar.activation(s_[:, 1, :], s_[:, 1, :], ACT.Exp).then_inc(S("ex"), 1)
                act.wait_ge(S("ex"), hd + 1)
                nc.scalar.activation(s_[:, 1, :], s_[:, 1, :], ACT.Ln, bias=1.0).then_inc(S("ln"), 1)

            def stick_out(hd):
                c, r = hd // 2, slice(64 * (hd % 2), 64 * (hd % 2) + 64)
                act.wait_ge(S("o_pe"), hd + 1)
                nc.scalar.activation(oT[r, c, :], ps[r, 6 + hd % 2, 0:256], ACT.Copy).then_inc(S("o_ev"), 1)

            stick_front(0)
            for i in range(16):
                if i < 15:
                    stick_front(i + 1)
                act.wait_ge(S("dd"), i + 1)
                if i >= 2:
                    act.wait_ge(S("o_pe"), i - 1)
                nc.scalar.activation(st0[:, i % 2, 3, :], st0[:, i % 2, 0, :], ACT.Exp).then_inc(S("w"), 1)
                if i:
                    stick_out(i - 1)
            stick_out(15)
            peer(1)

            act.wait_ge(S("ld_m"), 80)
            act.wait_ge(S("y1"), 2)
            squares("nm", lambda t: mrg[:, t, :], hT, [0, 1], 14)
            root("nm", rs[:, 14:16])
            for j in range(4):
                act.wait_ge(S("w_used"), U0["mem_k"] + j + 1)
                nc.scalar.activation(kmT[:, j, :], ps[:, j, 0:256], ACT.Copy).then_inc(S("m_ev"), 1)
            act.wait_ge(S("w_used"), U0["mem_v"] + 4)
            for t in range(2):
                nc.scalar.activation(vmem[:, t, :], ps[:, 4 + t, :], ACT.Copy).then_inc(S("m_ev"), 1)
            squares("n2", hh, hT, [0, 1], 12)
            root("n2", rs[:, 12:14])
            for j in range(20):
                act.wait_ge(S("w_used"), U0["in_T"] + j + 1)
                nc.scalar.activation(qkT[:, j, :], ps[:, j % 6, 0:256], ACT.Copy).then_inc(S("iT_ev"), 1)
            for k in range(3):
                act.wait_ge(S("w_used"), U0["in_v"] + 4 * k + 4)
                for t in range(2):
                    nc.scalar.activation(vtok[:, k, t, :], ps[:, 2 * k + t, :], ACT.Copy if k < 2 else ACT.Sigmoid)\
                        .then_inc(S("iv_ev" if k < 2 else "sg"), 1)
            for k in range(3):
                tokens_ev(U0["in_z"] + 8 * k + 8, [0, 1], lambda t: zs[:, k, t, :], f"z{k}_ev", ACT.Sigmoid, 4 * (k % 2))
            root("ry", tsb[:, 16:24])
            act.wait_ge(S("flip_pe"), 1)
            nc.scalar.activation(biasT.rearrange("p h y -> p (h y)"), ps[:, 0:4, :].rearrange("p b n -> p (b n)"),
                                 ACT.Copy).then_inc(S("bias"), 1)

            def soft_e(n):
                p_ = pw[:, n % 2, :]
                act.wait_ge(S("nmx"), n + 1)
                if n >= 2:
                    act.wait_ge(S("pt_pe"), n - 1)
                if n < 8:
                    spans, src, scale = [(0, 128), (128, 384)], p_, 1.0
                else:
                    spans, src, scale = [(0, 256), (256, 512)], ps[:, n % 2, :], RET_DK ** -0.5
                for t, (a, b) in enumerate(spans):
                    col = 8 * (n % 2) + t
                    nc.scalar.activation(p_[:, a:b], src[:, a:b], ACT.Exp, bias=nmx[:, col:col + 1], scale=scale,
                                         accum_out=nmx[:, col + 2:col + 3]).then_inc(S("pe_"), 1)

            def soft_tev(n):
                b = 2 + n % 2
                w_ = 384 if n < 8 else 512
                act.wait_ge(S("pt_pe"), n + 1)
                if n >= 2:
                    act.wait_ge(S("so_pe"), n - 1)
                nc.scalar.activation(pw[:, n % 2, 512:512 + w_], ps[:, b, 0:w_], ACT.Copy).then_inc(S("pt_ev"), 1)

            def soft_oev(n):
                act.wait_ge(S("so_pe"), n + 1)
                if n < 8:
                    c, r = n // 2, slice(64 * (n % 2), 64 * (n % 2) + 64)
                    dst = yT[r, 0, c, :]
                else:
                    r = slice(0, 128)
                    dst = yT[:, 2, n - 8, :]
                nc.scalar.activation(dst, ps[r, 4 + n % 2, 0:256], ACT.Copy).then_inc(S("so_ev"), 1)

            soft_e(0)
            for n in range(12):
                if n < 11:
                    soft_e(n + 1)
                soft_tev(n)
                if n:
                    soft_oev(n - 1)
            soft_oev(11)
            for t in range(2):
                act.wait_ge(S("turned"), AT["yr"][3] + t + 1)
                nc.scalar.activation(yT[:, 1, :, t * 128:(t + 1) * 128],
                                     ps[:, 6, :].rearrange("p (c n) -> p c n", n=128), ACT.Copy)\
                    .then_inc(S("turned_out"), 1)
            t_out("mg", [0, 1], lambda c0, P: xT[:, :, c0:c0 + P])
            act.wait_ge(S("out_h"), 2)
            squares("n3", hh, hT, [0, 1], 17)
            root("n3", rs[:, 17:19])
            for j in range(FFC):
                for k in range(2):
                    act.wait_ge(S("w_used"), U0["up"] + 2 * j + k + 1)
                    if j >= 2:
                        act.wait_ge(S("cv"), 2 * (j - 2) + k + 1)
                    else:
                        act.wait_ge(S("padded"), 1)
                    nc.scalar.activation(up_in[:, j % 2, k, 2:258], ps[:, (2 * j + k) % 6, 0:256], ACT.Copy)\
                        .then_inc(S("up_ev"), 1)
                act.wait_ge(S("cv"), 2 * j + 1)
                nc.scalar.activation(up_cv[:, j % 2, 0, :], up_cv[:, j % 2, 0, :], ACT.Gelu).then_inc(S("gate"), 1)
            act.wait_ge(S("down_h"), 2)
            squares("n4", hh, hT, [0, 1], 19)
            root("n4", rs[:, 19:21])

        @block.vector
        def _(dve):
            chain = [0]

            def link(ins):
                chain[0] += 1
                ins.then_inc(S("dve_chain"), 1)
                dve.wait_ge(S("dve_chain"), chain[0])

            v = nc.vector

            def hT(t):
                return hn[0:TILES[t][1], t, :]

            def hh(t):
                return h[0:TILES[t][1], t, :]

            def rstd(tag, src, dst, n_wait, width):
                if n_wait:
                    dve.wait_ge(S("squared"), AT[tag][0] + n_wait)
                v.tensor_scalar(dst, src, 1.0 / width, EPS, ALU.mult, ALU.add).then_inc(S("var_ready"), 1)
                dve.wait_ge(S("std_ready"), AT[tag][1] + 1)
                link(v.reciprocal(dst, dst))

            def norm(tag, tiles, col, src=hh, gain=None):
                rstd(tag, ss[:, col:col + len(tiles)], rs[:, col:col + len(tiles)], len(tiles), D)
                for n, t in enumerate(tiles):
                    P = TILES[t][1]
                    r = rs[0:P, col + n:col + n + 1]
                    if gain is None:
                        i = v.tensor_scalar(hT(t), src(t), r, None, ALU.mult)
                    else:
                        i = v.scalar_tensor_tensor(hT(t), src(t), r, gain[0:P, :], ALU.mult, ALU.mult)
                    i.then_inc(S("x_ready"), 1)

            def t_out(tag, tiles, gain, free=None):
                if free is not None:
                    dve.wait_ge(S("w_used"), free)
                for n, t in enumerate(tiles):
                    c0, P = TILES[t]
                    dve.wait_ge(S("turned"), AT[tag][3] + n + 1)
                    v.tensor_tensor(xT[:, :, c0:c0 + P], ps2(6).rearrange("p (c n) -> p c n", n=128)[:, :, 0:P],
                                    gains(gain, P), ALU.mult).then_inc(S("turned_out"), 1)

            def add_h(units_done, sem, tiles):
                dve.wait_ge(S("w_used"), units_done)
                for n, t in enumerate(tiles):
                    v.tensor_tensor(hh(t), hh(t), ps2(2 * n, TILES[t][1]), ALU.add).then_inc(S(sem), 1)

            dve.wait_ge(S("zb"), 3)
            dve.wait_ge(S("ld_h"), 48)
            dve.wait_ge(S("ld_c"), 96)
            norm("n0", [0, 1, 2], 0)
            dve.wait_ge(S("w_used"), U0["pool"] + 2)
            for t in range(3):
                P = TILES[t][1]
                v.tensor_tensor(hT(t), ps2(2 * t, P), bcP[0:P, :], ALU.mult).then_inc(S("mix0_ps"), 1)
                dve.wait_ge(S("mix0_ps"), t + 1)
                v.tensor_tensor(hh(t), hh(t), hT(t), ALU.add).then_inc(S("mix0_h"), 1)

            def topk(l, t):
                H = 1 if t == 2 else PEER_H
                s_ = (s_m if t == 2 else s_sb[t]).rearrange("p (j n) -> p j n", n=128)
                tv_ = tv[:, 0:32 * H].rearrange("p (j a) -> p j a", a=16)
                ti_ = ti[:, 0:32 * H].rearrange("p (j a) -> p j a", a=16)
                tif_ = tif[:, 0:32 * H].rearrange("p (j a) -> p j a", a=16)
                J = 2 * H

                def top16(n, val, idx, src):
                    for j in range(n):
                        i = v.max(val[:, j, 0:8], src[:, j, :])
                    link(i)
                    for j in range(n):
                        i = v.max_index(idx[:, j, 0:8], val[:, j, 0:8], src[:, j, :])
                    link(i)
                    for j in range(n):
                        i = v.match_replace(src[:, j, :], val[:, j, 0:8], src[:, j, :], -3.0e38)
                    link(i)
                    for j in range(n):
                        i = v.max(val[:, j, 8:16], src[:, j, :])
                    link(i)
                    for j in range(n):
                        i = v.max_index(idx[:, j, 8:16], val[:, j, 8:16], src[:, j, :])
                    link(i)

                top16(J, tv_, ti_, s_)
                cand = (oh if t == 2 else s_sb[t])[:, 0:256 * H]
                tv4 = tv_.rearrange("p (h s) a -> p h s a", s=2)
                link(v.tensor_tensor(cand.rearrange("p (h a b) -> p h a b", a=16, b=16),
                                     tv4[:, :, 0, :].unsqueeze(3).to_broadcast([128, H, 16, 16]),
                                     tv4[:, :, 1, :].unsqueeze(2).to_broadcast([128, H, 16, 16]), ALU.add))
                bv_ = bv[:, 0:16 * H].rearrange("p (h k) -> p h k", k=16)
                bp_ = bp[:, 0:16 * H].rearrange("p (h k) -> p h k", k=16)
                top16(H, bv_, bp_, cand.rearrange("p (h n) -> p h n", n=256))
                G = gates[t][:, 0:16 * H]
                G3 = G.rearrange("p (h k) -> p h k", k=16)
                q = tk_number(l, t)
                v.tensor_tensor(G3, bv_, bv_[:, :, 0:1].to_broadcast([128, H, 16]), ALU.subtract)\
                    .then_inc(S("gx"), 1)
                n = 16 * H
                v.tensor_copy(tif[:, 0:32 * H], ti[:, 0:32 * H])
                v.tensor_scalar(pab[:, 0, 0:n], bp[:, 0:n], 4, None, ALU.logical_shift_right)
                link(v.tensor_scalar(pab[:, 1, 0:n], bp[:, 0:n], 15, None, ALU.bitwise_and))
                v.tensor_copy(sel_a[:, 0:n], pab[:, 0, 0:n])
                link(v.tensor_copy(sel_b[:, 0:n], pab[:, 1, 0:n]))
                o_ = oh[:, 0:16 * n].rearrange("p (m a) -> p m a", a=16)
                o4 = oh[:, 0:16 * n].rearrange("p (h k a) -> p h k a", k=16, a=16)
                tif4 = tif_.rearrange("p (h s) a -> p h s a", s=2)
                for half, (pos, res) in enumerate([(sel_a, ia), (sel_b, ib)]):
                    link(v.tensor_tensor(o_, pos[:, 0:n].unsqueeze(2).to_broadcast([128, n, 16]),
                                         cc("iota", 16).unsqueeze(1).to_broadcast([128, n, 16]), ALU.is_equal))
                    link(v.tensor_tensor(o4, o4, tif4[:, :, half, :].unsqueeze(2).to_broadcast([128, H, 16, 16]),
                                         ALU.mult))
                    link(v.tensor_reduce(res[:, 0:n], o_, AX, ALU.add))
                link(v.tensor_scalar(ia[:, 0:n], ia[:, 0:n], 128.0, float(l * EXPERTS), ALU.mult, ALU.add))
                v.tensor_tensor(eidx[:, t, 0:n], ia[:, 0:n], ib[:, 0:n], ALU.add).then_inc(S("eidx"), 1)
                dve.wait_ge(S("ge"), q)
                link(v.tensor_reduce(gm[:, 0:H], G3, AX, ALU.add))
                link(v.reciprocal(gs[:, 0:H], gm[:, 0:H]))
                link(v.tensor_tensor(G3, G3, gs[:, 0:H].unsqueeze(2).to_broadcast([128, H, 16]), ALU.mult))

            def gather_sums(l, t, base):
                hsrc = hnm if t == 2 else hn[:, t, :]
                unit_mat = cc("sel", 16) if t == 2 else ident
                W = 16 if t == 2 else 128

                def dot(k, n, ufill):
                    dve.wait_ge(S(f"u{k % NU}"), ufill)
                    v.scalar_tensor_tensor(ug[:, k % NU, :], ug[:, k % NU, :], 1.0, hsrc, ALU.mult, ALU.mult,
                                           accum_out=dots[:, k % 8:k % 8 + 1]).then_inc(S("dot"), 1)

                def coef(k, n, col):
                    dve.wait_ge(S("gelu"), n + 1)
                    if not isinstance(n, int) or n >= 4:
                        dve.wait_ge(S("vsum"), n - 3)
                    v.tensor_scalar(diag[:, k % 4, 0:W], unit_mat, gel[:, k % 8:k % 8 + 1],
                                    gates[t][:, col] if isinstance(col, slice) else gates[t][:, ds(col, 1)],
                                    ALU.mult, ALU.mult).then_inc(S("diag"), 1)

                if t == 2:
                    dve.wait_ge(S("md2"), 128)
                    for k in range(16):
                        dot(k, base + k, 16 * ((base + k) // NU + 1))
                        if k >= 2:
                            coef(k - 2, base + k - 2, slice(k - 2, k - 1))
                    for k in (14, 15):
                        coef(k, base + k, slice(k, k + 1))
                    return
                with dve.Fori(0, SLOTS // GB) as i:
                    for k in range(GB):
                        dot(k, GB * i + (base + k), 16 * (GB // NU) * i + 16 * ((base + k) // NU + 1))
                        if k >= 2:
                            coef(k - 2, GB * i + (base + k - 2), GB * i + (k - 2))
                    for k in (GB - 2, GB - 1):
                        coef(k, GB * i + (base + k), GB * i + k)

            def peer(l):
                tiles = [0, 1, 2] if l == 0 else [0, 1]
                norm(f"f{l}", tiles, 3 + 8 * l, gain=bcF[:, l, :])
                for n, t in enumerate([2, 0, 1] if l == 0 else [0, 1]):
                    if t == 2:
                        dve.wait_ge(S("md"), 128)
                    else:
                        dve.wait_ge(S(f"sc{l}_ev"), n + 1)
                    topk(l, t)
                for t, base in gathers(l):
                    gather_sums(l, t, base)

            peer(0)

            def heads_norm(tag, tiles, cols):
                for t in tiles:
                    P = TILES[t][1]
                    link(v.tensor_tensor(sq[0:P, :], hT(t), hT(t), ALU.mult))
                    link(v.tensor_reduce(hsum[0:P, 16 * t:16 * t + 16], sq[0:P, :].rearrange("p (h e) -> p h e", e=64),
                                         AX, ALU.add))
                n = 16 * len(tiles)
                rstd(tag, hsum[:, 0:n], hsum[:, 0:n], 0, 64)
                for t in tiles:
                    P = TILES[t][1]
                    x3 = hT(t).rearrange("p (h e) -> p h e", e=64)
                    v.tensor_tensor(x3, x3, hsum[0:P, 16 * t:16 * t + 16].unsqueeze(2).to_broadcast([P, 16, 64]),
                                    ALU.mult).then_inc(S("x_ready"), 1)

            norm("kv", [0, 1, 2], 6)
            t_out("kv", [0, 1, 2], "kvn")
            dve.wait_ge(S("k_ev"), 3)
            heads_norm("kh", [0, 1, 2], 0)
            dve.wait_ge(S("turned"), AT["kh"][3] + 3)
            norm("n1", [0, 1], 9)
            t_out("n1", [0, 1], "mix1", free=U0["kv_v"] + 8)
            dve.wait_ge(S("q_ev"), 2)
            heads_norm("qh", [0, 1], 0)
            for b in range(2):
                i = v.memset(st0[:, b, 0, 384:640], 0.0)
            i.then_inc(S("stz"), 1)

            def stick_z(hd):
                s_ = st0[:, hd % 2, :, :]
                dve.wait_ge(S("z_pe"), hd + 1)
                if hd >= 2:
                    dve.wait_ge(S("w"), hd - 1)
                v.scalar_tensor_tensor(s_[:, 0, 0:384], ps[:, 2 * (hd % 2), 0:384], 0.125, cc("strict", 384),
                                       ALU.mult, ALU.add).then_inc(S("zA"), 1)
                dve.wait_ge(S("zA"), hd + 1)
                dve.wait_ge(S("zm"), hd + 1)
                v.scalar_tensor_tensor(s_[:, 1, :], s_[:, 0, :], -1.0, s_[:, 0, :], ALU.mult, ALU.min)\
                    .then_inc(S("tmin"), 1)

            stick_z(0)
            for i in range(16):
                s_ = st0[:, i % 2, :, :]
                dve.wait_ge(S("ln"), i + 1)
                if i >= 2:
                    dve.wait_ge(S("c_pe"), i - 1)
                v.scalar_tensor_tensor(s_[:, 2, :], s_[:, 0, :], 0.0, s_[:, 1, :], ALU.max, ALU.add)\
                    .then_inc(S("sp"), 1)
                if i < 15:
                    stick_z(i + 1)
                dve.wait_ge(S("c_pe"), i + 1)
                v.tensor_tensor(s_[:, 0, 0:384], s_[:, 0, 0:384], ps[:, 4, 0:384], ALU.subtract)
                v.tensor_tensor(s_[0:META, 0, 384:640], s_[0:META, 0, 384:640], ps[0:META, 5, 0:256], ALU.subtract)\
                    .then_inc(S("dd"), 1)
            add_h(U0["w_o"] + 8, "wo_h", [0, 1])
            peer(1)

            dve.wait_ge(S("ld_m"), 80)
            dve.wait_ge(S("vsum"), 16 + 4 * SLOTS)
            norm("nm", [0, 1], 14, src=lambda t: mrg[:, t, :])
            t_out("nm", [0, 1], "gmem", free=U0["wq1"] + 16)
            dve.wait_ge(S("trev_pe"), 1)
            v.tensor_tensor(pw[0:8, 0, 0:384], ps[0:8, 6, 0:384], cs2c[0:8, CS2["future"]:CS2["future"] + 384],
                            ALU.add).then_inc(S("trev_sb"), 1)
            norm("n2", [0, 1], 12)
            t_out("n2", [0, 1], "gmix", free=U0["mem_v"] + 4)
            for t in range(2):
                dve.wait_ge(S("sg"), t + 1)
                v.tensor_tensor(vtok[:, 2, t, :], ps[:, 4 + t, :], vtok[:, 2, t, :], ALU.mult).then_inc(S("iv_ev"), 1)

            def c2(name, a=0, n=256):
                return cs2c[:, CS2[name] + a:CS2[name] + a + n]

            for j in range(8):
                x_ = qkT[:, 8 + j, :]
                k_ = "q" if j < 4 else "k"
                tmp = oh2[:, (j % 2) * 256:(j % 2) * 256 + 256]
                dve.wait_ge(S("sw_pe"), j + 1)
                v.tensor_tensor(tmp, ps[:, j % 2, 0:256], c2("sin" + k_), ALU.mult).then_inc(S("rot_ps"), 1)
                link(v.tensor_tensor(x_, x_, c2("cos" + k_), ALU.mult))
                v.tensor_tensor(x_, x_, tmp, ALU.add).then_inc(S("rot"), 1)
            for hd in range(4):
                dve.wait_ge(S("rs_pe"), hd + 1)
                v.tensor_tensor(mrg[:, hd // 2, (hd % 2) * 384:(hd % 2) * 384 + 384], ps[:, 2 + hd % 2, 0:384],
                                c2("decay", 384 * hd, 384), ALU.mult).then_inc(S("rs_sb"), 1)
            dve.wait_ge(S("ry_pe"), 4)
            y3 = hn[:, 0, :].rearrange("p (g e) -> p g e", e=128)
            q3 = hn[:, 1, :].rearrange("p (g e) -> p g e", e=128)
            mu = tsb[:, 8:16]
            var = tsb[:, 16:24]
            link(v.tensor_copy(hn[:, 0, :], ps2(6)))
            v.tensor_reduce(mu, y3, AX, ALU.add).then_inc(S("ry_ps"), 1)
            dve.wait_ge(S("ry_ps"), 1)
            link(v.tensor_scalar(mu, mu, -1.0 / 128, None, ALU.mult))
            link(v.tensor_tensor(y3, y3, mu.unsqueeze(2).to_broadcast([128, 8, 128]), ALU.add))
            link(v.tensor_tensor(q3, y3, y3, ALU.mult))
            link(v.tensor_reduce(var, q3, AX, ALU.add))
            rstd("ry", var, var, 0, 128)
            link(v.tensor_tensor(y3, y3, var.unsqueeze(2).to_broadcast([128, 8, 128]), ALU.mult))
            y4 = hn[:, 0, :].rearrange("p (t d) -> p t d", t=2)
            link(v.tensor_tensor(y4, y4, bcG[:, :].unsqueeze(1).to_broadcast([128, 2, 512]), ALU.mult))
            for t in range(2):
                v.tensor_tensor(y4[:, t, :], y4[:, t, :], vtok[:, 2, t, :], ALU.mult).then_inc(S("x_ready"), 1)

            dve.wait_ge(S("bias"), 1)

            def soft_l(n):
                p_ = pw[:, n % 2, :]
                col = 8 * (n % 2)
                dve.wait_ge(S("ss_pe"), n + 1)
                if n >= 2:
                    dve.wait_ge(S("pt_pe"), n - 1)
                if n < 8:
                    v.scalar_tensor_tensor(p_[:, 0:128], ps[:, n % 2, 0:128], 0.125, biasT[:, n, 128:256],
                                           ALU.mult, ALU.add)
                    v.scalar_tensor_tensor(p_[:, 128:384], ps[:, n % 2, 128:384], 0.125, biasT[:, n, :],
                                           ALU.mult, ALU.add).then_inc(S("ss_ps"), 1)
                    dve.wait_ge(S("ss_ps"), n + 1)
                    v.tensor_reduce(nmx[:, col:col + 1], p_[:, 0:128], AX, ALU.max, negate=True)
                    v.tensor_reduce(nmx[:, col + 1:col + 2], p_[:, 128:384], AX, ALU.max, negate=True)\
                        .then_inc(S("nmx"), 1)
                else:
                    link(v.tensor_reduce(nmx[:, col:col + 2], ps[:, n % 2, :].rearrange("p (t m) -> p t m", t=2),
                                         AX, ALU.max, negate=True))
                    v.tensor_scalar(nmx[:, col:col + 2], nmx[:, col:col + 2], RET_DK ** -0.5, None, ALU.mult)\
                        .then_inc(S("nmx"), 1)

            def soft_n(n):
                p_ = pw[:, n % 2, :]
                col = 8 * (n % 2)
                dve.wait_ge(S("pe_"), 2 * n + 2)
                i = v.reciprocal(nmx[:, col + 4:col + 6], nmx[:, col + 2:col + 4])
                if n >= 8:
                    i.then_inc(S("ss_ps"), 1)
                    dve.wait_ge(S("ss_ps"), n + 1)
                else:
                    link(i)
                for t, (a, b) in enumerate([(0, 128), (128, 384)] if n < 8 else [(0, 256), (256, 512)]):
                    i = v.tensor_scalar(p_[:, a:b], p_[:, a:b], nmx[:, col + 4 + t:col + 5 + t], None, ALU.mult)
                i.then_inc(S("pn"), 1)

            soft_l(0)
            for n in range(12):
                if n < 11:
                    soft_l(n + 1)
                soft_n(n)
            for k in range(3):
                dve.wait_ge(S("w_used"), U0["br"] + 4 * k + 4)
                dve.wait_ge(S(f"z{k}_ev"), 2)
                for t in range(2):
                    P2 = ps2(4 * (k % 2) + 2 * t)
                    if k == 0:
                        v.tensor_tensor(mrg[:, t, :], P2, zs[:, k, t, :], ALU.mult).then_inc(S("br0_ps"), 1)
                    else:
                        v.tensor_tensor(zs[:, k, t, :], P2, zs[:, k, t, :], ALU.mult).then_inc(S(f"br{k}_ps"), 1)
                        dve.wait_ge(S(f"br{k}_ps"), t + 1)
                        i = v.tensor_tensor(mrg[:, t, :], mrg[:, t, :], zs[:, k, t, :], ALU.add)
                        if k == 2:
                            i.then_inc(S("x_ready"), 1)
                        else:
                            link(i)
                if k == 0:
                    dve.wait_ge(S("br0_ps"), 2)
            add_h(U0["out"] + 8, "out_h", [0, 1])
            norm("n3", [0, 1], 17)
            t_out("n3", [0, 1], "gffn")
            v.memset(up_in[:, :, :, 0:2], 0.0).then_inc(S("padded"), 1)
            for j in range(FFC):
                for k in range(2):
                    x_ = up_in[:, j % 2, k, :]
                    y_ = up_cv[:, j % 2, k, :]
                    m = k * FFC + j
                    w_ = [colc[:, COL["convw"] + 44 * i + m:COL["convw"] + 44 * i + m + 1] for i in range(3)]
                    dve.wait_ge(S("up_ev"), 2 * j + k + 1)
                    link(v.tensor_scalar(y_, x_[:, 0:256], w_[0], gcol("convb", m), ALU.mult, ALU.add))
                    link(v.scalar_tensor_tensor(y_, x_[:, 1:257], w_[1], y_, ALU.mult, ALU.add))
                    v.scalar_tensor_tensor(y_, x_[:, 2:258], w_[2], y_, ALU.mult, ALU.add).then_inc(S("cv"), 1)
                dve.wait_ge(S("gate"), j + 1)
                dve.wait_ge(S("cv"), 2 * j + 2)
                v.tensor_tensor(aT[:, j, :], up_cv[:, j % 2, 0, :], up_cv[:, j % 2, 1, :], ALU.mult)\
                    .then_inc(S("a_T"), 1)
            add_h(U0["down"] + 22, "down_h", [0, 1])
            rstd("n4", ss[:, 19:21], rs[:, 19:21], 2, D)
            dve.wait_ge(S("ld_g"), 16)
            for t in range(2):
                v.scalar_tensor_tensor(hn[:, t, :], h[:, t, :], rs[:, 19 + t:20 + t], bcL, ALU.mult, ALU.mult)\
                    .then_inc(S("fin"), 1)


def _t(w):
    J = w.shape[1] // 128
    return w.reshape(8, 128, J, 128).transpose(2, 1, 0, 3).reshape(J, 128, 1024)


def _n(w):
    return w.reshape(-1, 128, 1024)


def _n2(w):
    return w.reshape(4, 2, 128, 512).transpose(0, 2, 1, 3).reshape(4, 128, 1024)


def _pack_units(a):
    w_in, w_up = a["w_in_2"][0], a["w_up_2"][0]
    o = [0, 512, 1024, 1536, 2048, 2560, 3072, 3584, 4096, 5120, 6144, 7168]
    qa, ka, va, qr, kr, vr, gr, qm, za, zr, zm = [w_in[:, o[i]:o[i + 1]] for i in range(11)]
    up = np.stack([_t(w_up[:, :DFF]), _t(w_up[:, DFF:])], axis=1).reshape(-1, 128, 1024)
    keys = [a["peer_keys"][l].reshape(2, 8, 128, 128).transpose(0, 3, 1, 2).reshape(2, 128, 1024) for l in range(2)]
    parts = [
        a["pool_w"][0].reshape(2, 2, 2, 128, 256).transpose(0, 3, 1, 2, 4).reshape(2, 128, 1024),
        _t(a["peer_wq"][0]), keys[0], _n(a["w_kv"][:, :D]), _n(a["w_kv"][:, D:]), _n(a["w_q"][0]), _n(a["w_o"][0]),
        _t(a["peer_wq"][1]), keys[1], _t(a["w_mem_kv_2"][0][:, :512]), _n2(a["w_mem_kv_2"][0][:, 512:]),
        _t(qa), _t(ka), _t(qr), _t(kr), _t(qm), _n2(va), _n2(vr), _n2(gr), _n(za), _n(zr), _n(zm),
        _n(a["w_br_attn_2"][0]), _n(a["w_br_ret_2"][0]), _n(a["w_br_mem_2"][0]), _n(a["w_out_2"][0]), up,
        _n(a["w_down_2"][0])]
    return np.ascontiguousarray(np.concatenate(parts, axis=0))


def _cols(v):
    return v.reshape(-1, 128).T


def _pack_cols(a):
    two = lambda g: np.concatenate([g, g]).reshape(128, 1)
    cw = a["conv_w_2"][0]
    return np.ascontiguousarray(np.concatenate(
        [_cols(a["norm_mix"][0]), _cols(a["norm_mix"][1]), _cols(a["kv_norm"]), _cols(a["g_mix_2"][0]),
         _cols(a["g_mem_2"][0]), _cols(a["g_ffn_2"][0]), two(a["k_norm"]), two(a["q_norm"][0]),
         _cols(a["conv_b_2"][0]), _cols(cw[0]), _cols(cw[1]), _cols(cw[2])], axis=1))


def _constants():
    f = np.float32
    i = np.arange(128)
    strict = np.zeros((128, 384), f)
    future = np.where(i[:, None] < i[None, :], 0.0, NEG)
    strict[:, 0:128] = future
    strict[:, 256:384] = future
    c1 = [np.eye(128), (i[:, None] >= i[None, :]), np.ones((128, 128)), np.tile(np.arange(16), (128, 1)),
          (i[:, None] % META == np.arange(META)[None, :]), strict]
    cst = np.concatenate([np.asarray(x, f) for x in c1], axis=1)

    half = RET_DK // 2
    swap = np.roll(np.eye(128), half, axis=1)
    inv = f(10000.0) ** (-np.arange(half, dtype=f) / f(half))
    ang = (np.arange(SEQ, dtype=f)[None, :] * inv[:, None]).astype(f)
    cos = np.concatenate([np.cos(ang), np.cos(ang)]).astype(f)
    sin = np.concatenate([-np.sin(ang), np.sin(ang)]).astype(f)
    scale = f(RET_DK ** -0.5)
    decay = np.zeros((128, 4, 384))
    for hd in range(4):
        lg = np.log1p(-2.0 ** (-5.0 - hd))
        for a, (j0, i0, n) in {0: (0, 0, 256), 256: (128, 128, 128)}.items():
            diff = (i0 + np.arange(n))[None, :] - (j0 + i)[:, None]
            decay[:, hd, a:a + n] = np.where(diff >= 0, np.exp(lg * np.maximum(diff, 0)), 0.0)
    dist = 255 - np.arange(384)
    d = np.maximum(dist, 1).astype(f)
    large = 16 + (np.log(d / f(16)) / f(np.log(2048 / 16)) * f(16)).astype(np.int32)
    bucket = np.where(dist < 16, np.maximum(dist, 0), np.minimum(large, 31))
    hot = np.zeros((128, 384))
    hot[bucket, np.arange(384)] = 1.0
    fut = np.zeros((128, 384))
    fut[:, dist < 0] = NEG
    cs2 = np.concatenate([np.asarray(x, f) for x in
                          [swap, np.eye(128)[::-1], cos, sin, cos * scale, sin * scale, decay.reshape(128, -1), hot, fut]], axis=1)

    order = np.concatenate([np.arange(META, LTOK), np.arange(META)])
    pool = np.zeros((4, LTOK, LTOK))
    for g, w in enumerate((2, 4, 8, 16)):
        for t in range(LTOK):
            lo = max(0, t - w + 1)
            pool[g, lo:t + 1, t] = 1.0 / min(t + 1, w)
            pool[g, t, t] -= 1.0
    pool = pool[:, order][:, :, order]
    poolm = np.zeros((128, 4, 3, LTOK), f)
    for s, (c0, P) in enumerate(TILES):
        poolm[0:P, :, s, :] = pool[:, c0:c0 + P, :].transpose(1, 0, 2)
    return cst, cs2, poolm.reshape(128, -1)


def kernel(**inputs):
    import concourse.bacc as bacc
    from concourse.bass_utils import run_bass_kernel_spmd

    a = {k: np.asarray(v) for k, v in inputs.items()}
    cst, cs2, poolm = _constants()
    bc = np.zeros((5, D), np.float32)
    bc[0], bc[1], bc[2] = a["norm_ffn"][0], a["norm_ffn"][1], a["pool_scale"][0]
    bc[3, 0:512], bc[4] = a["ret_gn_gain_2"][0], a["g_final_2"]
    arrays = {
        "xin": a["x"][0], "metain": a["meta_tokens"], "units": _pack_units(a), "cols": _pack_cols(a),
        "cst": cst, "cs2": cs2, "poolm": poolm, "bc_rows": bc,
        "peer_u": a["peer_u"].reshape(2 * EXPERTS, D), "peer_v": a["peer_v"].reshape(2 * EXPERTS, D),
        "mem": a["mem_2"][0], "rel": a["rel_bias_2"]}
    arrays = {k: np.ascontiguousarray(v) for k, v in arrays.items()}
    nc = bacc.Bacc("TRN2", target_bir_lowering=False, num_devices=1)
    args = [nc.dram_tensor("in_" + k, v.shape, mybir.dt.from_np(v.dtype), kind="ExternalInput").ap()
            for k, v in arrays.items()]
    args.append(nc.dram_tensor("result", (SEQ, D), mybir.dt.float32, kind="ExternalOutput").ap())
    program(nc, *args)
    r = run_bass_kernel_spmd(nc, [{"in_" + k: v for k, v in arrays.items()}], core_ids=[0])
    return r.results[0]["result"].reshape(1, SEQ, D)
```

```python
from contextlib import ExitStack

import numpy as np

import concourse.bass as bass
from concourse import mybir

D = 1024
SEQ = 256
META = 16
LTOK = SEQ + META
DC = D // 128
EPS = 1e-6
NEG = -1e30
EXPERTS = 128 * 128
PEER_H = 8
TOPK = 16
DFF = 2816
FFC = DFF // 128
RET_DK = 128

R = 8
NU = 4
NV = 8
GB = 32
SLOTS = PEER_H * TOPK

TILES = [(0, 128), (128, 128), (256, META)]

UNITS = [("pool", 2), ("wq", 16), ("keys", 2),
         ("kA", 8), ("vA", 8), ("qA", 8), ("oA", 8), ("wqA", 16), ("keysA", 2),
         ("kB", 8), ("vB", 8), ("qB", 8), ("oB", 8), ("wqB", 16), ("keysB", 2),
         ("mem_k", 4), ("mem_v", 4), ("in_T", 20), ("in_v", 12), ("in_z", 24),
         ("br", 12), ("out", 8), ("up", 44), ("down", 22)]
N_UNITS = sum(n for _, n in UNITS)

STAGES = ["kv", "k", "v", "kh", "n1", "q", "qh", "stick", "o", "f1", "wq", "sc", "topk", "end"]
PLAN = [dict(zip(STAGES, (0, 5, 17, 29, 32, 36, 43, 47, 75, 82, 86, 98, 100, 126))),
        dict(zip(STAGES, (0, 4, 11, 18, 21, 25, 32, 36, 72, 79, 83, 95, 97, 126)))]
TOPK_STEPS = 5 * 16 + 10 + 2 * 5 * 8 + 60
GATE_AT = 5 * 16 + 10 + 2 * 5 * 8
LAG = 2

COL = {}
_at = 0
for _name, _n in [("mix0", 8), ("mix1", 8), ("kvn", 8), ("gmix", 8), ("gmem", 8), ("gffn", 8),
                  ("knorm", 1), ("qnorm", 1), ("convb", 44), ("convw", 132)]:
    COL[_name] = _at
    _at += _n
NCOL = _at

CST = {}
_at = 0
for _name, _n in [("ident", 128), ("tri", 128), ("ones", 128), ("iota", 16), ("sel", 16), ("valid", 384)]:
    CST[_name] = _at
    _at += _n
NCST = _at
CS2 = {}
_at = 0
for _name, _n in [("swap", 128), ("flip", 128), ("cosq", 256), ("sinq", 256), ("cosk", 256), ("sink", 256),
                  ("decay", 4 * 384), ("bucket", 384), ("future", 384)]:
    CS2[_name] = _at
    _at += _n
NCS2 = _at


def program(nc, xin, metain, units, cols, cst, cs2, poolm, bc_rows, peer_u, peer_v, mem, rel, out):
    fp32 = mybir.dt.float32
    bf16 = mybir.dt.bfloat16
    u32 = mybir.dt.uint32
    ALU = mybir.AluOpType
    ACT = mybir.ActivationFunctionType
    AX = mybir.AxisListType.X
    ds = bass.ds

    ctx = ExitStack()
    with ctx:
        def sb(name, shape, dt=fp32):
            return ctx.enter_context(nc.sbuf_tensor(name, shape, dt))

        sems = {}

        def S(name):
            if name not in sems:
                sems[name] = ctx.enter_context(nc.semaphore(name))
            return sems[name]

        h = sb("h", [128, 3, D])
        hn = sb("hn", [128, 3, D])
        xT = sb("xT", [128, DC, LTOK])
        wring = sb("wring", [128, R, 1024])
        colc = sb("colc", [128, NCOL])
        cstc = sb("cstc", [128, NCST])
        ss = sb("ss", [128, 32])
        rs = sb("rs", [128, 32])
        zb = sb("zb", [128, 512], bf16)
        bcF = sb("bcF", [128, D])
        hsum = sb("hsum", [128, 48])
        nmx = sb("nmx", [128, 16])

        def cc(name, n, p=128):
            return cstc[0:p, CST[name]:CST[name] + n]

        ident = cc("ident", 128)

        def gcol(name, i=0):
            return colc[:, COL[name] + i:COL[name] + i + 1]

        def gains(name, n):
            return colc[:, COL[name]:COL[name] + DC].unsqueeze(2).to_broadcast([128, DC, n])

        A1W = (NU + NV) * 1024
        a1 = sb("a1", [128, A1W])
        ug = a1[:, 0:NU * 1024].rearrange("p (n d) -> p n d", d=1024)
        vg = a1[:, NU * 1024:A1W].rearrange("p (n d) -> p n d", d=1024)
        A2W = 13840
        a2 = sb("a2", [128, A2W])
        free2 = [0]

        def take2(n, at=None):
            if at is None:
                at = free2[0]
                free2[0] += n
            assert at + n <= A2W, (at, n)
            return a2[:, at:at + n]

        tv = take2(256)
        tif = take2(256)
        bv = take2(128)
        sel_a = take2(128)
        sel_b = take2(128)
        ia = take2(128)
        ib = take2(128)
        gates = [take2(128) for _ in range(3)]
        gm = take2(8)
        gs = take2(8)
        SMALL = free2[0]
        s_m = take2(256)
        hnm = take2(1024)
        qT0 = take2(16 * LTOK).rearrange("p (j t) -> p j t", t=LTOK)
        s_sb0 = [take2(2048), take2(2048)]
        oh0 = take2(2048)
        ti = sb("ti", [128, 256], u32)
        bp = sb("bp", [128, 128], u32)
        pab = sb("pab", [128, 2, 128], u32)
        eidx = sb("eidx", [128, 3, 128], u32)
        ixc = sb("ixc", [128, 2, 16], u32)
        dots = sb("dots", [128, 8])
        gel = sb("gel", [128, 8])
        diag = sb("diag", [128, 4, 128])

        poolP = a1[:, 0:4 * 3 * LTOK].rearrange("p (g s t) -> p g s t", g=4, s=3)
        bcP = a1[:, 4096:5120]
        free2[0] = SMALL
        kT = take2(DC * 384).rearrange("p (c t) -> p c t", t=384)
        vk = take2(3 * D).rearrange("p (s d) -> p s d", d=D)
        LATE = free2[0]
        qT1 = take2(16 * 128).rearrange("p (j t) -> p j t", t=128)
        s_sb1 = take2(2048)
        oh1 = take2(2048)
        free2[0] = LATE
        qhT = take2(DC * 128).rearrange("p (c t) -> p c t", t=128)
        oT = take2(DC * 128).rearrange("p (c t) -> p c t", t=128)
        st = take2(2 * 2 * 768).rearrange("p (b k n) -> p b k n", b=2, k=2)
        sq = take2(D)
        free2[0] = 0
        qkT = take2(20 * SEQ).rearrange("p (j t) -> p j t", t=SEQ)
        vtok = take2(3 * 1024).rearrange("p (k t d) -> p k t d", k=3, t=2)
        biasT = take2(8 * 256).rearrange("p (h y) -> p h y", y=256)
        yT = take2(3 * 1024).rearrange("p (k c t) -> p k c t", k=3, c=4)
        zs = a1[:, 0:3 * 2048].rearrange("p (k t d) -> p k t d", k=3, t=2)
        kmT = a1[:, 6144:7168].rearrange("p (j t) -> p j t", t=SEQ)
        vmem = a1[:, 7168:8192].rearrange("p (t d) -> p t d", t=2)
        pw = a1[:, 8192:8192 + 2048].rearrange("p (b n) -> p b n", b=2)
        mrg = a1[:, 10240:12288].rearrange("p (t d) -> p t d", t=2)
        cs2c = sb("cs2c", [128, NCS2])
        bcG = sb("bcG", [128, 512])
        tsb = sb("tsb", [128, 32])
        aT = a2[:, 0:FFC * SEQ].rearrange("p (j t) -> p j t", t=SEQ)
        up_in = a2[:, 5632:5632 + 2 * 2 * 258].rearrange("p (b k t) -> p b k t", b=2, k=2)
        up_cv = a2[:, 6720:6720 + 2 * 2 * 256].rearrange("p (b k t) -> p b k t", b=2, k=2)
        bcL = a1[:, 0:1024]
        oh2 = sb("rot_tmp", [128, 512])

        ps = ctx.enter_context(nc.psum_tensor("ps", [128, 8, 512], fp32))
        trev_d = nc.dram_tensor("trev_scratch", [8, 384], fp32, kind="Internal").ap()

        def ps2(b, p=128):
            return ps[0:p, b:b + 2, :].rearrange("p a n -> p (a n)")

        U0, n_ = {}, 0
        for name, n in UNITS:
            U0[name] = n_
            n_ += n

        AT, n_ = {}, [0, 0, 0, 0]
        for tag, *k in [("n0", 3, 1, 3, 0), ("f0", 3, 1, 3, 3),
                        ("kvA", 2, 1, 2, 2), ("khA", 0, 1, 2, 2), ("n1A", 1, 1, 1, 1), ("qhA", 0, 1, 1, 1),
                        ("f1A", 1, 1, 1, 1),
                        ("kvB", 1, 1, 1, 1), ("khB", 0, 1, 1, 1), ("n1B", 1, 1, 1, 1), ("qhB", 0, 1, 1, 1),
                        ("f1B", 1, 1, 1, 1), ("nm", 2, 1, 2, 2),
                        ("n2", 2, 1, 2, 2), ("ry", 0, 1, 0, 0), ("yr", 0, 0, 2, 2), ("mg", 0, 0, 2, 2),
                        ("n3", 2, 1, 2, 2), ("n4", 2, 1, 0, 0)]:
            AT[tag] = tuple(n_)
            n_ = [a + b for a, b in zip(n_, k)]

        def tk_number(l, t):
            return [(0, 2), (0, 0), (0, 1), (1, 0), (1, 1)].index((l, t)) + 1

        block = ctx.enter_context(nc.Block())

        @block.sync
        def _(sp):
            for t, (c0, P) in enumerate(TILES[:2]):
                sp.dma_start(h[:, t, :], xin[c0:c0 + P, :]).then_inc(S("ld_h"), 16)
            sp.dma_start(h[0:META, 2, :], metain).then_inc(S("ld_h"), 16)
            sp.dma_start(cstc[:, :], cst).then_inc(S("ld_c"), 16)
            sp.dma_start(colc[:, :], cols).then_inc(S("ld_c"), 16)
            sp.dma_start(poolP.rearrange("p g s t -> p (g s t)"), poolm).then_inc(S("ld_c"), 16)
            sp.dma_start(bcP, bc_rows[2:3, :].to_broadcast([128, D])).then_inc(S("ld_c"), 16)
            sp.dma_start(bcF[:, :], bc_rows[0:1, :].to_broadcast([128, D])).then_inc(S("ld_c"), 16)
            for n in range(R):
                sp.dma_start(wring[:, n, :], units[n, :, :]).then_inc(S(f"w{n}"), 16)
            with sp.Fori(1, N_UNITS // R) as i:
                for s in range(R):
                    sp.wait_ge(S("w_used"), R * i + (s + 1 - R))
                    sp.dma_start(wring[:, s, :], units[ds(R * i + s, 1), :, :].rearrange("o p n -> (o p) n"))\
                        .then_inc(S(f"w{s}"), 16)
            for n in range(N_UNITS // R * R, N_UNITS):
                sp.wait_ge(S("w_used"), n + 1 - R)
                sp.dma_start(wring[:, n % R, :], units[n, :, :]).then_inc(S(f"w{n % R}"), 16)
            for t in range(2):
                sp.wait_ge(S("fin"), t + 1)
                sp.dma_start(out[t * 128:(t + 1) * 128, :], hn[:, t, :]).then_inc(S("stored"), 16)
            sp.wait_ge(S("stored"), 32)

        class Beside:

            def __init__(self, slot, lag=0):
                self.slot, self.lag, self.n = slot, lag, 0

            def to(self, n):
                for k in range(self.n, min(int(n) - self.lag, SLOTS)):
                    self.slot(k)
                    self.n = k + 1

        def gathers(l):
            base = 0 if l == 0 else 16 + 2 * SLOTS
            if l == 0:
                return [(2, 0), (0, 16), (1, 16 + SLOTS)]
            return [(0, base), (1, base + SLOTS)]

        @block.gpsimd
        def _(g):
            g.memset(zb[:, :], 0.0).then_inc(S("zb"), 1)
            g.memset(ss[:, :], 1.0).then_inc(S("zb"), 1)
            g.memset(hsum[:, :], 1.0).then_inc(S("zb"), 1)
            n_idx = [0]

            def indices(half, src):
                g.tensor_copy(ixc[:, half, :], src).then_inc(S("ixc"), 1)

            def slot(l, k, n, half, col):
                if not isinstance(n, int) or n >= NU:
                    g.wait_ge(S("dot"), n + (1 - NU))
                    g.sem_inc(S("u_go"), 1)
                g.indirect_dma_start(ug[:, k % NU, :], None, peer_u,
                                     bass.IndirectOffsetOnAxis(ap=ixc[:, half, col:col + 1], axis=0))\
                    .then_inc(S(f"u{k % NU}"), 16)
                if not isinstance(n, int) or n >= NV:
                    g.wait_ge(S("vsum"), n + (1 - NV))
                    g.sem_inc(S("v_go"), 1)
                g.indirect_dma_start(vg[:, k % NV, :], None, peer_v,
                                     bass.IndirectOffsetOnAxis(ap=ixc[:, half, col:col + 1], axis=0))\
                    .then_inc(S(f"v{k % NV}"), 16)

            for l in range(2):
                for t, base in gathers(l):
                    g.wait_ge(S("eidx"), tk_number(l, t))
                    if t == 2:
                        indices(1, eidx[:, t, 0:16])
                        n_idx[0] += 1
                        g.wait_ge(S("ixc"), n_idx[0])
                        for k in range(16):
                            slot(l, k, base + k, 1, k)
                        continue
                    done = n_idx[0]
                    with g.Fori(0, SLOTS // GB) as i:
                        for half in range(2):
                            indices(half, eidx[:, t, ds(i * GB + 16 * half, 16)])
                            g.wait_ge(S("ixc"), 2 * i + (done + half + 1))
                            for kk in range(16):
                                k = 16 * half + kk
                                slot(l, k, GB * i + (base + k), half, kk)
                    n_idx[0] += 2 * (SLOTS // GB)
            g.wait_ge(S("vsum"), 16 + 4 * SLOTS)
            g.wait_ge(S("y"), 5)
            for t in range(2):
                g.dma_start(mrg[:, t, :], mem[t * 128:(t + 1) * 128, :]).then_inc(S("ld_m"), 16)
            g.dma_start(cs2c[:, :], cs2).then_inc(S("ld_m"), 16)
            g.dma_start(bcG[:, :], bc_rows[3:4, 0:512].to_broadcast([128, 512])).then_inc(S("ld_m"), 16)
            g.dma_start(tsb[0:32, 0:8], rel).then_inc(S("ld_m"), 16)
            g.wait_ge(S("trev_sb"), 1)
            g.dma_start(trev_d, pw[0:8, 0, 0:384]).then_inc(S("trev_d"), 16)
            g.wait_ge(S("trev_d"), 16)
            rows = bass.AP(trev_d.tensor, 0, [[1, 128], [384, 8], [1, 256]])
            g.dma_start(pw.rearrange("p b n -> p (b n)").rearrange("p (h y) -> p h y", y=256), rows)\
                .then_inc(S("ld_b"), 16)
            g.wait_ge(S("out_h"), 2)
            g.dma_start(bcL, bc_rows[4:5, :].to_broadcast([128, D])).then_inc(S("ld_g"), 16)

        @block.tensor
        def _(pe):
            owed = {}

            def claim(*banks):
                for b in banks:
                    if b in owed:
                        pe.wait_ge(*owed.pop(b))

            def owe(sem, val, *banks):
                for b in banks:
                    owed[b] = (S(sem), val)

            unit_n = [0]

            def unit():
                n = unit_n[0]
                unit_n[0] += 1
                pe.wait_ge(S(f"w{n % R}"), 16 * (n // R + 1))
                return wring[:, n % R, :]

            def used(ins):
                ins.then_inc(S("w_used"), 1)

            def transposes(tag, src, tiles, chunks=DC, tb=6):
                for n, t in enumerate(tiles):
                    P = TILES[t][1]
                    pe.wait_ge(S("x_ready"), AT[tag][2] + n + 1)
                    claim(tb, tb + 1)
                    for c in range(chunks):
                        last = nc.tensor.transpose(ps2(tb)[:, c * 128:c * 128 + P],
                                                   src(t)[:, c * 128:(c + 1) * 128], ident[0:P, 0:P])
                    last.then_inc(S("turned"), 1)
                    owe("turned_out", AT[tag][3] + n + 1, tb, tb + 1)

            def tokens_out(lhs, tiles, chunks, reader, b0=0, first=0, between=None):
                for n, t in enumerate(tiles):
                    claim(b0 + 2 * n, b0 + 2 * n + 1)
                for c in range(chunks):
                    w = unit()
                    for n, t in enumerate(tiles):
                        c0, P = TILES[t]
                        for j in range(2):
                            last = nc.tensor.matmul(ps[0:P, b0 + 2 * n + j, :], lhs(c, c0, P),
                                                    w[:, j * 512:(j + 1) * 512], start=c == 0, stop=c == chunks - 1)
                    used(last)
                    if between:
                        between(c + 1)
                for n, t in enumerate(tiles):
                    owe(reader, first + n + 1, b0 + 2 * n, b0 + 2 * n + 1)

            def cols_out(J, N, reader, banks, first=0, between=None, c0=0):
                for j in range(J):
                    w = unit()
                    b = banks[j % len(banks)]
                    claim(b)
                    for c in range(DC):
                        last = nc.tensor.matmul(ps[:, b, 0:N], w[:, c * 128:(c + 1) * 128], xT[:, c, c0:c0 + N],
                                                start=c == 0, stop=c == DC - 1)
                    used(last)
                    owe(reader, first + j + 1, b)
                    if between:
                        between(j + 1)

            def x_at(c, c0, P):
                return xT[:, c, c0:c0 + P]

            pe.wait_ge(S("ld_c"), 80)
            pe.wait_ge(S("zb"), 3)
            pe.wait_ge(S("x_ready"), AT["n0"][2] + 3)
            for c in range(DC):
                b = c % 6
                claim(b)
                for s, (c0, P) in enumerate(TILES):
                    last = nc.tensor.matmul(ps[:, b, 0:LTOK], hn[0:P, s, c * 128:(c + 1) * 128],
                                            poolP[0:P, c // 2, s, :], start=s == 0, stop=s == 2)
                last.then_inc(S("pool_pe"), 1)
                owe("pool_ev", c + 1, b)
            pe.wait_ge(S("pool_ev"), DC)
            claim(0, 1, 2, 3, 4, 5)
            for u in range(2):
                w = unit()
                for t, (c0, P) in enumerate(TILES):
                    for g in range(2):
                        for c in range(2):
                            last = nc.tensor.matmul(ps[0:P, 2 * t + u, g * 256:(g + 1) * 256],
                                                    xT[:, 4 * u + 2 * g + c, c0:c0 + P],
                                                    w[:, (2 * g + c) * 256:(2 * g + c + 1) * 256],
                                                    start=c == 0, stop=c == 1)
                used(last)
            for t in range(3):
                owe("mix0_ps", t + 1, 2 * t, 2 * t + 1)

            def scores(order, qT, reader, first, tick):
                ks = [unit(), unit()]
                for n, t in enumerate(order):
                    c0, P = TILES[t]
                    q0 = c0 if reader == "sc0_ev" else 0
                    claim(0, 1, 2, 3)
                    for j in range(16):
                        last = nc.tensor.matmul(ps[0:P, j // 4, (j % 4) * 128:(j % 4 + 1) * 128],
                                                qT[:, j, q0:q0 + P], ks[j // 8][:, (j % 8) * 128:(j % 8 + 1) * 128],
                                                start=True, stop=True)
                    last.then_inc(S(tick), 1)
                    owe(reader, first + n + 1, 0, 1, 2, 3)
                claim(5)
                for _ in ks:
                    used(nc.tensor.matmul(ps[0:1, 5, 0:2], zb[:, 0:1], zb[:, 0:2], start=True, stop=True))

            def sums_begin(P):
                claim(6, 7)
                for j in range(2):
                    nc.tensor.matmul(ps[0:P, 6 + j, :], zb[:, 0:P], zb[:, :], start=True, stop=False)

            def sums_slot(P, k, n, vfill):
                pe.wait_ge(S("diag"), n + 1)
                pe.wait_ge(S(f"v{k % NV}"), vfill)
                for j in range(2):
                    last = nc.tensor.matmul(ps[0:P, 6 + j, :], diag[:, k % 4, 0:P],
                                            vg[:, k % NV, j * 512:(j + 1) * 512], start=False, stop=False)
                last.then_inc(S("vsum"), 1)

            def sums_end(t, m):
                P = TILES[t][1]
                for j in range(2):
                    last = nc.tensor.matmul(ps[0:P, 6 + j, :], ident[0:P, 0:P],
                                            h[0:P, t, j * 512:(j + 1) * 512], start=False, stop=True)
                last.then_inc(S("y_pe"), 1)
                owe("y", m, 6, 7)

            def sums_loop(base, start=0):
                with pe.Fori(start // GB, SLOTS // GB) as i:
                    for k in range(GB):
                        sums_slot(128, k, GB * i + (base + k), 16 * (GB // NV) * i + 16 * ((base + k) // NV + 1))

            def beside(base):
                return Beside(lambda k: sums_slot(128, k, base + k, 16 * ((base + k) // NV + 1)), LAG)

            transposes("f0", lambda t: hn[0:TILES[t][1], t, :], [0, 1, 2])
            pe.wait_ge(S("turned_out"), AT["f0"][3] + 3)
            cols_out(16, LTOK, "q0_ev", range(6))
            pe.wait_ge(S("q0_ev"), 16)
            scores([2, 0, 1], qT0, "sc0_ev", 0, "sc0_pe")
            (_, m_base), (_, a_base), (_, b_base) = gathers(0)
            sums_begin(META)
            for k in range(16):
                sums_slot(META, k, m_base + k, 16 * ((m_base + k) // NV + 1))
            sums_end(2, 1)
            sums_begin(128)
            first = beside(a_base)
            first.to(GB + LAG)
            sums_loop(a_base, GB)
            sums_end(0, 2)

            def front(i, bg):
                X = "AB"[i]
                kvt = [0, 2] if i == 0 else [1]
                c0 = TILES[i][0]
                plan = PLAN[i]

                def at(stage, j=0, J=1):
                    a = plan[stage]
                    bg.to(a + (plan[STAGES[STAGES.index(stage) + 1]] - a) * j / J)

                hT = lambda t: hn[0:TILES[t][1], t, :]
                at("kv")
                transposes("kv" + X, hT, kvt, tb=4)
                at("k")
                pe.wait_ge(S("turned_out"), AT["kv" + X][3] + len(kvt))
                tokens_out(x_at, kvt, DC, "k_ev", first=2 * i, between=lambda c: at("k", c, DC))
                tokens_out(x_at, kvt, DC, "v_ev", first=2 * i, between=lambda c: at("v", c, DC))
                at("kh")
                transposes("kh" + X, hT, kvt, tb=4)
                at("n1")
                transposes("n1" + X, hT, [i], tb=4)
                at("q")
                pe.wait_ge(S("turned_out"), AT["n1" + X][3] + 1)
                tokens_out(x_at, [i], DC, "q_ev", first=i, between=lambda c: at("q", c, DC))
                at("qh")
                transposes("qh" + X, hT, [i], tb=4)
                pe.wait_ge(S("turned_out"), AT["qh" + X][3] + 1)
                pe.wait_ge(S("v_ev"), 2 + i)
                stick(i, lambda p: at("stick", p, 8))
                at("o")
                pe.wait_ge(S("o_ev"), 16 * (i + 1))
                tokens_out(lambda c, c0, P: oT[:, c, 0:P], [i], DC, "wo_h", first=i,
                           between=lambda c: at("o", c, DC))
                at("f1")
                transposes("f1" + X, hT, [i], tb=4)
                at("wq")
                pe.wait_ge(S("turned_out"), AT["f1" + X][3] + 1)
                cols_out(16, 128, "q1_ev", range(4), first=16 * i, c0=c0, between=lambda j: at("wq", j, 16))
                at("sc")
                pe.wait_ge(S("q1_ev"), 16 * (i + 1))
                scores([i], qT1, "sc1_ev", i, "sc1_pe")
                bg.to(SLOTS + LAG)

            def stick(i, tick):
                kt = [0, 2] if i == 0 else [0, 1, 2]
                nk = len(kt)
                ones, tri = cc("ones", 128), cc("tri", 128)

                def z(p):
                    n = 8 * i + p
                    claim(0, 1)
                    for r in range(2):
                        rows = slice(64 * r, 64 * r + 64)
                        for a, k in enumerate(kt):
                            last = nc.tensor.matmul(ps[:, r, a * 128:(a + 1) * 128], kT[rows, p, k * 128:(k + 1) * 128],
                                                    qhT[rows, p, :], start=True, stop=True)
                    last.then_inc(S("z_pe"), 1)
                    owe("z_sb", n + 1, 0, 1)

                def after(p):
                    n = 8 * i + p
                    sp_ = st[:, p % 2, 1, 0:nk * 256].rearrange("p (r k n) -> p r k n", r=2, k=nk)
                    pe.wait_ge(S("sp"), n + 1)
                    claim(2, 3)
                    for a in range(nk):
                        later = list(range(a + 1, nk - 1)) if a < nk - 1 else list(range(nk - 1))
                        out_ = ps2(2)[:, a * 256:(a + 1) * 256]
                        last = nc.tensor.matmul(out_, tri, sp_[:, :, a, :], start=True, stop=not later)
                        for b in later:
                            last = nc.tensor.matmul(out_, ones, sp_[:, :, b, :], start=False, stop=b == later[-1])
                    last.then_inc(S("c_pe"), 1)
                    owe("dd", n + 1, 2, 3)

                def values(p):
                    n = 8 * i + p
                    w_ = st[:, p % 2, 0, 0:nk * 256].rearrange("p (r k n) -> p r k n", r=2, k=nk)
                    pe.wait_ge(S("w"), n + 1)
                    for r in range(2):
                        rows = slice(64 * r, 64 * r + 64)
                        claim(4 + r)
                        v = slice(p * 128 + 64 * r, p * 128 + 64 * r + 64)
                        for a, k in enumerate(kt):
                            last = nc.tensor.matmul(ps[rows, 4 + r, 0:128], vk[:, k, v], w_[:, r, a, :],
                                                    start=a == 0, stop=a == nk - 1)
                        owe("o_ev", 2 * n + r + 1, 4 + r)
                    last.then_inc(S("o_pe"), 1)

                z(0)
                for p in range(8):
                    tick(p)
                    if p < 7:
                        z(p + 1)
                    after(p)
                    if p:
                        values(p - 1)
                values(7)

            sums_begin(128)
            front(0, beside(b_base))
            sums_end(1, 3)
            (_, a_base), (_, b_base) = gathers(1)
            sums_begin(128)
            front(1, beside(a_base))
            sums_end(0, 4)
            sums_begin(128)
            sums_loop(b_base)
            sums_end(1, 5)

            transposes("nm", lambda t: hn[0:128, t, :], [0, 1])
            pe.wait_ge(S("turned_out"), AT["nm"][3] + 2)
            cols_out(4, SEQ, "m_ev", [0, 1, 2, 3])

            def halves_out(reader, val, b0):
                claim(b0, b0 + 1)
                for u in range(4):
                    w = unit()
                    for c in range(2):
                        for t in range(2):
                            last = nc.tensor.matmul(ps[:, b0 + t, :], xT[:, 2 * u + c, t * 128:t * 128 + 128],
                                                    w[:, c * 512:(c + 1) * 512], start=u + c == 0, stop=u + c == 4)
                    used(last)
                owe(reader, val, b0, b0 + 1)

            halves_out("m_ev", 6, 4)
            pe.wait_ge(S("ld_m"), 80)
            claim(6)
            nc.tensor.matmul(ps[0:8, 6, 0:384], tsb[0:32, 0:8], cs2c[0:32, CS2["bucket"]:CS2["bucket"] + 384],
                             start=True, stop=True).then_inc(S("trev_pe"), 1)
            owe("trev_sb", 1, 6)
            transposes("n2", lambda t: hn[0:128, t, :], [0, 1])
            pe.wait_ge(S("turned_out"), AT["n2"][3] + 2)
            cols_out(20, SEQ, "iT_ev", range(6))
            for k in range(3):
                halves_out("iv_ev", 2 * k + 2, 2 * k)
            for k in range(3):
                tokens_out(x_at, [0, 1], DC, f"z{k}_ev", b0=4 * (k % 2))

            for j in range(8):
                b = j % 2
                pe.wait_ge(S("iT_ev"), 8 + j + 1)
                claim(b)
                nc.tensor.matmul(ps[:, b, 0:256], cs2c[:, 0:128], qkT[:, 8 + j, :], start=True, stop=True)\
                    .then_inc(S("sw_pe"), 1)
                owe("rot_ps", j + 1, b)
            for hd in range(4):
                b = 2 + hd % 2
                pe.wait_ge(S("rot"), 4 + hd + 1)
                claim(b)
                nc.tensor.matmul(ps[:, b, 0:256], qkT[:, 12 + hd, 0:128], qkT[:, 8 + hd, :], start=True, stop=True)
                nc.tensor.matmul(ps[:, b, 256:384], qkT[:, 12 + hd, 128:256], qkT[:, 8 + hd, 128:256],
                                 start=True, stop=True).then_inc(S("rs_pe"), 1)
                owe("rs_sb", hd + 1, b)
            pe.wait_ge(S("iv_ev"), 4)
            claim(6, 7)
            for hd in range(4):
                e = slice(hd * 128, hd * 128 + 128)
                sT = mrg[:, hd // 2, (hd % 2) * 384:(hd % 2) * 384 + 384]
                pe.wait_ge(S("rs_sb"), hd + 1)
                nc.tensor.matmul(ps[:, 6, e], sT[:, 0:128], vtok[:, 1, 0, e], start=True, stop=True)
                nc.tensor.matmul(ps[:, 7, e], sT[:, 128:256], vtok[:, 1, 0, e], start=True, stop=False)
                nc.tensor.matmul(ps[:, 7, e], sT[:, 256:384], vtok[:, 1, 1, e], start=False, stop=True)\
                    .then_inc(S("ry_pe"), 1)
            owe("ry_ps", 1, 6, 7)

            def soft_s(n):
                b = n % 2
                claim(b)
                if n < 8:
                    c, r = n // 2, slice(64 * (n % 2), 64 * (n % 2) + 64)
                    nc.tensor.matmul(ps[:, b, 0:128], qkT[r, c, 0:128], qkT[r, 4 + c, 0:128], start=True, stop=True)
                    nc.tensor.matmul(ps[:, b, 128:384], qkT[r, c, 128:256], qkT[r, 4 + c, :], start=True, stop=True)\
                        .then_inc(S("ss_pe"), 1)
                else:
                    for t in range(2):
                        last = nc.tensor.matmul(ps[:, b, t * 256:(t + 1) * 256],
                                                qkT[:, 16 + n - 8, t * 128:(t + 1) * 128], kmT[:, n - 8, :],
                                                start=True, stop=True)
                    last.then_inc(S("ss_pe"), 1)
                owe("ss_ps", n + 1, b)

            def soft_t(n):
                b = 2 + n % 2
                p_ = pw[:, n % 2, :]
                pe.wait_ge(S("pn"), n + 1)
                claim(b)
                if n < 8:
                    order = [(0, 0), (1, 128), (2, 256)]
                else:
                    order = [(0, 0), (2, 128), (1, 256), (3, 384)]
                for src, dst in order:
                    last = nc.tensor.transpose(ps[:, b, dst:dst + 128], p_[:, src * 128:(src + 1) * 128], ident)
                last.then_inc(S("pt_pe"), 1)
                owe("pt_ev", n + 1, b)

            def soft_o(n):
                b = 4 + n % 2
                pT_ = pw[:, n % 2, 512:1024]
                pe.wait_ge(S("pt_ev"), n + 1)
                claim(b)
                if n < 8:
                    c, r = n // 2, slice(64 * (n % 2), 64 * (n % 2) + 64)
                    v = slice(n * 64, n * 64 + 64)
                    nc.tensor.matmul(ps[r, b, 0:256], vtok[:, 0, 0, v], pT_[:, 0:256], start=True, stop=False)
                    nc.tensor.matmul(ps[r, b, 128:256], vtok[:, 0, 1, v], pT_[:, 256:384], start=False, stop=True)\
                        .then_inc(S("so_pe"), 1)
                else:
                    v = slice((n - 8) * 128, (n - 8) * 128 + 128)
                    nc.tensor.matmul(ps[:, b, 0:256], vmem[:, 0, v], pT_[:, 0:256], start=True, stop=False)
                    nc.tensor.matmul(ps[:, b, 0:256], vmem[:, 1, v], pT_[:, 256:512], start=False, stop=True)\
                        .then_inc(S("so_pe"), 1)
                owe("so_ev", n + 1, b)

            pe.wait_ge(S("ld_b"), 16)
            claim(0, 1, 2, 3)
            for j in range(4):
                last = nc.tensor.matmul(ps[:, j, :], cs2c[:, CS2["flip"]:CS2["flip"] + 128],
                                        pw.rearrange("p b n -> p (b n)")[:, j * 512:(j + 1) * 512],
                                        start=True, stop=True)
            last.then_inc(S("flip_pe"), 1)
            owe("bias", 1, 0, 1, 2, 3)
            soft_s(0)
            for n in range(12):
                if n < 11:
                    soft_s(n + 1)
                soft_t(n)
                if n:
                    soft_o(n - 1)
            soft_o(11)
            transposes("yr", lambda t: hn[:, 0, t * 512:(t + 1) * 512], [0, 1], chunks=4)
            pe.wait_ge(S("so_ev"), 12)
            pe.wait_ge(S("turned_out"), AT["yr"][3] + 2)
            for k in range(3):
                tokens_out(lambda c, c0, P: yT[:, k, c, c0:c0 + P], [0, 1], 4, f"br{k}_ps", b0=0 if k != 1 else 4)
            transposes("mg", lambda t: mrg[:, t, :], [0, 1])
            pe.wait_ge(S("turned_out"), AT["mg"][3] + 2)
            tokens_out(x_at, [0, 1], DC, "out_h")
            transposes("n3", lambda t: hn[0:128, t, :], [0, 1])
            pe.wait_ge(S("turned_out"), AT["n3"][3] + 2)
            cols_out(2 * FFC, SEQ, "up_ev", range(6))
            claim(0, 1, 2, 3)
            for c in range(FFC):
                w = unit()
                pe.wait_ge(S("a_T"), c + 1)
                for t in range(2):
                    for j in range(2):
                        last = nc.tensor.matmul(ps[:, 2 * t + j, :], aT[:, c, t * 128:(t + 1) * 128],
                                                w[:, j * 512:(j + 1) * 512], start=c == 0, stop=c == FFC - 1)
                used(last)

        @block.scalar
        def _(act):
            def squares(tag, src, dst, tiles, col):
                for n, t in enumerate(tiles):
                    P = TILES[t][1]
                    nc.scalar.activation(dst(t), src(t), ACT.Square, accum_out=ss[0:P, col + n:col + n + 1])\
                        .then_inc(S("squared"), 1)

            def root(tag, ap):
                act.wait_ge(S("var_ready"), AT[tag][1] + 1)
                nc.scalar.activation(ap, ap, ACT.Sqrt).then_inc(S("std_ready"), 1)

            def hT(t):
                return hn[0:TILES[t][1], t, :]

            def hh(t):
                return h[0:TILES[t][1], t, :]

            def t_out(tag, tiles, dst, scale=1.0, tb=6):
                for n, t in enumerate(tiles):
                    c0, P = TILES[t]
                    act.wait_ge(S("turned"), AT[tag][3] + n + 1)
                    nc.scalar.activation(dst(c0, P), ps2(tb).rearrange("p (c n) -> p c n", n=128)[:, :, 0:P],
                                         ACT.Copy, scale=scale).then_inc(S("turned_out"), 1)

            def tokens_ev(units_done, tiles, dst, sem, func=ACT.Copy, b0=0):
                act.wait_ge(S("w_used"), units_done)
                for n, t in enumerate(tiles):
                    nc.scalar.activation(dst(t), ps2(b0 + 2 * n, TILES[t][1]), func).then_inc(S(sem), 1)

            act.wait_ge(S("ld_h"), 48)
            act.wait_ge(S("ld_c"), 80)
            act.wait_ge(S("zb"), 3)
            squares("n0", hh, hT, [0, 1, 2], 0)
            root("n0", rs[:, 0:3])
            for c in range(DC):
                act.wait_ge(S("pool_pe"), c + 1)
                nc.scalar.activation(xT[:, c, :], ps[:, c % 6, 0:LTOK], ACT.Copy, scale=gcol("mix0", c))\
                    .then_inc(S("pool_ev"), 1)

            def gelu(k, n):
                act.wait_ge(S("dot"), n + 1)
                nc.scalar.activation(gel[:, k % 8:k % 8 + 1], dots[:, k % 8:k % 8 + 1], ACT.Gelu)\
                    .then_inc(S("gelu"), 1)

            def gelu_loop(base, start=0):
                with act.Fori(start // GB, SLOTS // GB) as i:
                    for k in range(GB):
                        gelu(k, GB * i + (base + k))

            def beside(base):
                return Beside(lambda k: gelu(k, base + k))

            def y_out(t, m):
                act.wait_ge(S("y_pe"), m)
                nc.scalar.activation(hh(t), ps2(6, TILES[t][1]), ACT.Copy).then_inc(S("y"), 1)

            def gate_exps(l, t):
                act.wait_ge(S("gx"), tk_number(l, t))
                G = gates[t][:, 0:16 if t == 2 else 128]
                nc.scalar.activation(G, G, ACT.Exp).then_inc(S("ge"), 1)

            act.wait_ge(S("mix0_h"), 3)
            squares("f0", hh, hT, [0, 1, 2], 3)
            root("f0", rs[:, 3:6])
            t_out("f0", [0, 1, 2], lambda c0, P: xT[:, :, c0:c0 + P])
            for j in range(16):
                act.wait_ge(S("w_used"), U0["wq"] + j + 1)
                nc.scalar.activation(qT0[:, j, :], ps[:, j % 6, 0:LTOK], ACT.Copy).then_inc(S("q0_ev"), 1)
            for n, t in enumerate([2, 0, 1]):
                P = TILES[t][1]
                act.wait_ge(S("sc0_pe"), n + 1)
                if t == 1:
                    act.wait_ge(S("md"), 128)
                nc.scalar.activation(s_sb0[0 if t == 0 else 1][0:P, :], ps[0:P, 0:4, :].rearrange("p b n -> p (b n)"),
                                     ACT.Copy).then_inc(S("sc0_ev"), 1)
                if t == 2:
                    act.wait_ge(S("sc0_ev"), 1)
                    for hd in range(PEER_H):
                        r = slice(hd * META, (hd + 1) * META)
                        act.dma_start(s_m[r, :], s_sb0[1][0:META, hd * 256:(hd + 1) * 256]).then_inc(S("md"), 16)
                    for hd in range(PEER_H):
                        r = slice(hd * META, (hd + 1) * META)
                        act.dma_start(hnm[r, :], hn[0:META, 2, :]).then_inc(S("md2"), 16)
            act.wait_ge(S("x_ready"), AT["f0"][2] + 3)
            act.dma_start(bcF[:, :], bc_rows[1:2, :].to_broadcast([128, D])).then_inc(S("ld_f1"), 16)
            gate_exps(0, 2)
            (_, m_base), (_, a_base), (_, b_base) = gathers(0)
            for k in range(16):
                if k == 14:
                    gate_exps(0, 0)
                gelu(k, m_base + k)
            y_out(2, 1)
            first = beside(a_base)
            first.to(20)
            gate_exps(0, 1)
            first.to(GB)
            gelu_loop(a_base, GB)
            y_out(0, 2)

            def front(i, bg):
                X = "AB"[i]
                kvt = [0, 2] if i == 0 else [1]
                plan = PLAN[i]

                def at(stage, j=0, J=1):
                    a = plan[stage]
                    bg.to(a + (plan[STAGES[STAGES.index(stage) + 1]] - a) * j / J)

                at("kv")
                act.wait_ge(S("y"), 2 + i)
                squares("kv" + X, hh, hT, kvt, (6, 8)[i])
                root("kv" + X, rs[:, (6, 8)[i]:(6, 8)[i] + len(kvt)])
                at("v")
                tokens_ev(U0["k" + X] + 8, kvt, hT, "k_ev")
                root("kh" + X, hsum[:, 0:16 * len(kvt)])
                at("kh")
                act.wait_ge(S("kv_zero"), 1)
                tokens_ev(U0["v" + X] + 8, kvt, lambda t: vk[0:TILES[t][1], t, :], "v_ev")
                t_out("kh" + X, kvt, lambda c0, P: kT[:, :, c0:c0 + P], gcol("knorm"), tb=4)
                at("n1")
                squares("n1" + X, hh, hT, [i], 9 + i)
                root("n1" + X, rs[:, 9 + i:10 + i])
                at("qh")
                tokens_ev(U0["q" + X] + 8, [i], hT, "q_ev")
                root("qh" + X, hsum[:, 0:16])
                t_out("qh" + X, [i], lambda c0, P: qhT[:, :, 0:P], gcol("qnorm"), tb=4)
                stick(i, lambda p: at("stick", p, 8))
                at("f1")
                act.wait_ge(S("wo_h"), i + 1)
                squares("f1" + X, hh, hT, [i], 11 + i)
                root("f1" + X, rs[:, 11 + i:12 + i])
                t_out("f1" + X, [i], lambda c0, P: xT[:, :, c0:c0 + P], tb=4)
                for j in range(16):
                    at("wq", j + 1, 16)
                    act.wait_ge(S("w_used"), U0["wq" + X] + j + 1)
                    nc.scalar.activation(qT1[:, j, :], ps[:, j % 4, 0:128], ACT.Copy).then_inc(S("q1_ev"), 1)
                at("topk")
                act.wait_ge(S("sc1_pe"), i + 1)
                nc.scalar.activation(s_sb1[:, :], ps[:, 0:4, :].rearrange("p b n -> p (b n)"), ACT.Copy)\
                    .then_inc(S("sc1_ev"), 1)
                at("topk", GATE_AT, TOPK_STEPS)
                gate_exps(1, i)
                bg.to(SLOTS)

            def stick(i, tick):
                nk = 2 + i

                def front_(p):
                    n = 8 * i + p
                    t_ = st[:, p % 2, 1, 0:nk * 256]
                    act.wait_ge(S("tmin"), n + 1)
                    nc.scalar.activation(t_, t_, ACT.Exp).then_inc(S("ex"), 1)
                    act.wait_ge(S("ex"), n + 1)
                    nc.scalar.activation(t_, t_, ACT.Ln, bias=1.0).then_inc(S("ln"), 1)

                def weights(p):
                    n = 8 * i + p
                    w_ = st[:, p % 2, 0, 0:nk * 256]
                    act.wait_ge(S("dd"), n + 1)
                    nc.scalar.activation(w_, w_, ACT.Exp).then_inc(S("w"), 1)

                def out_(p):
                    n = 8 * i + p
                    act.wait_ge(S("o_pe"), n + 1)
                    for r in range(2):
                        rows = slice(64 * r, 64 * r + 64)
                        nc.scalar.activation(oT[rows, p, :], ps[rows, 4 + r, 0:128], ACT.Copy).then_inc(S("o_ev"), 1)

                front_(0)
                for p in range(8):
                    tick(p)
                    if p:
                        out_(p - 1)
                    weights(p)
                    if p < 7:
                        front_(p + 1)
                out_(7)

            front(0, beside(b_base))
            y_out(1, 3)
            (_, a_base), (_, b_base) = gathers(1)
            front(1, beside(a_base))
            y_out(0, 4)
            gelu_loop(b_base)
            y_out(1, 5)

            act.wait_ge(S("ld_m"), 80)
            squares("nm", lambda t: mrg[:, t, :], hT, [0, 1], 15)
            root("nm", rs[:, 15:17])
            for j in range(4):
                act.wait_ge(S("w_used"), U0["mem_k"] + j + 1)
                nc.scalar.activation(kmT[:, j, :], ps[:, j, 0:256], ACT.Copy).then_inc(S("m_ev"), 1)
            act.wait_ge(S("w_used"), U0["mem_v"] + 4)
            for t in range(2):
                nc.scalar.activation(vmem[:, t, :], ps[:, 4 + t, :], ACT.Copy).then_inc(S("m_ev"), 1)
            act.wait_ge(S("y"), 5)
            squares("n2", hh, hT, [0, 1], 13)
            root("n2", rs[:, 13:15])
            for j in range(20):
                act.wait_ge(S("w_used"), U0["in_T"] + j + 1)
                nc.scalar.activation(qkT[:, j, :], ps[:, j % 6, 0:256], ACT.Copy).then_inc(S("iT_ev"), 1)
            for k in range(3):
                act.wait_ge(S("w_used"), U0["in_v"] + 4 * k + 4)
                for t in range(2):
                    nc.scalar.activation(vtok[:, k, t, :], ps[:, 2 * k + t, :], ACT.Copy if k < 2 else ACT.Sigmoid)\
                        .then_inc(S("iv_ev" if k < 2 else "sg"), 1)
            for k in range(3):
                tokens_ev(U0["in_z"] + 8 * k + 8, [0, 1], lambda t: zs[:, k, t, :], f"z{k}_ev", ACT.Sigmoid, 4 * (k % 2))
            root("ry", tsb[:, 16:24])
            act.wait_ge(S("flip_pe"), 1)
            nc.scalar.activation(biasT.rearrange("p h y -> p (h y)"), ps[:, 0:4, :].rearrange("p b n -> p (b n)"),
                                 ACT.Copy).then_inc(S("bias"), 1)

            def soft_e(n):
                p_ = pw[:, n % 2, :]
                act.wait_ge(S("nmx"), n + 1)
                if n >= 2:
                    act.wait_ge(S("pt_pe"), n - 1)
                if n < 8:
                    spans, src, scale = [(0, 128), (128, 384)], p_, 1.0
                else:
                    spans, src, scale = [(0, 256), (256, 512)], ps[:, n % 2, :], RET_DK ** -0.5
                for t, (a, b) in enumerate(spans):
                    col = 8 * (n % 2) + t
                    nc.scalar.activation(p_[:, a:b], src[:, a:b], ACT.Exp, bias=nmx[:, col:col + 1], scale=scale,
                                         accum_out=nmx[:, col + 2:col + 3]).then_inc(S("pe_"), 1)

            def soft_tev(n):
                b = 2 + n % 2
                w_ = 384 if n < 8 else 512
                act.wait_ge(S("pt_pe"), n + 1)
                if n >= 2:
                    act.wait_ge(S("so_pe"), n - 1)
                nc.scalar.activation(pw[:, n % 2, 512:512 + w_], ps[:, b, 0:w_], ACT.Copy).then_inc(S("pt_ev"), 1)

            def soft_oev(n):
                act.wait_ge(S("so_pe"), n + 1)
                if n < 8:
                    c, r = n // 2, slice(64 * (n % 2), 64 * (n % 2) + 64)
                    dst = yT[r, 0, c, :]
                else:
                    r = slice(0, 128)
                    dst = yT[:, 2, n - 8, :]
                nc.scalar.activation(dst, ps[r, 4 + n % 2, 0:256], ACT.Copy).then_inc(S("so_ev"), 1)

            soft_e(0)
            for n in range(12):
                if n < 11:
                    soft_e(n + 1)
                soft_tev(n)
                if n:
                    soft_oev(n - 1)
            soft_oev(11)
            for t in range(2):
                act.wait_ge(S("turned"), AT["yr"][3] + t + 1)
                nc.scalar.activation(yT[:, 1, :, t * 128:(t + 1) * 128],
                                     ps[:, 6, :].rearrange("p (c n) -> p c n", n=128), ACT.Copy)\
                    .then_inc(S("turned_out"), 1)
            t_out("mg", [0, 1], lambda c0, P: xT[:, :, c0:c0 + P])
            act.wait_ge(S("out_h"), 2)
            squares("n3", hh, hT, [0, 1], 17)
            root("n3", rs[:, 17:19])
            for j in range(FFC):
                for k in range(2):
                    act.wait_ge(S("w_used"), U0["up"] + 2 * j + k + 1)
                    if j >= 2:
                        act.wait_ge(S("cv"), 2 * (j - 2) + k + 1)
                    else:
                        act.wait_ge(S("padded"), 1)
                    nc.scalar.activation(up_in[:, j % 2, k, 2:258], ps[:, (2 * j + k) % 6, 0:256], ACT.Copy)\
                        .then_inc(S("up_ev"), 1)
                act.wait_ge(S("cv"), 2 * j + 1)
                nc.scalar.activation(up_cv[:, j % 2, 0, :], up_cv[:, j % 2, 0, :], ACT.Gelu).then_inc(S("gate"), 1)
            act.wait_ge(S("down_h"), 2)
            squares("n4", hh, hT, [0, 1], 19)
            root("n4", rs[:, 19:21])

        @block.vector
        def _(dve):
            chain = [0]

            def link(ins):
                chain[0] += 1
                ins.then_inc(S("dve_chain"), 1)
                dve.wait_ge(S("dve_chain"), chain[0])

            v = nc.vector

            def hT(t):
                return hn[0:TILES[t][1], t, :]

            def hh(t):
                return h[0:TILES[t][1], t, :]

            def rstd(tag, src, dst, n_wait, width):
                if n_wait:
                    dve.wait_ge(S("squared"), AT[tag][0] + n_wait)
                v.tensor_scalar(dst, src, 1.0 / width, EPS, ALU.mult, ALU.add).then_inc(S("var_ready"), 1)
                dve.wait_ge(S("std_ready"), AT[tag][1] + 1)
                link(v.reciprocal(dst, dst))

            def norm(tag, tiles, col, src=hh, gain=None):
                rstd(tag, ss[:, col:col + len(tiles)], rs[:, col:col + len(tiles)], len(tiles), D)
                for n, t in enumerate(tiles):
                    P = TILES[t][1]
                    r = rs[0:P, col + n:col + n + 1]
                    if gain is None:
                        i = v.tensor_scalar(hT(t), src(t), r, None, ALU.mult)
                    else:
                        i = v.scalar_tensor_tensor(hT(t), src(t), r, gain[0:P, :], ALU.mult, ALU.mult)
                    i.then_inc(S("x_ready"), 1)

            def t_out(tag, tiles, gain, free=None, tb=6):
                if free is not None:
                    dve.wait_ge(S("w_used"), free)
                for n, t in enumerate(tiles):
                    c0, P = TILES[t]
                    dve.wait_ge(S("turned"), AT[tag][3] + n + 1)
                    v.tensor_tensor(xT[:, :, c0:c0 + P], ps2(tb).rearrange("p (c n) -> p c n", n=128)[:, :, 0:P],
                                    gains(gain, P), ALU.mult).then_inc(S("turned_out"), 1)

            def add_h(units_done, sem, tiles):
                dve.wait_ge(S("w_used"), units_done)
                for n, t in enumerate(tiles):
                    v.tensor_tensor(hh(t), hh(t), ps2(2 * n, TILES[t][1]), ALU.add).then_inc(S(sem), 1)

            dve.wait_ge(S("zb"), 3)
            dve.wait_ge(S("ld_h"), 48)
            dve.wait_ge(S("ld_c"), 80)
            norm("n0", [0, 1, 2], 0)
            dve.wait_ge(S("w_used"), U0["pool"] + 2)
            for t in range(3):
                P = TILES[t][1]
                v.tensor_tensor(hT(t), ps2(2 * t, P), bcP[0:P, :], ALU.mult).then_inc(S("mix0_ps"), 1)
                dve.wait_ge(S("mix0_ps"), t + 1)
                v.tensor_tensor(hh(t), hh(t), hT(t), ALU.add).then_inc(S("mix0_h"), 1)

            def topk(l, t, tick=lambda n: None):
                H = 1 if t == 2 else PEER_H
                scores_ = s_m if t == 2 else s_sb0[t] if l == 0 else s_sb1
                oh = oh0 if l == 0 else oh1
                steps = [0]

                def step(n=1):
                    steps[0] += n
                    tick(steps[0])

                s_ = scores_.rearrange("p (j n) -> p j n", n=128)
                tv_ = tv[:, 0:32 * H].rearrange("p (j a) -> p j a", a=16)
                ti_ = ti[:, 0:32 * H].rearrange("p (j a) -> p j a", a=16)
                tif_ = tif[:, 0:32 * H].rearrange("p (j a) -> p j a", a=16)
                J = 2 * H

                def top16(n, val, idx, src, W_):
                    for j in range(n):
                        i = v.max(val[:, j, 0:8], src[:, j, :])
                        if j < n - 1:
                            step(W_)
                    link(i)
                    step(W_)
                    for j in range(n):
                        i = v.max_index(idx[:, j, 0:8], val[:, j, 0:8], src[:, j, :])
                        if j < n - 1:
                            step(W_)
                    link(i)
                    step(W_)
                    for j in range(n):
                        i = v.match_replace(src[:, j, :], val[:, j, 0:8], src[:, j, :], -3.0e38)
                        if j < n - 1:
                            step(W_)
                    link(i)
                    step(W_)
                    for j in range(n):
                        i = v.max(val[:, j, 8:16], src[:, j, :])
                        if j < n - 1:
                            step(W_)
                    link(i)
                    step(W_)
                    for j in range(n):
                        i = v.max_index(idx[:, j, 8:16], val[:, j, 8:16], src[:, j, :])
                        if j < n - 1:
                            step(W_)
                    link(i)
                    step(W_)

                top16(J, tv_, ti_, s_, 1)
                cand = (oh if t == 2 else scores_)[:, 0:256 * H]
                tv4 = tv_.rearrange("p (h s) a -> p h s a", s=2)
                link(v.tensor_tensor(cand.rearrange("p (h a b) -> p h a b", a=16, b=16),
                                     tv4[:, :, 0, :].unsqueeze(3).to_broadcast([128, H, 16, 16]),
                                     tv4[:, :, 1, :].unsqueeze(2).to_broadcast([128, H, 16, 16]), ALU.add))
                bv_ = bv[:, 0:16 * H].rearrange("p (h k) -> p h k", k=16)
                bp_ = bp[:, 0:16 * H].rearrange("p (h k) -> p h k", k=16)
                step(10)
                top16(H, bv_, bp_, cand.rearrange("p (h n) -> p h n", n=256), 2)
                G = gates[t][:, 0:16 * H]
                G3 = G.rearrange("p (h k) -> p h k", k=16)
                q = tk_number(l, t)
                v.tensor_tensor(G3, bv_, bv_[:, :, 0:1].to_broadcast([128, H, 16]), ALU.subtract)\
                    .then_inc(S("gx"), 1)
                n = 16 * H
                v.tensor_copy(tif[:, 0:32 * H], ti[:, 0:32 * H])
                v.tensor_scalar(pab[:, 0, 0:n], bp[:, 0:n], 4, None, ALU.logical_shift_right)
                link(v.tensor_scalar(pab[:, 1, 0:n], bp[:, 0:n], 15, None, ALU.bitwise_and))
                v.tensor_copy(sel_a[:, 0:n], pab[:, 0, 0:n])
                link(v.tensor_copy(sel_b[:, 0:n], pab[:, 1, 0:n]))
                o_ = oh[:, 0:16 * n].rearrange("p (m a) -> p m a", a=16)
                o4 = oh[:, 0:16 * n].rearrange("p (h k a) -> p h k a", k=16, a=16)
                tif4 = tif_.rearrange("p (h s) a -> p h s a", s=2)
                for half, (pos, res) in enumerate([(sel_a, ia), (sel_b, ib)]):
                    step(10)
                    link(v.tensor_tensor(o_, pos[:, 0:n].unsqueeze(2).to_broadcast([128, n, 16]),
                                         cc("iota", 16).unsqueeze(1).to_broadcast([128, n, 16]), ALU.is_equal))
                    step(10)
                    link(v.tensor_tensor(o4, o4, tif4[:, :, half, :].unsqueeze(2).to_broadcast([128, H, 16, 16]),
                                         ALU.mult))
                    step(10)
                    link(v.tensor_reduce(res[:, 0:n], o_, AX, ALU.add))
                link(v.tensor_scalar(ia[:, 0:n], ia[:, 0:n], 128.0, float(l * EXPERTS), ALU.mult, ALU.add))
                v.tensor_tensor(eidx[:, t, 0:n], ia[:, 0:n], ib[:, 0:n], ALU.add).then_inc(S("eidx"), 1)
                dve.wait_ge(S("ge"), q)
                link(v.tensor_reduce(gm[:, 0:H], G3, AX, ALU.add))
                link(v.reciprocal(gs[:, 0:H], gm[:, 0:H]))
                link(v.tensor_tensor(G3, G3, gs[:, 0:H].unsqueeze(2).to_broadcast([128, H, 16]), ALU.mult))

            def dot(t, k, n, ufill):
                dve.wait_ge(S(f"u{k % NU}"), ufill)
                v.scalar_tensor_tensor(ug[:, k % NU, :], ug[:, k % NU, :], 1.0, hnm if t == 2 else hn[:, t, :],
                                       ALU.mult, ALU.mult, accum_out=dots[:, k % 8:k % 8 + 1]).then_inc(S("dot"), 1)

            def coef(t, k, n, gate):
                unit_mat, W = (cc("sel", 16), 16) if t == 2 else (ident, 128)
                dve.wait_ge(S("gelu"), n + 1)
                if not isinstance(n, int) or n >= 4:
                    dve.wait_ge(S("vsum"), n - 3)
                v.tensor_scalar(diag[:, k % 4, 0:W], unit_mat, gel[:, k % 8:k % 8 + 1], gate,
                                ALU.mult, ALU.mult).then_inc(S("diag"), 1)

            def straight(t, base):
                def slot(k):
                    if k < SLOTS:
                        dot(t, k, base + k, 16 * ((base + k) // NU + 1))
                    if k >= 2:
                        coef(t, k - 2, base + k - 2, gates[t][:, k - 2:k - 1])
                return slot

            def flush(t, base, n):
                for k in (n - 2, n - 1):
                    coef(t, k, base + k, gates[t][:, k:k + 1])

            def slots_loop(t, base, start=0):
                with dve.Fori(start // GB, SLOTS // GB) as i:
                    for k in range(GB):
                        dot(t, k, GB * i + (base + k), 16 * (GB // NU) * i + 16 * ((base + k) // NU + 1))
                        if k >= 2:
                            coef(t, k - 2, GB * i + (base + k - 2), gates[t][:, ds(GB * i + (k - 2), 1)])
                    for k in (GB - 2, GB - 1):
                        coef(t, k, GB * i + (base + k), gates[t][:, ds(GB * i + k, 1)])

            norm("f0", [0, 1, 2], 3, gain=bcF[:, :])
            dve.wait_ge(S("md"), 128)
            topk(0, 2)
            (_, m_base), (_, a_base), (_, b_base) = gathers(0)
            dve.wait_ge(S("md2"), 128)
            dve.wait_ge(S("sc0_ev"), 2)
            bg = Beside(straight(2, m_base))
            topk(0, 0, lambda n: bg.to(min(16, 16 * n / GATE_AT)))
            flush(2, m_base, 16)
            dve.wait_ge(S("sc0_ev"), 3)
            bg = Beside(straight(0, a_base))
            topk(0, 1, lambda n: bg.to(min(GB, 20 * n / GATE_AT)))
            bg.to(GB)
            flush(0, a_base, GB)
            slots_loop(0, a_base, GB)

            def heads_norm(tag, tiles):
                for m, t in enumerate(tiles):
                    P = TILES[t][1]
                    link(v.tensor_tensor(sq[0:P, :], hT(t), hT(t), ALU.mult))
                    link(v.tensor_reduce(hsum[0:P, 16 * m:16 * m + 16], sq[0:P, :].rearrange("p (h e) -> p h e", e=64),
                                         AX, ALU.add))
                n = 16 * len(tiles)
                rstd(tag, hsum[:, 0:n], hsum[:, 0:n], 0, 64)
                for m, t in enumerate(tiles):
                    P = TILES[t][1]
                    x3 = hT(t).rearrange("p (h e) -> p h e", e=64)
                    v.tensor_tensor(x3, x3, hsum[0:P, 16 * m:16 * m + 16].unsqueeze(2).to_broadcast([P, 16, 64]),
                                    ALU.mult).then_inc(S("x_ready"), 1)

            def front(i, bg):
                X = "AB"[i]
                kvt = [0, 2] if i == 0 else [1]
                plan = PLAN[i]

                def at(stage, j=0, J=1):
                    a = plan[stage]
                    bg.to(a + (plan[STAGES[STAGES.index(stage) + 1]] - a) * j / J)

                if i == 0:
                    v.memset(kT[:, :, LTOK:384], 0.0)
                    v.memset(vk[:, 2, :], 0.0).then_inc(S("kv_zero"), 1)
                at("kv")
                norm("kv" + X, kvt, (6, 8)[i])
                t_out("kv" + X, kvt, "kvn", free=U0["wq"] + 16 if i == 0 else U0["wqA"] + 16, tb=4)
                at("v")
                dve.wait_ge(S("k_ev"), 2 + i)
                heads_norm("kh" + X, kvt)
                at("n1")
                dve.wait_ge(S("turned"), AT["kh" + X][3] + len(kvt))
                norm("n1" + X, [i], 9 + i)
                t_out("n1" + X, [i], "mix1", free=U0["v" + X] + 8, tb=4)
                at("qh")
                dve.wait_ge(S("q_ev"), i + 1)
                heads_norm("qh" + X, [i])
                stick(i, lambda p: at("stick", p, 8))
                at("f1")
                dve.wait_ge(S("w_used"), U0["o" + X] + 8)
                v.tensor_tensor(hh(i), hh(i), ps2(0), ALU.add).then_inc(S("wo_h"), 1)
                dve.wait_ge(S("ld_f1"), 16)
                norm("f1" + X, [i], 11 + i, gain=bcF[:, :])
                at("topk")
                dve.wait_ge(S("sc1_ev"), i + 1)
                topk(1, i, lambda n: at("topk", n, TOPK_STEPS))
                bg.to(SLOTS)

            def stick(i, tick):
                nk = 2 + i
                W = nk * 128
                valid = cc("valid", 384)[:, 384 - W:384].unsqueeze(1).to_broadcast([128, 2, W])

                def logits(p):
                    n = 8 * i + p
                    z_, t_ = st[:, p % 2, 0, 0:2 * W], st[:, p % 2, 1, 0:2 * W]
                    dve.wait_ge(S("z_pe"), n + 1)
                    if n >= 2:
                        dve.wait_ge(S("o_pe"), n - 1)
                    v.scalar_tensor_tensor(z_.rearrange("p (r w) -> p r w", r=2), ps[:, 0:2, 0:W], 0.125, valid,
                                           ALU.mult, ALU.add).then_inc(S("z_sb"), 1)
                    dve.wait_ge(S("z_sb"), n + 1)
                    v.scalar_tensor_tensor(t_, z_, -1.0, z_, ALU.mult, ALU.min).then_inc(S("tmin"), 1)

                logits(0)
                for p in range(8):
                    n = 8 * i + p
                    tick(p)
                    z_, t_ = st[:, p % 2, 0, 0:2 * W], st[:, p % 2, 1, 0:2 * W]
                    dve.wait_ge(S("ln"), n + 1)
                    v.scalar_tensor_tensor(t_, z_, 0.0, t_, ALU.max, ALU.add).then_inc(S("sp"), 1)
                    if p < 7:
                        logits(p + 1)
                    dve.wait_ge(S("c_pe"), n + 1)
                    v.tensor_tensor(z_.rearrange("p (r k n) -> p r k n", r=2, k=nk),
                                    z_.rearrange("p (r k n) -> p r k n", r=2, k=nk),
                                    ps2(2)[:, 0:2 * W].rearrange("p (k r n) -> p r k n", r=2, k=nk), ALU.subtract)\
                        .then_inc(S("dd"), 1)

            front(0, Beside(straight(1, b_base)))
            flush(1, b_base, SLOTS)
            (_, a_base), (_, b_base) = gathers(1)
            front(1, Beside(straight(0, a_base)))
            flush(0, a_base, SLOTS)
            slots_loop(1, b_base)

            dve.wait_ge(S("ld_m"), 80)
            dve.wait_ge(S("vsum"), 16 + 4 * SLOTS)
            norm("nm", [0, 1], 15, src=lambda t: mrg[:, t, :])
            t_out("nm", [0, 1], "gmem", free=U0["wqB"] + 16)
            dve.wait_ge(S("trev_pe"), 1)
            v.tensor_tensor(pw[0:8, 0, 0:384], ps[0:8, 6, 0:384], cs2c[0:8, CS2["future"]:CS2["future"] + 384],
                            ALU.add).then_inc(S("trev_sb"), 1)
            norm("n2", [0, 1], 13)
            t_out("n2", [0, 1], "gmix", free=U0["mem_v"] + 4)
            for t in range(2):
                dve.wait_ge(S("sg"), t + 1)
                v.tensor_tensor(vtok[:, 2, t, :], ps[:, 4 + t, :], vtok[:, 2, t, :], ALU.mult).then_inc(S("iv_ev"), 1)

            def c2(name, a=0, n=256):
                return cs2c[:, CS2[name] + a:CS2[name] + a + n]

            for j in range(8):
                x_ = qkT[:, 8 + j, :]
                k_ = "q" if j < 4 else "k"
                tmp = oh2[:, (j % 2) * 256:(j % 2) * 256 + 256]
                dve.wait_ge(S("sw_pe"), j + 1)
                v.tensor_tensor(tmp, ps[:, j % 2, 0:256], c2("sin" + k_), ALU.mult).then_inc(S("rot_ps"), 1)
                link(v.tensor_tensor(x_, x_, c2("cos" + k_), ALU.mult))
                v.tensor_tensor(x_, x_, tmp, ALU.add).then_inc(S("rot"), 1)
            for hd in range(4):
                dve.wait_ge(S("rs_pe"), hd + 1)
                v.tensor_tensor(mrg[:, hd // 2, (hd % 2) * 384:(hd % 2) * 384 + 384], ps[:, 2 + hd % 2, 0:384],
                                c2("decay", 384 * hd, 384), ALU.mult).then_inc(S("rs_sb"), 1)
            dve.wait_ge(S("ry_pe"), 4)
            y3 = hn[:, 0, :].rearrange("p (g e) -> p g e", e=128)
            q3 = hn[:, 1, :].rearrange("p (g e) -> p g e", e=128)
            mu = tsb[:, 8:16]
            var = tsb[:, 16:24]
            link(v.tensor_copy(hn[:, 0, :], ps2(6)))
            v.tensor_reduce(mu, y3, AX, ALU.add).then_inc(S("ry_ps"), 1)
            dve.wait_ge(S("ry_ps"), 1)
            link(v.tensor_scalar(mu, mu, -1.0 / 128, None, ALU.mult))
            link(v.tensor_tensor(y3, y3, mu.unsqueeze(2).to_broadcast([128, 8, 128]), ALU.add))
            link(v.tensor_tensor(q3, y3, y3, ALU.mult))
            link(v.tensor_reduce(var, q3, AX, ALU.add))
            rstd("ry", var, var, 0, 128)
            link(v.tensor_tensor(y3, y3, var.unsqueeze(2).to_broadcast([128, 8, 128]), ALU.mult))
            y4 = hn[:, 0, :].rearrange("p (t d) -> p t d", t=2)
            link(v.tensor_tensor(y4, y4, bcG[:, :].unsqueeze(1).to_broadcast([128, 2, 512]), ALU.mult))
            for t in range(2):
                v.tensor_tensor(y4[:, t, :], y4[:, t, :], vtok[:, 2, t, :], ALU.mult).then_inc(S("x_ready"), 1)

            dve.wait_ge(S("bias"), 1)

            def soft_l(n):
                p_ = pw[:, n % 2, :]
                col = 8 * (n % 2)
                dve.wait_ge(S("ss_pe"), n + 1)
                if n >= 2:
                    dve.wait_ge(S("pt_pe"), n - 1)
                if n < 8:
                    v.scalar_tensor_tensor(p_[:, 0:128], ps[:, n % 2, 0:128], 0.125, biasT[:, n, 128:256],
                                           ALU.mult, ALU.add)
                    v.scalar_tensor_tensor(p_[:, 128:384], ps[:, n % 2, 128:384], 0.125, biasT[:, n, :],
                                           ALU.mult, ALU.add).then_inc(S("ss_ps"), 1)
                    dve.wait_ge(S("ss_ps"), n + 1)
                    v.tensor_reduce(nmx[:, col:col + 1], p_[:, 0:128], AX, ALU.max, negate=True)
                    v.tensor_reduce(nmx[:, col + 1:col + 2], p_[:, 128:384], AX, ALU.max, negate=True)\
                        .then_inc(S("nmx"), 1)
                else:
                    link(v.tensor_reduce(nmx[:, col:col + 2], ps[:, n % 2, :].rearrange("p (t m) -> p t m", t=2),
                                         AX, ALU.max, negate=True))
                    v.tensor_scalar(nmx[:, col:col + 2], nmx[:, col:col + 2], RET_DK ** -0.5, None, ALU.mult)\
                        .then_inc(S("nmx"), 1)

            def soft_n(n):
                p_ = pw[:, n % 2, :]
                col = 8 * (n % 2)
                dve.wait_ge(S("pe_"), 2 * n + 2)
                i = v.reciprocal(nmx[:, col + 4:col + 6], nmx[:, col + 2:col + 4])
                if n >= 8:
                    i.then_inc(S("ss_ps"), 1)
                    dve.wait_ge(S("ss_ps"), n + 1)
                else:
                    link(i)
                for t, (a, b) in enumerate([(0, 128), (128, 384)] if n < 8 else [(0, 256), (256, 512)]):
                    i = v.tensor_scalar(p_[:, a:b], p_[:, a:b], nmx[:, col + 4 + t:col + 5 + t], None, ALU.mult)
                i.then_inc(S("pn"), 1)

            soft_l(0)
            for n in range(12):
                if n < 11:
                    soft_l(n + 1)
                soft_n(n)
            for k in range(3):
                dve.wait_ge(S("w_used"), U0["br"] + 4 * k + 4)
                dve.wait_ge(S(f"z{k}_ev"), 2)
                for t in range(2):
                    P2 = ps2(4 * (k % 2) + 2 * t)
                    if k == 0:
                        v.tensor_tensor(mrg[:, t, :], P2, zs[:, k, t, :], ALU.mult).then_inc(S("br0_ps"), 1)
                    else:
                        v.tensor_tensor(zs[:, k, t, :], P2, zs[:, k, t, :], ALU.mult).then_inc(S(f"br{k}_ps"), 1)
                        dve.wait_ge(S(f"br{k}_ps"), t + 1)
                        i = v.tensor_tensor(mrg[:, t, :], mrg[:, t, :], zs[:, k, t, :], ALU.add)
                        if k == 2:
                            i.then_inc(S("x_ready"), 1)
                        else:
                            link(i)
                if k == 0:
                    dve.wait_ge(S("br0_ps"), 2)
            add_h(U0["out"] + 8, "out_h", [0, 1])
            norm("n3", [0, 1], 17)
            t_out("n3", [0, 1], "gffn")
            v.memset(up_in[:, :, :, 0:2], 0.0).then_inc(S("padded"), 1)
            for j in range(FFC):
                for k in range(2):
                    x_ = up_in[:, j % 2, k, :]
                    y_ = up_cv[:, j % 2, k, :]
                    m = k * FFC + j
                    w_ = [colc[:, COL["convw"] + 44 * i + m:COL["convw"] + 44 * i + m + 1] for i in range(3)]
                    dve.wait_ge(S("up_ev"), 2 * j + k + 1)
                    link(v.tensor_scalar(y_, x_[:, 0:256], w_[0], gcol("convb", m), ALU.mult, ALU.add))
                    link(v.scalar_tensor_tensor(y_, x_[:, 1:257], w_[1], y_, ALU.mult, ALU.add))
                    v.scalar_tensor_tensor(y_, x_[:, 2:258], w_[2], y_, ALU.mult, ALU.add).then_inc(S("cv"), 1)
                dve.wait_ge(S("gate"), j + 1)
                dve.wait_ge(S("cv"), 2 * j + 2)
                v.tensor_tensor(aT[:, j, :], up_cv[:, j % 2, 0, :], up_cv[:, j % 2, 1, :], ALU.mult)\
                    .then_inc(S("a_T"), 1)
            add_h(U0["down"] + 22, "down_h", [0, 1])
            rstd("n4", ss[:, 19:21], rs[:, 19:21], 2, D)
            dve.wait_ge(S("ld_g"), 16)
            for t in range(2):
                v.scalar_tensor_tensor(hn[:, t, :], h[:, t, :], rs[:, 19 + t:20 + t], bcL, ALU.mult, ALU.mult)\
                    .then_inc(S("fin"), 1)


def _t(w):
    J = w.shape[1] // 128
    return w.reshape(8, 128, J, 128).transpose(2, 1, 0, 3).reshape(J, 128, 1024)


def _n(w):
    return w.reshape(-1, 128, 1024)


def _n2(w):
    return w.reshape(4, 2, 128, 512).transpose(0, 2, 1, 3).reshape(4, 128, 1024)


def _pack_units(a):
    w_in, w_up = a["w_in_2"][0], a["w_up_2"][0]
    o = [0, 512, 1024, 1536, 2048, 2560, 3072, 3584, 4096, 5120, 6144, 7168]
    qa, ka, va, qr, kr, vr, gr, qm, za, zr, zm = [w_in[:, o[i]:o[i + 1]] for i in range(11)]
    up = np.stack([_t(w_up[:, :DFF]), _t(w_up[:, DFF:])], axis=1).reshape(-1, 128, 1024)
    keys = [a["peer_keys"][l].reshape(2, 8, 128, 128).transpose(0, 3, 1, 2).reshape(2, 128, 1024) for l in range(2)]
    kv, wq = a["w_kv"], a["peer_wq"]
    front = [_n(kv[:, :D]), _n(kv[:, D:]), _n(a["w_q"][0]), _n(a["w_o"][0]), _t(wq[1]), keys[1]]
    parts = [
        a["pool_w"][0].reshape(2, 2, 2, 128, 256).transpose(0, 3, 1, 2, 4).reshape(2, 128, 1024),
        _t(wq[0]), keys[0], *front, *front,
        _t(a["w_mem_kv_2"][0][:, :512]), _n2(a["w_mem_kv_2"][0][:, 512:]),
        _t(qa), _t(ka), _t(qr), _t(kr), _t(qm), _n2(va), _n2(vr), _n2(gr), _n(za), _n(zr), _n(zm),
        _n(a["w_br_attn_2"][0]), _n(a["w_br_ret_2"][0]), _n(a["w_br_mem_2"][0]), _n(a["w_out_2"][0]), up,
        _n(a["w_down_2"][0])]
    return np.ascontiguousarray(np.concatenate(parts, axis=0))


def _cols(v):
    return v.reshape(-1, 128).T


def _pack_cols(a):
    two = lambda g: np.concatenate([g, g]).reshape(128, 1)
    cw = a["conv_w_2"][0]
    return np.ascontiguousarray(np.concatenate(
        [_cols(a["norm_mix"][0]), _cols(a["norm_mix"][1]), _cols(a["kv_norm"]), _cols(a["g_mix_2"][0]),
         _cols(a["g_mem_2"][0]), _cols(a["g_ffn_2"][0]), two(a["k_norm"]), two(a["q_norm"][0]),
         _cols(a["conv_b_2"][0]), _cols(cw[0]), _cols(cw[1]), _cols(cw[2])], axis=1))


def _constants():
    f = np.float32
    i = np.arange(128)
    valid = np.zeros((128, 384), f)
    future = np.where(i[:, None] < i[None, :], 0.0, NEG)
    valid[:, 128:256] = future
    valid[META:, 256:384] = NEG
    c1 = [np.eye(128), (i[:, None] >= i[None, :]), np.ones((128, 128)), np.tile(np.arange(16), (128, 1)),
          (i[:, None] % META == np.arange(META)[None, :]), valid]
    cst = np.concatenate([np.asarray(x, f) for x in c1], axis=1)

    half = RET_DK // 2
    swap = np.roll(np.eye(128), half, axis=1)
    inv = f(10000.0) ** (-np.arange(half, dtype=f) / f(half))
    ang = (np.arange(SEQ, dtype=f)[None, :] * inv[:, None]).astype(f)
    cos = np.concatenate([np.cos(ang), np.cos(ang)]).astype(f)
    sin = np.concatenate([-np.sin(ang), np.sin(ang)]).astype(f)
    scale = f(RET_DK ** -0.5)
    decay = np.zeros((128, 4, 384))
    for hd in range(4):
        lg = np.log1p(-2.0 ** (-5.0 - hd))
        for a, (j0, i0, n) in {0: (0, 0, 256), 256: (128, 128, 128)}.items():
            diff = (i0 + np.arange(n))[None, :] - (j0 + i)[:, None]
            decay[:, hd, a:a + n] = np.where(diff >= 0, np.exp(lg * np.maximum(diff, 0)), 0.0)
    dist = 255 - np.arange(384)
    d = np.maximum(dist, 1).astype(f)
    large = 16 + (np.log(d / f(16)) / f(np.log(2048 / 16)) * f(16)).astype(np.int32)
    bucket = np.where(dist < 16, np.maximum(dist, 0), np.minimum(large, 31))
    hot = np.zeros((128, 384))
    hot[bucket, np.arange(384)] = 1.0
    fut = np.zeros((128, 384))
    fut[:, dist < 0] = NEG
    cs2 = np.concatenate([np.asarray(x, f) for x in
                          [swap, np.eye(128)[::-1], cos, sin, cos * scale, sin * scale, decay.reshape(128, -1), hot, fut]], axis=1)

    order = np.concatenate([np.arange(META, LTOK), np.arange(META)])
    pool = np.zeros((4, LTOK, LTOK))
    for g, w in enumerate((2, 4, 8, 16)):
        for t in range(LTOK):
            lo = max(0, t - w + 1)
            pool[g, lo:t + 1, t] = 1.0 / min(t + 1, w)
            pool[g, t, t] -= 1.0
    pool = pool[:, order][:, :, order]
    poolm = np.zeros((128, 4, 3, LTOK), f)
    for s, (c0, P) in enumerate(TILES):
        poolm[0:P, :, s, :] = pool[:, c0:c0 + P, :].transpose(1, 0, 2)
    return cst, cs2, poolm.reshape(128, -1)


def kernel(**inputs):
    import concourse.bacc as bacc
    from concourse.bass_utils import run_bass_kernel_spmd

    a = {k: np.asarray(v) for k, v in inputs.items()}
    cst, cs2, poolm = _constants()
    bc = np.zeros((5, D), np.float32)
    bc[0], bc[1], bc[2] = a["norm_ffn"][0], a["norm_ffn"][1], a["pool_scale"][0]
    bc[3, 0:512], bc[4] = a["ret_gn_gain_2"][0], a["g_final_2"]
    arrays = {
        "xin": a["x"][0], "metain": a["meta_tokens"], "units": _pack_units(a), "cols": _pack_cols(a),
        "cst": cst, "cs2": cs2, "poolm": poolm, "bc_rows": bc,
        "peer_u": a["peer_u"].reshape(2 * EXPERTS, D), "peer_v": a["peer_v"].reshape(2 * EXPERTS, D),
        "mem": a["mem_2"][0], "rel": a["rel_bias_2"]}
    arrays = {k: np.ascontiguousarray(v) for k, v in arrays.items()}
    nc = bacc.Bacc("TRN2", target_bir_lowering=False, num_devices=1)
    args = [nc.dram_tensor("in_" + k, v.shape, mybir.dt.from_np(v.dtype), kind="ExternalInput").ap()
            for k, v in arrays.items()]
    args.append(nc.dram_tensor("result", (SEQ, D), mybir.dt.float32, kind="ExternalOutput").ap())
    program(nc, *args)
    r = run_bass_kernel_spmd(nc, [{"in_" + k: v for k, v in arrays.items()}], core_ids=[0])
    return r.results[0]["result"].reshape(1, SEQ, D)
```

```python
from contextlib import ExitStack

import numpy as np

import concourse.bass as bass
from concourse import mybir

D = 1024
SEQ = 256
META = 16
LTOK = SEQ + META
DC = D // 128
EPS = 1e-6
NEG = -1e30
EXPERTS = 128 * 128
PEER_H = 8
TOPK = 16
DFF = 2816
FFC = DFF // 128
RET_DK = 128

R = 8
NU = 4
NV = 8
GB = 32
SLOTS = PEER_H * TOPK

TILES = [(0, 128), (128, 128), (256, META)]

UNITS = [("pool", 2), ("wq", 16), ("keys", 2),
         ("kA", 8), ("vA", 8), ("qA", 8), ("oA", 8), ("wqA", 16), ("keysA", 2),
         ("kB", 8), ("vB", 8), ("qB", 8), ("oB", 8), ("wqB", 16), ("keysB", 2),
         ("in_T", 20), ("in_v", 12), ("mem_k", 4), ("mem_v", 4), ("in_z", 24),
         ("br", 12), ("out", 8), ("up", 44), ("down", 22)]
N_UNITS = sum(n for _, n in UNITS)

STAGES = ["kv", "k", "v", "kh", "n1", "q", "qh", "stick", "o", "f1", "wq", "sc", "topk", "end"]
PLAN = [dict(zip(STAGES, (6, 7, 17, 29, 32, 36, 43, 47, 75, 82, 86, 98, 100, 126))),
        dict(zip(STAGES, (6, 7, 13, 18, 21, 25, 32, 36, 72, 79, 83, 95, 97, 126)))]
TOPK_STEPS = 5 * 16 + 10 + 2 * 5 * 8 + 60
GATE_AT = 5 * 16 + 10 + 2 * 5 * 8
HALF_GATE_AT = 5 * 8 + 10 + 2 * 5 * 4
TOPK_A, TOPK_B, STRAIGHT = 26, 74, 96
LAG = 2

COL = {}
_at = 0
for _name, _n in [("mix0", 8), ("mix1", 8), ("kvn", 8), ("gmix", 8), ("gmem", 8), ("gffn", 8),
                  ("knorm", 1), ("qnorm", 1), ("convb", 44), ("convw", 132)]:
    COL[_name] = _at
    _at += _n
NCOL = _at

CST = {}
_at = 0
for _name, _n in [("ident", 128), ("tri", 128), ("ones", 128), ("iota", 16), ("sel", 16), ("valid", 384)]:
    CST[_name] = _at
    _at += _n
NCST = _at
CS2 = {}
_at = 0
for _name, _n in [("swap", 128), ("flip", 128), ("cosq", 256), ("sinq", 256), ("cosk", 256), ("sink", 256),
                  ("decay", 4 * 384), ("bucket", 384), ("future", 384)]:
    CS2[_name] = _at
    _at += _n
NCS2 = _at


def program(nc, xin, metain, units, cols, cst, cs2, poolm, bc_rows, peer_u, peer_v, mem, rel, out):
    fp32 = mybir.dt.float32
    bf16 = mybir.dt.bfloat16
    u32 = mybir.dt.uint32
    fp32r = mybir.dt.float32r
    ALU = mybir.AluOpType
    ACT = mybir.ActivationFunctionType
    AX = mybir.AxisListType.X
    ds = bass.ds

    ctx = ExitStack()
    with ctx:
        def sb(name, shape, dt=fp32):
            return ctx.enter_context(nc.sbuf_tensor(name, shape, dt))

        sems = {}

        def S(name):
            if name not in sems:
                sems[name] = ctx.enter_context(nc.semaphore(name))
            return sems[name]

        h = sb("h", [128, 3, D])
        hn = sb("hn", [128, 3, D])
        xT = sb("xT", [128, DC, LTOK])
        wring = sb("wring", [128, R, 1024])
        colc = sb("colc", [128, NCOL])
        cstc = sb("cstc", [128, NCST])
        ss = sb("ss", [128, 32])
        rs = sb("rs", [128, 32])
        zb = sb("zb", [128, 512], bf16)
        bcF = sb("bcF", [128, D])
        hsum = sb("hsum", [128, 48])
        nmx = sb("nmx", [128, 16])

        def cc(name, n, p=128):
            return cstc[0:p, CST[name]:CST[name] + n]

        ident = cc("ident", 128)

        def gcol(name, i=0):
            return colc[:, COL[name] + i:COL[name] + i + 1]

        def gains(name, n):
            return colc[:, COL[name]:COL[name] + DC].unsqueeze(2).to_broadcast([128, DC, n])

        with ExitStack() as shared:
            f1 = shared.enter_context(nc.sbuf_tensor("parts1", [128, 8192], fp32r))
            shared.enter_context(nc.sbuf_tensor("parts_gap", [128, (NU + NV) * 1024 - 8192], fp32r))
            f2 = shared.enter_context(nc.sbuf_tensor("parts2", [128, 13312], fp32r))

        A1W = (NU + NV) * 1024
        a1 = sb("a1", [128, A1W])
        ug = a1[:, 0:NU * 1024].rearrange("p (n d) -> p n d", d=1024)
        vg = a1[:, NU * 1024:A1W].rearrange("p (n d) -> p n d", d=1024)
        A2W = 13840
        a2 = sb("a2", [128, A2W])
        free2 = [0]

        def take2(n, at=None):
            if at is None:
                at = free2[0]
                free2[0] += n
            assert at + n <= A2W, (at, n)
            return a2[:, at:at + n]

        tv = take2(256)
        tif = take2(256)
        bv = take2(128)
        sel_a = take2(128)
        sel_b = take2(128)
        ia = take2(128)
        ib = take2(128)
        gates = [take2(128) for _ in range(3)]
        gm = take2(8)
        gs = take2(8)
        SMALL = free2[0]
        s_m = take2(256)
        hnm = take2(1024)
        qT0 = take2(16 * LTOK).rearrange("p (j t) -> p j t", t=LTOK)
        s_sb0 = [take2(2048), take2(2048)]
        oh0 = take2(2048)
        ti = sb("ti", [128, 256], u32)
        bp = sb("bp", [128, 128], u32)
        pab = sb("pab", [128, 2, 128], u32)
        eidx = sb("eidx", [128, 3, 128], u32)
        ixc = sb("ixc", [128, 2, 16], u32)
        dots = sb("dots", [128, 8])
        gel = sb("gel", [128, 8])
        diag = sb("diag", [128, 4, 128])

        poolP = a1[:, 0:4 * 3 * LTOK].rearrange("p (g s t) -> p g s t", g=4, s=3)
        bcP = a1[:, 4096:5120]
        free2[0] = SMALL
        kT = take2(DC * 384).rearrange("p (c t) -> p c t", t=384)
        vk = take2(3 * D).rearrange("p (s d) -> p s d", d=D)
        LATE = free2[0]
        qT1 = take2(16 * 128).rearrange("p (j t) -> p j t", t=128)
        s_sb1 = take2(2048)
        oh1 = take2(2048)
        free2[0] = LATE
        qhT = take2(DC * 128).rearrange("p (c t) -> p c t", t=128)
        oT = take2(DC * 128).rearrange("p (c t) -> p c t", t=128)
        st = take2(2 * 2 * 768).rearrange("p (b k n) -> p b k n", b=2, k=2)
        sq = take2(D)
        free2[0] = 0
        qkT = take2(20 * SEQ).rearrange("p (j t) -> p j t", t=SEQ)
        vtok = take2(3 * 1024).rearrange("p (k t d) -> p k t d", k=3, t=2)
        biasT = take2(8 * 256).rearrange("p (h y) -> p h y", y=256)
        yT = take2(3 * 1024)
        memT = yT[:, 0:2048].rearrange("p (c t) -> p c t", t=SEQ)
        yT = yT.rearrange("p (k c t) -> p k c t", k=3, c=4)
        zs = a1[:, 0:3 * 2048].rearrange("p (k t d) -> p k t d", k=3, t=2)
        kmT = a1[:, 6144:7168].rearrange("p (j t) -> p j t", t=SEQ)
        vmem = a1[:, 7168:8192].rearrange("p (t d) -> p t d", t=2)
        pw = a1[:, 8192:8192 + 2048].rearrange("p (b n) -> p b n", b=2)
        mrg = a1[:, 10240:12288].rearrange("p (t d) -> p t d", t=2)
        cs2c = sb("cs2c", [128, NCS2])
        bcG = sb("bcG", [128, 512])
        tsb = sb("tsb", [128, 32])
        aT = a1[:, 11520:11520 + 2 * SEQ].rearrange("p (j t) -> p j t", t=SEQ)
        up_in = a1[:, 9216:9216 + 2 * 2 * 258].rearrange("p (b k t) -> p b k t", b=2, k=2)
        up_cv = a1[:, 10248:10248 + 2 * 2 * 256].rearrange("p (b k t) -> p b k t", b=2, k=2)
        bcL = a1[:, 8192:9216]
        oh2 = sb("rot_tmp", [128, 512])
        WH = 3
        xH, xL = [f1[:, o:o + 2048].rearrange("p (c t) -> p c t", t=SEQ) for o in (0, 2048)]
        w_part = [f1[:, 4096 + i * 1024:5120 + i * 1024] for i in range(4)]
        w_part += [f2[:, 11264:12288], f2[:, 12288:13312]]
        aH, aL = [f2[:, o:o + FFC * SEQ].rearrange("p (j t) -> p j t", t=SEQ) for o in (0, FFC * SEQ)]

        ps = ctx.enter_context(nc.psum_tensor("ps", [128, 8, 512], fp32))
        trev_d = nc.dram_tensor("trev_scratch", [8, 384], fp32, kind="Internal").ap()

        def ps2(b, p=128):
            return ps[0:p, b:b + 2, :].rearrange("p a n -> p (a n)")

        U0, n_ = {}, 0
        for name, n in UNITS:
            U0[name] = n_
            n_ += n

        AT, n_ = {}, [0, 0, 0, 0]
        for tag, *k in [("n0", 3, 1, 3, 0), ("f0", 3, 1, 3, 3),
                        ("kvA", 2, 1, 2, 2), ("khA", 0, 1, 2, 2), ("n1A", 1, 1, 1, 1), ("qhA", 0, 1, 1, 1),
                        ("f1A", 1, 1, 1, 1),
                        ("kvB", 1, 1, 1, 1), ("khB", 0, 1, 1, 1), ("n1B", 1, 1, 1, 1), ("qhB", 0, 1, 1, 1),
                        ("f1B", 1, 1, 1, 1), ("n2", 2, 1, 2, 2), ("nm", 2, 1, 2, 2), ("ry", 0, 1, 0, 0), ("yr", 0, 0, 2, 2), ("mg", 0, 0, 2, 2),
                        ("n3", 2, 1, 2, 2), ("n4", 2, 1, 0, 0)]:
            AT[tag] = tuple(n_)
            n_ = [a + b for a, b in zip(n_, k)]

        split_in = list(range(U0["in_T"], U0["mem_k"]))
        split_up = list(range(U0["up"], U0["down"] + FFC))
        split_no = {n: i for i, n in enumerate(split_in + split_up)}

        def high(n):
            return w_part[split_no[n] % WH]

        def low(n):
            return w_part[WH + split_no[n] % WH]

        def tk_number(l, t, part=0):
            return [(0, 2, 0), (0, 0, 0), (0, 0, 1), (0, 1, 0), (1, 0, 0), (1, 1, 0)].index((l, t, part)) + 1

        block = ctx.enter_context(nc.Block())

        @block.sync
        def _(sp):
            for t, (c0, P) in enumerate(TILES[:2]):
                sp.dma_start(h[:, t, :], xin[c0:c0 + P, :]).then_inc(S("ld_h"), 16)
            sp.dma_start(h[0:META, 2, :], metain).then_inc(S("ld_h"), 16)
            sp.dma_start(cstc[:, :], cst).then_inc(S("ld_c"), 16)
            sp.dma_start(colc[:, :], cols).then_inc(S("ld_c"), 16)
            sp.dma_start(poolP.rearrange("p g s t -> p (g s t)"), poolm).then_inc(S("ld_c"), 16)
            sp.dma_start(bcP, bc_rows[2:3, :].to_broadcast([128, D])).then_inc(S("ld_c"), 16)
            sp.dma_start(bcF[:, :], bc_rows[0:1, :].to_broadcast([128, D])).then_inc(S("ld_c"), 16)
            for n in range(R):
                sp.dma_start(wring[:, n, :], units[n, :, :]).then_inc(S(f"w{n}"), 16)
            with sp.Fori(1, N_UNITS // R) as i:
                for s in range(R):
                    sp.wait_ge(S("w_used"), R * i + (s + 1 - R))
                    sp.dma_start(wring[:, s, :], units[ds(R * i + s, 1), :, :].rearrange("o p n -> (o p) n"))\
                        .then_inc(S(f"w{s}"), 16)
            for n in range(N_UNITS // R * R, N_UNITS):
                sp.wait_ge(S("w_used"), n + 1 - R)
                sp.dma_start(wring[:, n % R, :], units[n, :, :]).then_inc(S(f"w{n % R}"), 16)
            for t in range(2):
                sp.wait_ge(S("fin"), t + 1)
                sp.dma_start(out[t * 128:(t + 1) * 128, :], hn[:, t, :]).then_inc(S("stored"), 16)
            sp.wait_ge(S("stored"), 32)

        class Beside:

            def __init__(self, slot, lag=0):
                self.slot, self.lag, self.n = slot, lag, 0

            def to(self, n):
                for k in range(self.n, min(int(n) - self.lag, SLOTS)):
                    self.slot(k)
                    self.n = k + 1

        def gathers(l):
            base = 0 if l == 0 else 16 + 2 * SLOTS
            if l == 0:
                return [(2, 0), (0, 16), (1, 16 + SLOTS)]
            return [(0, base), (1, base + SLOTS)]

        @block.gpsimd
        def _(g):
            g.memset(zb[:, :], 0.0).then_inc(S("zeroed"), 1)
            g.memset(ss[:, :], 1.0).then_inc(S("zeroed"), 1)
            g.memset(hsum[:, :], 1.0).then_inc(S("zeroed"), 1)
            n_idx = [0]

            def indices(half, src):
                g.tensor_copy(ixc[:, half, :], src).then_inc(S("ixc"), 1)

            def slot(l, k, n, half, col):
                if not isinstance(n, int) or n >= NU:
                    g.wait_ge(S("dot"), n + (1 - NU))
                    g.sem_inc(S("u_go"), 1)
                g.indirect_dma_start(ug[:, k % NU, :], None, peer_u,
                                     bass.IndirectOffsetOnAxis(ap=ixc[:, half, col:col + 1], axis=0))\
                    .then_inc(S(f"u{k % NU}"), 16)
                if not isinstance(n, int) or n >= NV:
                    g.wait_ge(S("vsum"), n + (1 - NV))
                    g.sem_inc(S("v_go"), 1)
                g.indirect_dma_start(vg[:, k % NV, :], None, peer_v,
                                     bass.IndirectOffsetOnAxis(ap=ixc[:, half, col:col + 1], axis=0))\
                    .then_inc(S(f"v{k % NV}"), 16)

            for l in range(2):
                for t, base in gathers(l):
                    g.wait_ge(S("eidx"), tk_number(l, t))
                    if t == 2:
                        indices(1, eidx[:, t, 0:16])
                        n_idx[0] += 1
                        g.wait_ge(S("ixc"), n_idx[0])
                        for k in range(16):
                            slot(l, k, base + k, 1, k)
                        continue
                    done = n_idx[0]
                    turns = SLOTS // GB
                    for part, (i0, i1) in enumerate([(0, turns // 2), (turns // 2, turns)] if (l, t) == (0, 0)
                                                    else [(0, turns)]):
                        if part:
                            g.wait_ge(S("eidx"), tk_number(l, t, part))
                        with g.Fori(i0, i1) as i:
                            for half in range(2):
                                indices(half, eidx[:, t, ds(i * GB + 16 * half, 16)])
                                g.wait_ge(S("ixc"), 2 * i + (done + half + 1))
                                for kk in range(16):
                                    k = 16 * half + kk
                                    slot(l, k, GB * i + (base + k), half, kk)
                    n_idx[0] += 2 * (SLOTS // GB)

            def low_parts(units_):
                for n in units_:
                    g.wait_ge(S("w_high"), split_no[n] + 1)
                    g.tensor_tensor(low(n), wring[:, n % R, :], high(n), ALU.subtract).then_inc(S("w_low"), 1)

            g.wait_ge(S("vsum"), 16 + 4 * SLOTS)
            g.wait_ge(S("y"), 5)
            for t in range(2):
                g.dma_start(mrg[:, t, :], mem[t * 128:(t + 1) * 128, :]).then_inc(S("ld_m"), 16)
            g.dma_start(cs2c[:, :], cs2).then_inc(S("ld_m"), 16)
            g.dma_start(bcG[:, :], bc_rows[3:4, 0:512].to_broadcast([128, 512])).then_inc(S("ld_m"), 16)
            g.dma_start(tsb[0:32, 0:8], rel).then_inc(S("ld_m"), 16)
            low_parts(split_in)
            g.wait_ge(S("trev_sb"), 1)
            g.dma_start(trev_d, pw[0:8, 0, 0:384]).then_inc(S("trev_d"), 16)
            g.wait_ge(S("trev_d"), 16)
            rows = bass.AP(trev_d.tensor, 0, [[1, 128], [384, 8], [1, 256]])
            g.dma_start(pw.rearrange("p b n -> p (b n)").rearrange("p (h y) -> p h y", y=256), rows)\
                .then_inc(S("ld_b"), 16)
            g.wait_ge(S("out_h"), 2)
            g.dma_start(bcL, bc_rows[4:5, :].to_broadcast([128, D])).then_inc(S("ld_g"), 16)
            low_parts(split_up)

        @block.tensor
        def _(pe):
            owed = {}

            def claim(*banks):
                for b in banks:
                    if b in owed:
                        pe.wait_ge(*owed.pop(b))

            def owe(sem, val, *banks):
                for b in banks:
                    owed[b] = (S(sem), val)

            unit_n = [0]

            def unit():
                n = unit_n[0]
                unit_n[0] += 1
                pe.wait_ge(S(f"w{n % R}"), 16 * (n // R + 1))
                return wring[:, n % R, :]

            def used(ins):
                ins.then_inc(S("w_used"), 1)

            def transposes(tag, src, tiles, chunks=DC, tb=6):
                for n, t in enumerate(tiles):
                    P = TILES[t][1]
                    pe.wait_ge(S("x_ready"), AT[tag][2] + n + 1)
                    claim(tb, tb + 1)
                    for c in range(chunks):
                        last = nc.tensor.transpose(ps2(tb)[:, c * 128:c * 128 + P],
                                                   src(t)[:, c * 128:(c + 1) * 128], ident[0:P, 0:P])
                    last.then_inc(S("turned"), 1)
                    owe("turned_out", AT[tag][3] + n + 1, tb, tb + 1)

            def tokens_out(lhs, tiles, chunks, reader, b0=0, first=0, between=None):
                for n, t in enumerate(tiles):
                    claim(b0 + 2 * n, b0 + 2 * n + 1)
                for c in range(chunks):
                    w = unit()
                    for n, t in enumerate(tiles):
                        c0, P = TILES[t]
                        for j in range(2):
                            last = nc.tensor.matmul(ps[0:P, b0 + 2 * n + j, :], lhs(c, c0, P),
                                                    w[:, j * 512:(j + 1) * 512], start=c == 0, stop=c == chunks - 1)
                    used(last)
                    if between:
                        between(c + 1)
                for n, t in enumerate(tiles):
                    owe(reader, first + n + 1, b0 + 2 * n, b0 + 2 * n + 1)

            def cols_out(J, N, reader, banks, first=0, between=None, c0=0, x=xT):
                for j in range(J):
                    w = unit()
                    b = banks[j % len(banks)]
                    claim(b)
                    for c in range(DC):
                        last = nc.tensor.matmul(ps[:, b, 0:N], w[:, c * 128:(c + 1) * 128], x[:, c, c0:c0 + N],
                                                start=c == 0, stop=c == DC - 1)
                    used(last)
                    owe(reader, first + j + 1, b)
                    if between:
                        between(j + 1)

            def x_at(c, c0, P):
                return xT[:, c, c0:c0 + P]

            pe.wait_ge(S("ld_c"), 80)
            pe.wait_ge(S("zeroed"), 3)
            pe.wait_ge(S("x_ready"), AT["n0"][2] + 3)
            for c in range(DC):
                b = c % 6
                claim(b)
                for s, (c0, P) in enumerate(TILES):
                    last = nc.tensor.matmul(ps[:, b, 0:LTOK], hn[0:P, s, c * 128:(c + 1) * 128],
                                            poolP[0:P, c // 2, s, :], start=s == 0, stop=s == 2)
                last.then_inc(S("pool_pe"), 1)
                owe("pool_ev", c + 1, b)
            pe.wait_ge(S("pool_ev"), DC)
            claim(0, 1, 2, 3, 4, 5)
            for u in range(2):
                w = unit()
                for t, (c0, P) in enumerate(TILES):
                    for g in range(2):
                        for c in range(2):
                            last = nc.tensor.matmul(ps[0:P, 2 * t + u, g * 256:(g + 1) * 256],
                                                    xT[:, 4 * u + 2 * g + c, c0:c0 + P],
                                                    w[:, (2 * g + c) * 256:(2 * g + c + 1) * 256],
                                                    start=c == 0, stop=c == 1)
                used(last)
            for t in range(3):
                owe("mix0_ps", t + 1, 2 * t, 2 * t + 1)

            def scores(order, qT, reader, first, tick):
                ks = [unit(), unit()]
                for n, t in enumerate(order):
                    c0, P = TILES[t]
                    q0 = c0 if reader == "sc0_ev" else 0
                    claim(0, 1, 2, 3)
                    for j in range(16):
                        last = nc.tensor.matmul(ps[0:P, j // 4, (j % 4) * 128:(j % 4 + 1) * 128],
                                                qT[:, j, q0:q0 + P], ks[j // 8][:, (j % 8) * 128:(j % 8 + 1) * 128],
                                                start=True, stop=True)
                    last.then_inc(S(tick), 1)
                    owe(reader, first + n + 1, 0, 1, 2, 3)
                claim(5)
                for _ in ks:
                    used(nc.tensor.matmul(ps[0:1, 5, 0:2], zb[:, 0:1], zb[:, 0:2], start=True, stop=True))

            def sums_begin(P):
                claim(6, 7)
                for j in range(2):
                    nc.tensor.matmul(ps[0:P, 6 + j, :], zb[:, 0:P], zb[:, :], start=True, stop=False)

            def sums_slot(P, k, n, vfill):
                pe.wait_ge(S("diag"), n + 1)
                pe.wait_ge(S(f"v{k % NV}"), vfill)
                for j in range(2):
                    last = nc.tensor.matmul(ps[0:P, 6 + j, :], diag[:, k % 4, 0:P],
                                            vg[:, k % NV, j * 512:(j + 1) * 512], start=False, stop=False)
                last.then_inc(S("vsum"), 1)

            def sums_end(t, m):
                P = TILES[t][1]
                for j in range(2):
                    last = nc.tensor.matmul(ps[0:P, 6 + j, :], ident[0:P, 0:P],
                                            h[0:P, t, j * 512:(j + 1) * 512], start=False, stop=True)
                last.then_inc(S("y_pe"), 1)
                owe("y", m, 6, 7)

            def sums_loop(base, start=0):
                with pe.Fori(start // GB, SLOTS // GB) as i:
                    for k in range(GB):
                        sums_slot(128, k, GB * i + (base + k), 16 * (GB // NV) * i + 16 * ((base + k) // NV + 1))

            def beside(base):
                return Beside(lambda k: sums_slot(128, k, base + k, 16 * ((base + k) // NV + 1)), LAG)

            transposes("f0", lambda t: hn[0:TILES[t][1], t, :], [0, 1, 2])
            pe.wait_ge(S("turned_out"), AT["f0"][3] + 3)
            cols_out(16, LTOK, "q0_ev", range(6))
            pe.wait_ge(S("q0_ev"), 16)
            scores([2, 0, 1], qT0, "sc0_ev", 0, "sc0_pe")
            (_, m_base), (_, a_base), (_, b_base) = gathers(0)
            sums_begin(META)
            for k in range(16):
                sums_slot(META, k, m_base + k, 16 * ((m_base + k) // NV + 1))
            sums_end(2, 1)
            sums_begin(128)
            first = beside(a_base)
            first.to(STRAIGHT + LAG)
            sums_loop(a_base, STRAIGHT)
            sums_end(0, 2)

            def front(i, bg):
                X = "AB"[i]
                kvt = [0, 2] if i == 0 else [1]
                c0 = TILES[i][0]
                plan = PLAN[i]

                def at(stage, j=0, J=1):
                    a = plan[stage]
                    bg.to(a + (plan[STAGES[STAGES.index(stage) + 1]] - a) * j / J)

                hT = lambda t: hn[0:TILES[t][1], t, :]
                at("kv")
                transposes("kv" + X, hT, kvt, tb=4)
                at("k")
                pe.wait_ge(S("turned_out"), AT["kv" + X][3] + len(kvt))
                tokens_out(x_at, kvt, DC, "k_ev", first=2 * i, between=lambda c: at("k", c, DC))
                tokens_out(x_at, kvt, DC, "v_ev", first=2 * i, between=lambda c: at("v", c, DC))
                at("kh")
                transposes("kh" + X, hT, kvt, tb=4)
                at("n1")
                transposes("n1" + X, hT, [i], tb=4)
                at("q")
                pe.wait_ge(S("turned_out"), AT["n1" + X][3] + 1)
                tokens_out(x_at, [i], DC, "q_ev", first=i, between=lambda c: at("q", c, DC))
                at("qh")
                transposes("qh" + X, hT, [i], tb=4)
                pe.wait_ge(S("turned_out"), AT["qh" + X][3] + 1)
                pe.wait_ge(S("v_ev"), 2 + i)
                stick(i, lambda p: at("stick", p, 8))
                at("o")
                pe.wait_ge(S("o_ev"), 16 * (i + 1))
                tokens_out(lambda c, c0, P: oT[:, c, 0:P], [i], DC, "wo_h", first=i,
                           between=lambda c: at("o", c, DC))
                at("f1")
                transposes("f1" + X, hT, [i], tb=4)
                at("wq")
                pe.wait_ge(S("turned_out"), AT["f1" + X][3] + 1)
                cols_out(16, 128, "q1_ev", range(4), first=16 * i, c0=c0, between=lambda j: at("wq", j, 16))
                at("sc")
                pe.wait_ge(S("q1_ev"), 16 * (i + 1))
                scores([i], qT1, "sc1_ev", i, "sc1_pe")
                bg.to(SLOTS + LAG)

            def stick(i, tick):
                kt = [0, 2] if i == 0 else [0, 1, 2]
                nk = len(kt)
                ones, tri = cc("ones", 128), cc("tri", 128)

                def z(p):
                    n = 8 * i + p
                    claim(0, 1)
                    for r in range(2):
                        rows = slice(64 * r, 64 * r + 64)
                        for a, k in enumerate(kt):
                            last = nc.tensor.matmul(ps[:, r, a * 128:(a + 1) * 128], kT[rows, p, k * 128:(k + 1) * 128],
                                                    qhT[rows, p, :], start=True, stop=True)
                    last.then_inc(S("z_pe"), 1)
                    owe("z_sb", n + 1, 0, 1)

                def after(p):
                    n = 8 * i + p
                    sp_ = st[:, p % 2, 1, 0:nk * 256].rearrange("p (r k n) -> p r k n", r=2, k=nk)
                    pe.wait_ge(S("sp"), n + 1)
                    claim(2, 3)
                    for a in range(nk):
                        later = list(range(a + 1, nk - 1)) if a < nk - 1 else list(range(nk - 1))
                        out_ = ps2(2)[:, a * 256:(a + 1) * 256]
                        last = nc.tensor.matmul(out_, tri, sp_[:, :, a, :], start=True, stop=not later)
                        for b in later:
                            last = nc.tensor.matmul(out_, ones, sp_[:, :, b, :], start=False, stop=b == later[-1])
                    last.then_inc(S("c_pe"), 1)
                    owe("dd", n + 1, 2, 3)

                def values(p):
                    n = 8 * i + p
                    w_ = st[:, p % 2, 0, 0:nk * 256].rearrange("p (r k n) -> p r k n", r=2, k=nk)
                    pe.wait_ge(S("w"), n + 1)
                    for r in range(2):
                        rows = slice(64 * r, 64 * r + 64)
                        claim(4 + r)
                        v = slice(p * 128 + 64 * r, p * 128 + 64 * r + 64)
                        for a, k in enumerate(kt):
                            last = nc.tensor.matmul(ps[rows, 4 + r, 0:128], vk[:, k, v], w_[:, r, a, :],
                                                    start=a == 0, stop=a == nk - 1)
                        owe("o_ev", 2 * n + r + 1, 4 + r)
                    last.then_inc(S("o_pe"), 1)

                z(0)
                for p in range(8):
                    tick(p)
                    if p < 7:
                        z(p + 1)
                    after(p)
                    if p:
                        values(p - 1)
                values(7)

            sums_begin(128)
            front(0, beside(b_base))
            sums_end(1, 3)
            (_, a_base), (_, b_base) = gathers(1)
            sums_begin(128)
            front(1, beside(a_base))
            sums_end(0, 4)
            sums_begin(128)
            sums_loop(b_base)
            sums_end(1, 5)

            def halves_out(x, reader, val, b0):
                claim(b0, b0 + 1)
                for u in range(4):
                    w = unit()
                    for c in range(2):
                        for t in range(2):
                            last = nc.tensor.matmul(ps[:, b0 + t, :], x[:, 2 * u + c, t * 128:t * 128 + 128],
                                                    w[:, c * 512:(c + 1) * 512], start=u + c == 0, stop=u + c == 4)
                    used(last)
                owe(reader, val, b0, b0 + 1)

            def split_unit():
                n = unit_n[0]
                unit()
                pe.wait_ge(S("w_low"), split_no[n] + 1)
                return high(n), low(n)

            def by_parts(dst, x, w, start, stop):
                for m, (a, b) in enumerate([(x[0], w[0]), (x[0], w[1]), (x[1], w[0])]):
                    last = nc.tensor.matmul(dst, a, b, start=start and m == 0, stop=stop and m == 2)
                return last

            def split_cols_out(J, xs, reader, banks):
                for j in range(J):
                    wh, wl = split_unit()
                    b = banks[j % len(banks)]
                    claim(b)
                    for c in range(DC):
                        e = slice(c * 128, (c + 1) * 128)
                        last = by_parts(ps[:, b, 0:SEQ], (wh[:, e], wl[:, e]),
                                        [x[:, c, :] for x in xs], c == 0, c == DC - 1)
                    used(last)
                    owe(reader, j + 1, b)

            def split_halves_out(xs, reader, val, b0):
                claim(b0, b0 + 1)
                for u in range(4):
                    wh, wl = split_unit()
                    for c in range(2):
                        e = slice(c * 512, (c + 1) * 512)
                        for t in range(2):
                            last = by_parts(ps[:, b0 + t, :],
                                            [x[:, 2 * u + c, t * 128:t * 128 + 128] for x in xs],
                                            (wh[:, e], wl[:, e]), u + c == 0, u + c == 4)
                    used(last)
                owe(reader, val, b0, b0 + 1)

            transposes("n2", lambda t: hn[0:128, t, :], [0, 1])
            pe.wait_ge(S("x_low"), 2)
            split_cols_out(20, (xH, xL), "iT_ev", range(6))
            pe.wait_ge(S("ld_m"), 80)
            claim(6)
            nc.tensor.matmul(ps[0:8, 6, 0:384], tsb[0:32, 0:8], cs2c[0:32, CS2["bucket"]:CS2["bucket"] + 384],
                             start=True, stop=True).then_inc(S("trev_pe"), 1)
            owe("trev_sb", 1, 6)
            for k in range(3):
                split_halves_out((xH, xL), "iv_ev", 2 * k + 2, 2 * k)
            transposes("nm", lambda t: hn[0:128, t, :], [0, 1])
            pe.wait_ge(S("turned_out"), AT["nm"][3] + 2)
            cols_out(4, SEQ, "m_ev", [0, 1, 2, 3], x=memT)
            halves_out(memT, "m_ev", 6, 4)

            for j in range(8):
                b = j % 2
                pe.wait_ge(S("iT_ev"), 8 + j + 1)
                claim(b)
                nc.tensor.matmul(ps[:, b, 0:256], cs2c[:, 0:128], qkT[:, 8 + j, :], start=True, stop=True)\
                    .then_inc(S("sw_pe"), 1)
                owe("rot_ps", j + 1, b)
            for hd in range(4):
                b = 2 + hd % 2
                pe.wait_ge(S("rot"), 4 + hd + 1)
                claim(b)
                nc.tensor.matmul(ps[:, b, 0:256], qkT[:, 12 + hd, 0:128], qkT[:, 8 + hd, :], start=True, stop=True)
                nc.tensor.matmul(ps[:, b, 256:384], qkT[:, 12 + hd, 128:256], qkT[:, 8 + hd, 128:256],
                                 start=True, stop=True).then_inc(S("rs_pe"), 1)
                owe("rs_sb", hd + 1, b)
            pe.wait_ge(S("iv_ev"), 4)
            claim(6, 7)
            for hd in range(4):
                e = slice(hd * 128, hd * 128 + 128)
                sT = mrg[:, hd // 2, (hd % 2) * 384:(hd % 2) * 384 + 384]
                pe.wait_ge(S("rs_sb"), hd + 1)
                nc.tensor.matmul(ps[:, 6, e], sT[:, 0:128], vtok[:, 1, 0, e], start=True, stop=True)
                nc.tensor.matmul(ps[:, 7, e], sT[:, 128:256], vtok[:, 1, 0, e], start=True, stop=False)
                nc.tensor.matmul(ps[:, 7, e], sT[:, 256:384], vtok[:, 1, 1, e], start=False, stop=True)\
                    .then_inc(S("ry_pe"), 1)
            owe("ry_ps", 1, 6, 7)

            def soft_s(n):
                b = n % 2
                claim(b)
                if n < 8:
                    c, r = n // 2, slice(64 * (n % 2), 64 * (n % 2) + 64)
                    nc.tensor.matmul(ps[:, b, 0:128], qkT[r, c, 0:128], qkT[r, 4 + c, 0:128], start=True, stop=True)
                    nc.tensor.matmul(ps[:, b, 128:384], qkT[r, c, 128:256], qkT[r, 4 + c, :], start=True, stop=True)\
                        .then_inc(S("ss_pe"), 1)
                else:
                    for t in range(2):
                        last = nc.tensor.matmul(ps[:, b, t * 256:(t + 1) * 256],
                                                qkT[:, 16 + n - 8, t * 128:(t + 1) * 128], kmT[:, n - 8, :],
                                                start=True, stop=True)
                    last.then_inc(S("ss_pe"), 1)
                owe("ss_ps", n + 1, b)

            def soft_t(n):
                b = 2 + n % 2
                p_ = pw[:, n % 2, :]
                pe.wait_ge(S("pn"), n + 1)
                claim(b)
                if n < 8:
                    order = [(0, 0), (1, 128), (2, 256)]
                else:
                    order = [(0, 0), (2, 128), (1, 256), (3, 384)]
                for src, dst in order:
                    last = nc.tensor.transpose(ps[:, b, dst:dst + 128], p_[:, src * 128:(src + 1) * 128], ident)
                last.then_inc(S("pt_pe"), 1)
                owe("pt_ev", n + 1, b)

            def soft_o(n):
                b = 4 + n % 2
                pT_ = pw[:, n % 2, 512:1024]
                pe.wait_ge(S("pt_ev"), n + 1)
                claim(b)
                if n < 8:
                    c, r = n // 2, slice(64 * (n % 2), 64 * (n % 2) + 64)
                    v = slice(n * 64, n * 64 + 64)
                    nc.tensor.matmul(ps[r, b, 0:256], vtok[:, 0, 0, v], pT_[:, 0:256], start=True, stop=False)
                    nc.tensor.matmul(ps[r, b, 128:256], vtok[:, 0, 1, v], pT_[:, 256:384], start=False, stop=True)\
                        .then_inc(S("so_pe"), 1)
                else:
                    v = slice((n - 8) * 128, (n - 8) * 128 + 128)
                    nc.tensor.matmul(ps[:, b, 0:256], vmem[:, 0, v], pT_[:, 0:256], start=True, stop=False)
                    nc.tensor.matmul(ps[:, b, 0:256], vmem[:, 1, v], pT_[:, 256:512], start=False, stop=True)\
                        .then_inc(S("so_pe"), 1)
                owe("so_ev", n + 1, b)

            pe.wait_ge(S("ld_b"), 16)
            claim(0, 1, 2, 3)
            for j in range(4):
                last = nc.tensor.matmul(ps[:, j, :], cs2c[:, CS2["flip"]:CS2["flip"] + 128],
                                        pw.rearrange("p b n -> p (b n)")[:, j * 512:(j + 1) * 512],
                                        start=True, stop=True)
            last.then_inc(S("flip_pe"), 1)
            owe("bias", 1, 0, 1, 2, 3)

            def z_unit(u):
                w = unit()
                if u % 4 == 0:
                    claim(6, 7)
                for c in range(2):
                    for t in range(2):
                        last = nc.tensor.matmul(ps[:, 6 + t, :], xT[:, 2 * (u % 4) + c, t * 128:t * 128 + 128],
                                                w[:, c * 512:(c + 1) * 512], start=u % 4 + c == 0, stop=u % 4 + c == 4)
                used(last)
                if u % 4 == 3:
                    owe("z_ev", u // 4 + 1, 6, 7)

            soft_s(0)
            for n in range(12):
                if n < 11:
                    soft_s(n + 1)
                z_unit(2 * n)
                soft_t(n)
                z_unit(2 * n + 1)
                if n:
                    soft_o(n - 1)
            soft_o(11)
            transposes("yr", lambda t: hn[:, 0, t * 512:(t + 1) * 512], [0, 1], chunks=4)
            pe.wait_ge(S("so_ev"), 12)
            pe.wait_ge(S("turned_out"), AT["yr"][3] + 2)
            for k in range(3):
                tokens_out(lambda c, c0, P: yT[:, k, c, c0:c0 + P], [0, 1], 4, f"br{k}_ps", b0=0 if k != 1 else 4)
            transposes("mg", lambda t: mrg[:, t, :], [0, 1])
            pe.wait_ge(S("turned_out"), AT["mg"][3] + 2)
            tokens_out(x_at, [0, 1], DC, "out_h")
            transposes("n3", lambda t: hn[0:128, t, :], [0, 1])
            pe.wait_ge(S("x_low"), 4)
            split_cols_out(2 * FFC, (xH, xL), "up_ev", range(6))
            claim(0, 1, 2, 3)
            for c in range(FFC):
                wh, wl = split_unit()
                pe.wait_ge(S("a_low"), c + 1)
                for t in range(2):
                    for j in range(2):
                        e = slice(j * 512, (j + 1) * 512)
                        last = by_parts(ps[:, 2 * t + j, :],
                                        [a_[:, c, t * 128:(t + 1) * 128] for a_ in (aH, aL)],
                                        (wh[:, e], wl[:, e]), c == 0, c == FFC - 1)
                used(last)

        @block.scalar
        def _(act):
            def squares(tag, src, dst, tiles, col):
                for n, t in enumerate(tiles):
                    P = TILES[t][1]
                    nc.scalar.activation(dst(t), src(t), ACT.Square, accum_out=ss[0:P, col + n:col + n + 1])\
                        .then_inc(S("squared"), 1)

            def root(tag, ap):
                act.wait_ge(S("var_ready"), AT[tag][1] + 1)
                nc.scalar.activation(ap, ap, ACT.Sqrt).then_inc(S("std_ready"), 1)

            def hT(t):
                return hn[0:TILES[t][1], t, :]

            def hh(t):
                return h[0:TILES[t][1], t, :]

            def t_out(tag, tiles, dst, scale=1.0, tb=6):
                for n, t in enumerate(tiles):
                    c0, P = TILES[t]
                    act.wait_ge(S("turned"), AT[tag][3] + n + 1)
                    nc.scalar.activation(dst(c0, P), ps2(tb).rearrange("p (c n) -> p c n", n=128)[:, :, 0:P],
                                         ACT.Copy, scale=scale).then_inc(S("turned_out"), 1)

            def tokens_ev(units_done, tiles, dst, sem, func=ACT.Copy, b0=0):
                act.wait_ge(S("w_used"), units_done)
                for n, t in enumerate(tiles):
                    nc.scalar.activation(dst(t), ps2(b0 + 2 * n, TILES[t][1]), func).then_inc(S(sem), 1)

            act.wait_ge(S("ld_h"), 48)
            act.wait_ge(S("ld_c"), 80)
            act.wait_ge(S("zeroed"), 3)
            squares("n0", hh, hT, [0, 1, 2], 0)
            root("n0", rs[:, 0:3])
            for c in range(DC):
                act.wait_ge(S("pool_pe"), c + 1)
                nc.scalar.activation(xT[:, c, :], ps[:, c % 6, 0:LTOK], ACT.Copy, scale=gcol("mix0", c))\
                    .then_inc(S("pool_ev"), 1)

            def gelu(k, n):
                act.wait_ge(S("dot"), n + 1)
                nc.scalar.activation(gel[:, k % 8:k % 8 + 1], dots[:, k % 8:k % 8 + 1], ACT.Gelu)\
                    .then_inc(S("gelu"), 1)

            def gelu_loop(base, start=0):
                with act.Fori(start // GB, SLOTS // GB) as i:
                    for k in range(GB):
                        gelu(k, GB * i + (base + k))

            def beside(base):
                return Beside(lambda k: gelu(k, base + k))

            def y_out(t, m):
                act.wait_ge(S("y_pe"), m)
                nc.scalar.activation(hh(t), ps2(6, TILES[t][1]), ACT.Copy).then_inc(S("y"), 1)

            def gate_exps(l, t, part=0):
                act.wait_ge(S("gx"), tk_number(l, t, part))
                G = gates[t][:, 64 * part:16 if t == 2 else 64 * (part + 1) if (l, t) == (0, 0) else 128]
                nc.scalar.activation(G, G, ACT.Exp).then_inc(S("ge"), 1)

            act.wait_ge(S("mix0_h"), 3)
            squares("f0", hh, hT, [0, 1, 2], 3)
            root("f0", rs[:, 3:6])
            t_out("f0", [0, 1, 2], lambda c0, P: xT[:, :, c0:c0 + P])
            for j in range(16):
                act.wait_ge(S("w_used"), U0["wq"] + j + 1)
                nc.scalar.activation(qT0[:, j, :], ps[:, j % 6, 0:LTOK], ACT.Copy).then_inc(S("q0_ev"), 1)
            for n, t in enumerate([2, 0, 1]):
                P = TILES[t][1]
                act.wait_ge(S("sc0_pe"), n + 1)
                if t == 1:
                    act.wait_ge(S("md"), 128)
                nc.scalar.activation(s_sb0[0 if t == 0 else 1][0:P, :], ps[0:P, 0:4, :].rearrange("p b n -> p (b n)"),
                                     ACT.Copy).then_inc(S("sc0_ev"), 1)
                if t == 2:
                    act.wait_ge(S("sc0_ev"), 1)
                    for hd in range(PEER_H):
                        r = slice(hd * META, (hd + 1) * META)
                        act.dma_start(s_m[r, :], s_sb0[1][0:META, hd * 256:(hd + 1) * 256]).then_inc(S("md"), 16)
                    for hd in range(PEER_H):
                        r = slice(hd * META, (hd + 1) * META)
                        act.dma_start(hnm[r, :], hn[0:META, 2, :]).then_inc(S("md2"), 16)
            act.wait_ge(S("x_ready"), AT["f0"][2] + 3)
            act.dma_start(bcF[:, :], bc_rows[1:2, :].to_broadcast([128, D])).then_inc(S("ld_f1"), 16)
            gate_exps(0, 2)
            (_, m_base), (_, a_base), (_, b_base) = gathers(0)
            for k in range(16):
                if k == 14:
                    gate_exps(0, 0)
                gelu(k, m_base + k)
            y_out(2, 1)
            first = beside(a_base)
            first.to(TOPK_A)
            gate_exps(0, 0, 1)
            first.to(TOPK_B)
            gate_exps(0, 1)
            first.to(STRAIGHT)
            gelu_loop(a_base, STRAIGHT)
            y_out(0, 2)

            def front(i, bg):
                X = "AB"[i]
                kvt = [0, 2] if i == 0 else [1]
                plan = PLAN[i]

                def at(stage, j=0, J=1):
                    a = plan[stage]
                    bg.to(a + (plan[STAGES[STAGES.index(stage) + 1]] - a) * j / J)

                at("kv")
                act.wait_ge(S("y"), 2 + i)
                squares("kv" + X, hh, hT, kvt, (6, 8)[i])
                root("kv" + X, rs[:, (6, 8)[i]:(6, 8)[i] + len(kvt)])
                at("v")
                tokens_ev(U0["k" + X] + 8, kvt, hT, "k_ev")
                root("kh" + X, hsum[:, 0:16 * len(kvt)])
                at("kh")
                act.wait_ge(S("kv_zero"), 1)
                tokens_ev(U0["v" + X] + 8, kvt, lambda t: vk[0:TILES[t][1], t, :], "v_ev")
                t_out("kh" + X, kvt, lambda c0, P: kT[:, :, c0:c0 + P], gcol("knorm"), tb=4)
                at("n1")
                squares("n1" + X, hh, hT, [i], 9 + i)
                root("n1" + X, rs[:, 9 + i:10 + i])
                at("qh")
                tokens_ev(U0["q" + X] + 8, [i], hT, "q_ev")
                root("qh" + X, hsum[:, 0:16])
                t_out("qh" + X, [i], lambda c0, P: qhT[:, :, 0:P], gcol("qnorm"), tb=4)
                stick(i, lambda p: at("stick", p, 8))
                at("f1")
                act.wait_ge(S("wo_h"), i + 1)
                squares("f1" + X, hh, hT, [i], 11 + i)
                root("f1" + X, rs[:, 11 + i:12 + i])
                t_out("f1" + X, [i], lambda c0, P: xT[:, :, c0:c0 + P], tb=4)
                for j in range(16):
                    at("wq", j + 1, 16)
                    act.wait_ge(S("w_used"), U0["wq" + X] + j + 1)
                    nc.scalar.activation(qT1[:, j, :], ps[:, j % 4, 0:128], ACT.Copy).then_inc(S("q1_ev"), 1)
                at("topk")
                act.wait_ge(S("sc1_pe"), i + 1)
                nc.scalar.activation(s_sb1[:, :], ps[:, 0:4, :].rearrange("p b n -> p (b n)"), ACT.Copy)\
                    .then_inc(S("sc1_ev"), 1)
                at("topk", GATE_AT, TOPK_STEPS)
                gate_exps(1, i)
                bg.to(SLOTS)

            def stick(i, tick):
                nk = 2 + i

                def front_(p):
                    n = 8 * i + p
                    t_ = st[:, p % 2, 1, 0:nk * 256]
                    act.wait_ge(S("tmin"), n + 1)
                    nc.scalar.activation(t_, t_, ACT.Exp).then_inc(S("ex"), 1)
                    act.wait_ge(S("ex"), n + 1)
                    nc.scalar.activation(t_, t_, ACT.Ln, bias=1.0).then_inc(S("ln"), 1)

                def weights(p):
                    n = 8 * i + p
                    w_ = st[:, p % 2, 0, 0:nk * 256]
                    act.wait_ge(S("dd"), n + 1)
                    nc.scalar.activation(w_, w_, ACT.Exp).then_inc(S("w"), 1)

                def out_(p):
                    n = 8 * i + p
                    act.wait_ge(S("o_pe"), n + 1)
                    for r in range(2):
                        rows = slice(64 * r, 64 * r + 64)
                        nc.scalar.activation(oT[rows, p, :], ps[rows, 4 + r, 0:128], ACT.Copy).then_inc(S("o_ev"), 1)

                front_(0)
                for p in range(8):
                    tick(p)
                    if p:
                        out_(p - 1)
                    weights(p)
                    if p < 7:
                        front_(p + 1)
                out_(7)

            front(0, beside(b_base))
            y_out(1, 3)
            (_, a_base), (_, b_base) = gathers(1)
            front(1, beside(a_base))
            y_out(0, 4)
            gelu_loop(b_base)
            y_out(1, 5)

            act.wait_ge(S("y"), 5)
            squares("n2", hh, hT, [0, 1], 13)
            root("n2", rs[:, 13:15])

            def w_high(n):
                if n in split_no:
                    act.wait_ge(S(f"w{n % R}"), 16 * (n // R + 1))
                    act.wait_ge(S("w_used"), n - WH + 1)
                    nc.scalar.activation(high(n), wring[:, n % R, :], ACT.Copy).then_inc(S("w_high"), 1)

            def x_high(tag):
                for t in range(2):
                    act.wait_ge(S("turned_out"), AT[tag][3] + t + 1)
                    nc.scalar.activation(xH[:, :, t * 128:(t + 1) * 128],
                                         xT[:, :, t * 128:(t + 1) * 128], ACT.Copy).then_inc(S("x_high"), 1)

            x_high("n2")
            for n in range(WH - 1):
                w_high(U0["in_T"] + n)
            for j in range(20):
                if j == 6:
                    act.wait_ge(S("ld_m"), 80)
                    squares("nm", lambda t: mrg[:, t, :], hT, [0, 1], 15)
                    root("nm", rs[:, 15:17])
                w_high(U0["in_T"] + j + WH - 1)
                act.wait_ge(S("w_used"), U0["in_T"] + j + 1)
                nc.scalar.activation(qkT[:, j, :], ps[:, j % 6, 0:256], ACT.Copy).then_inc(S("iT_ev"), 1)
            for k in range(3):
                for n in range(4):
                    if U0["in_v"] + 4 * k + n + WH - 1 < U0["mem_k"]:
                        w_high(U0["in_v"] + 4 * k + n + WH - 1)
                act.wait_ge(S("w_used"), U0["in_v"] + 4 * k + 4)
                for t in range(2):
                    nc.scalar.activation(vtok[:, k, t, :], ps[:, 2 * k + t, :], ACT.Copy if k < 2 else ACT.Sigmoid)\
                        .then_inc(S("iv_ev" if k < 2 else "sg"), 1)
            for j in range(4):
                act.wait_ge(S("w_used"), U0["mem_k"] + j + 1)
                nc.scalar.activation(kmT[:, j, :], ps[:, j, 0:256], ACT.Copy).then_inc(S("m_ev"), 1)
            act.wait_ge(S("w_used"), U0["mem_v"] + 4)
            for t in range(2):
                nc.scalar.activation(vmem[:, t, :], ps[:, 4 + t, :], ACT.Copy).then_inc(S("m_ev"), 1)
            root("ry", tsb[:, 16:24])
            act.wait_ge(S("flip_pe"), 1)
            nc.scalar.activation(biasT.rearrange("p h y -> p (h y)"), ps[:, 0:4, :].rearrange("p b n -> p (b n)"),
                                 ACT.Copy).then_inc(S("bias"), 1)

            def soft_e(n):
                p_ = pw[:, n % 2, :]
                act.wait_ge(S("nmx"), n + 1)
                if n >= 2:
                    act.wait_ge(S("pt_pe"), n - 1)
                if n < 8:
                    spans, src, scale = [(0, 128), (128, 384)], p_, 1.0
                else:
                    spans, src, scale = [(0, 256), (256, 512)], ps[:, n % 2, :], RET_DK ** -0.5
                for t, (a, b) in enumerate(spans):
                    col = 8 * (n % 2) + t
                    nc.scalar.activation(p_[:, a:b], src[:, a:b], ACT.Exp, bias=nmx[:, col:col + 1], scale=scale,
                                         accum_out=nmx[:, col + 2:col + 3]).then_inc(S("pe_"), 1)

            def soft_tev(n):
                b = 2 + n % 2
                w_ = 384 if n < 8 else 512
                act.wait_ge(S("pt_pe"), n + 1)
                if n >= 2:
                    act.wait_ge(S("so_pe"), n - 1)
                nc.scalar.activation(pw[:, n % 2, 512:512 + w_], ps[:, b, 0:w_], ACT.Copy).then_inc(S("pt_ev"), 1)

            def soft_oev(n):
                act.wait_ge(S("so_pe"), n + 1)
                if n < 8:
                    c, r = n // 2, slice(64 * (n % 2), 64 * (n % 2) + 64)
                    dst = yT[r, 0, c, :]
                else:
                    r = slice(0, 128)
                    dst = yT[:, 2, n - 8, :]
                nc.scalar.activation(dst, ps[r, 4 + n % 2, 0:256], ACT.Copy).then_inc(S("so_ev"), 1)

            soft_e(0)
            for n in range(12):
                if n < 11:
                    soft_e(n + 1)
                soft_tev(n)
                if n:
                    soft_oev(n - 1)
                if n % 2:
                    m = n // 2
                    act.wait_ge(S("w_used"), U0["in_z"] + 4 * m + 4)
                    nc.scalar.activation(zs[:, m // 2, :, (m % 2) * 512:(m % 2 + 1) * 512], ps[:, 6:8, :], ACT.Copy)\
                        .then_inc(S("z_ev"), 1)
            soft_oev(11)
            for t in range(2):
                act.wait_ge(S("turned"), AT["yr"][3] + t + 1)
                nc.scalar.activation(yT[:, 1, :, t * 128:(t + 1) * 128],
                                     ps[:, 6, :].rearrange("p (c n) -> p c n", n=128), ACT.Copy)\
                    .then_inc(S("turned_out"), 1)
            for k in range(3):
                act.wait_ge(S("z_ev"), 2 * k + 2)
                nc.scalar.activation(zs[:, k, :, :], zs[:, k, :, :], ACT.Sigmoid).then_inc(S("z_sig"), 1)
            t_out("mg", [0, 1], lambda c0, P: xT[:, :, c0:c0 + P])
            act.wait_ge(S("out_h"), 2)
            squares("n3", hh, hT, [0, 1], 17)
            root("n3", rs[:, 17:19])
            x_high("n3")
            for n in range(WH - 1):
                w_high(U0["up"] + n)

            def a_high(j):
                act.wait_ge(S("a_T"), j + 1)
                nc.scalar.activation(aH[:, j, :], aT[:, j % 2, :], ACT.Copy).then_inc(S("a_high"), 1)

            for j in range(FFC):
                for k in range(2):
                    w_high(U0["up"] + 2 * j + k + WH - 1)
                    act.wait_ge(S("w_used"), U0["up"] + 2 * j + k + 1)
                    if j >= 2:
                        act.wait_ge(S("cv"), 2 * (j - 2) + k + 1)
                    else:
                        act.wait_ge(S("padded"), 1)
                    nc.scalar.activation(up_in[:, j % 2, k, 2:258], ps[:, (2 * j + k) % 6, 0:256], ACT.Copy)\
                        .then_inc(S("up_ev"), 1)
                act.wait_ge(S("cv"), 2 * j + 1)
                nc.scalar.activation(up_cv[:, j % 2, 0, :], up_cv[:, j % 2, 0, :], ACT.Gelu).then_inc(S("gate"), 1)
                if j:
                    a_high(j - 1)
            a_high(FFC - 1)
            for c in range(FFC - WH + 1):
                w_high(U0["down"] + c + WH - 1)
            act.wait_ge(S("down_h"), 2)
            squares("n4", hh, hT, [0, 1], 19)
            root("n4", rs[:, 19:21])

        @block.vector
        def _(dve):
            chain = [0]

            def link(ins):
                chain[0] += 1
                ins.then_inc(S("dve_chain"), 1)
                dve.wait_ge(S("dve_chain"), chain[0])

            v = nc.vector

            def hT(t):
                return hn[0:TILES[t][1], t, :]

            def hh(t):
                return h[0:TILES[t][1], t, :]

            def rstd(tag, src, dst, n_wait, width):
                if n_wait:
                    dve.wait_ge(S("squared"), AT[tag][0] + n_wait)
                v.tensor_scalar(dst, src, 1.0 / width, EPS, ALU.mult, ALU.add).then_inc(S("var_ready"), 1)
                dve.wait_ge(S("std_ready"), AT[tag][1] + 1)
                link(v.reciprocal(dst, dst))

            def norm(tag, tiles, col, src=hh, gain=None):
                rstd(tag, ss[:, col:col + len(tiles)], rs[:, col:col + len(tiles)], len(tiles), D)
                for n, t in enumerate(tiles):
                    P = TILES[t][1]
                    r = rs[0:P, col + n:col + n + 1]
                    if gain is None:
                        i = v.tensor_scalar(hT(t), src(t), r, None, ALU.mult)
                    else:
                        i = v.scalar_tensor_tensor(hT(t), src(t), r, gain[0:P, :], ALU.mult, ALU.mult)
                    i.then_inc(S("x_ready"), 1)

            def t_out(tag, tiles, gain, free=None, tb=6, dst=xT):
                if free is not None:
                    dve.wait_ge(S("w_used"), free)
                for n, t in enumerate(tiles):
                    c0, P = TILES[t]
                    dve.wait_ge(S("turned"), AT[tag][3] + n + 1)
                    v.tensor_tensor(dst[:, :, c0:c0 + P], ps2(tb).rearrange("p (c n) -> p c n", n=128)[:, :, 0:P],
                                    gains(gain, P), ALU.mult).then_inc(S("turned_out"), 1)

            def add_h(units_done, sem, tiles):
                dve.wait_ge(S("w_used"), units_done)
                for n, t in enumerate(tiles):
                    v.tensor_tensor(hh(t), hh(t), ps2(2 * n, TILES[t][1]), ALU.add).then_inc(S(sem), 1)

            dve.wait_ge(S("zeroed"), 3)
            dve.wait_ge(S("ld_h"), 48)
            dve.wait_ge(S("ld_c"), 80)
            norm("n0", [0, 1, 2], 0)
            dve.wait_ge(S("w_used"), U0["pool"] + 2)
            for t in range(3):
                P = TILES[t][1]
                v.tensor_tensor(hT(t), ps2(2 * t, P), bcP[0:P, :], ALU.mult).then_inc(S("mix0_ps"), 1)
                dve.wait_ge(S("mix0_ps"), t + 1)
                v.tensor_tensor(hh(t), hh(t), hT(t), ALU.add).then_inc(S("mix0_h"), 1)

            def topk(l, t, tick=lambda n: None, part=0):
                H = 1 if t == 2 else PEER_H // 2 if (l, t) == (0, 0) else PEER_H
                h0 = H * part
                e = slice(16 * h0, 16 * (h0 + H))
                e2 = slice(32 * h0, 32 * (h0 + H))
                scores_ = s_m if t == 2 else s_sb0[t] if l == 0 else s_sb1
                scores_ = scores_[:, 256 * h0:256 * (h0 + H)]
                oh = oh0 if l == 0 else oh1
                steps = [0]

                def step(n=1):
                    steps[0] += n
                    tick(steps[0])

                s_ = scores_.rearrange("p (j n) -> p j n", n=128)
                tv_ = tv[:, e2].rearrange("p (j a) -> p j a", a=16)
                ti_ = ti[:, e2].rearrange("p (j a) -> p j a", a=16)
                tif_ = tif[:, e2].rearrange("p (j a) -> p j a", a=16)
                J = 2 * H

                def top16(n, val, idx, src, W_):
                    for j in range(n):
                        i = v.max(val[:, j, 0:8], src[:, j, :])
                        if j < n - 1:
                            step(W_)
                    link(i)
                    step(W_)
                    for j in range(n):
                        i = v.max_index(idx[:, j, 0:8], val[:, j, 0:8], src[:, j, :])
                        if j < n - 1:
                            step(W_)
                    link(i)
                    step(W_)
                    for j in range(n):
                        i = v.match_replace(src[:, j, :], val[:, j, 0:8], src[:, j, :], -3.0e38)
                        if j < n - 1:
                            step(W_)
                    link(i)
                    step(W_)
                    for j in range(n):
                        i = v.max(val[:, j, 8:16], src[:, j, :])
                        if j < n - 1:
                            step(W_)
                    link(i)
                    step(W_)
                    for j in range(n):
                        i = v.max_index(idx[:, j, 8:16], val[:, j, 8:16], src[:, j, :])
                        if j < n - 1:
                            step(W_)
                    link(i)
                    step(W_)

                top16(J, tv_, ti_, s_, 1)
                cand = (oh if t == 2 else scores_)[:, 0:256 * H]
                tv4 = tv_.rearrange("p (h s) a -> p h s a", s=2)
                link(v.tensor_tensor(cand.rearrange("p (h a b) -> p h a b", a=16, b=16),
                                     tv4[:, :, 0, :].unsqueeze(3).to_broadcast([128, H, 16, 16]),
                                     tv4[:, :, 1, :].unsqueeze(2).to_broadcast([128, H, 16, 16]), ALU.add))
                bv_ = bv[:, e].rearrange("p (h k) -> p h k", k=16)
                bp_ = bp[:, e].rearrange("p (h k) -> p h k", k=16)
                step(10)
                top16(H, bv_, bp_, cand.rearrange("p (h n) -> p h n", n=256), 2)
                G = gates[t][:, e]
                G3 = G.rearrange("p (h k) -> p h k", k=16)
                q = tk_number(l, t, part)
                v.tensor_tensor(G3, bv_, bv_[:, :, 0:1].to_broadcast([128, H, 16]), ALU.subtract)\
                    .then_inc(S("gx"), 1)
                n = 16 * H
                v.tensor_copy(tif[:, e2], ti[:, e2])
                v.tensor_scalar(pab[:, 0, e], bp[:, e], 4, None, ALU.logical_shift_right)
                link(v.tensor_scalar(pab[:, 1, e], bp[:, e], 15, None, ALU.bitwise_and))
                v.tensor_copy(sel_a[:, e], pab[:, 0, e])
                link(v.tensor_copy(sel_b[:, e], pab[:, 1, e]))
                o_ = oh[:, 0:16 * n].rearrange("p (m a) -> p m a", a=16)
                o4 = oh[:, 0:16 * n].rearrange("p (h k a) -> p h k a", k=16, a=16)
                tif4 = tif_.rearrange("p (h s) a -> p h s a", s=2)
                for half, (pos, res) in enumerate([(sel_a, ia), (sel_b, ib)]):
                    step(10)
                    link(v.tensor_tensor(o_, pos[:, e].unsqueeze(2).to_broadcast([128, n, 16]),
                                         cc("iota", 16).unsqueeze(1).to_broadcast([128, n, 16]), ALU.is_equal))
                    step(10)
                    link(v.tensor_tensor(o4, o4, tif4[:, :, half, :].unsqueeze(2).to_broadcast([128, H, 16, 16]),
                                         ALU.mult))
                    step(10)
                    link(v.tensor_reduce(res[:, e], o_, AX, ALU.add))
                link(v.tensor_scalar(ia[:, e], ia[:, e], 128.0, float(l * EXPERTS), ALU.mult, ALU.add))
                v.tensor_tensor(eidx[:, t, e], ia[:, e], ib[:, e], ALU.add).then_inc(S("eidx"), 1)
                dve.wait_ge(S("ge"), q)
                link(v.tensor_reduce(gm[:, h0:h0 + H], G3, AX, ALU.add))
                link(v.reciprocal(gs[:, h0:h0 + H], gm[:, h0:h0 + H]))
                link(v.tensor_tensor(G3, G3, gs[:, h0:h0 + H].unsqueeze(2).to_broadcast([128, H, 16]), ALU.mult))

            def dot(t, k, n, ufill):
                dve.wait_ge(S(f"u{k % NU}"), ufill)
                v.scalar_tensor_tensor(ug[:, k % NU, :], ug[:, k % NU, :], 1.0, hnm if t == 2 else hn[:, t, :],
                                       ALU.mult, ALU.mult, accum_out=dots[:, k % 8:k % 8 + 1]).then_inc(S("dot"), 1)

            def coef(t, k, n, gate):
                unit_mat, W = (cc("sel", 16), 16) if t == 2 else (ident, 128)
                dve.wait_ge(S("gelu"), n + 1)
                if not isinstance(n, int) or n >= 4:
                    dve.wait_ge(S("vsum"), n - 3)
                v.tensor_scalar(diag[:, k % 4, 0:W], unit_mat, gel[:, k % 8:k % 8 + 1], gate,
                                ALU.mult, ALU.mult).then_inc(S("diag"), 1)

            def straight(t, base):
                def slot(k):
                    if k < SLOTS:
                        dot(t, k, base + k, 16 * ((base + k) // NU + 1))
                    if k >= 2:
                        coef(t, k - 2, base + k - 2, gates[t][:, k - 2:k - 1])
                return slot

            def flush(t, base, n):
                for k in (n - 2, n - 1):
                    coef(t, k, base + k, gates[t][:, k:k + 1])

            def slots_loop(t, base, start=0):
                with dve.Fori(start // GB, SLOTS // GB) as i:
                    for k in range(GB):
                        dot(t, k, GB * i + (base + k), 16 * (GB // NU) * i + 16 * ((base + k) // NU + 1))
                        if k >= 2:
                            coef(t, k - 2, GB * i + (base + k - 2), gates[t][:, ds(GB * i + (k - 2), 1)])
                    for k in (GB - 2, GB - 1):
                        coef(t, k, GB * i + (base + k), gates[t][:, ds(GB * i + k, 1)])

            norm("f0", [0, 1, 2], 3, gain=bcF[:, :])
            dve.wait_ge(S("md"), 128)
            topk(0, 2)
            (_, m_base), (_, a_base), (_, b_base) = gathers(0)
            dve.wait_ge(S("md2"), 128)
            dve.wait_ge(S("sc0_ev"), 2)
            bg = Beside(straight(2, m_base))
            topk(0, 0, lambda n: bg.to(min(16, 16 * n / HALF_GATE_AT)))
            flush(2, m_base, 16)
            bg = Beside(straight(0, a_base))
            topk(0, 0, lambda n: bg.to(min(TOPK_A, TOPK_A * n / HALF_GATE_AT)), part=1)
            dve.wait_ge(S("sc0_ev"), 3)
            topk(0, 1, lambda n: bg.to(min(STRAIGHT, TOPK_A + (TOPK_B - TOPK_A) * n / GATE_AT)))
            bg.to(STRAIGHT)
            flush(0, a_base, STRAIGHT)
            slots_loop(0, a_base, STRAIGHT)

            def heads_norm(tag, tiles):
                for m, t in enumerate(tiles):
                    P = TILES[t][1]
                    link(v.tensor_tensor(sq[0:P, :], hT(t), hT(t), ALU.mult))
                    link(v.tensor_reduce(hsum[0:P, 16 * m:16 * m + 16], sq[0:P, :].rearrange("p (h e) -> p h e", e=64),
                                         AX, ALU.add))
                n = 16 * len(tiles)
                rstd(tag, hsum[:, 0:n], hsum[:, 0:n], 0, 64)
                for m, t in enumerate(tiles):
                    P = TILES[t][1]
                    x3 = hT(t).rearrange("p (h e) -> p h e", e=64)
                    v.tensor_tensor(x3, x3, hsum[0:P, 16 * m:16 * m + 16].unsqueeze(2).to_broadcast([P, 16, 64]),
                                    ALU.mult).then_inc(S("x_ready"), 1)

            def front(i, bg):
                X = "AB"[i]
                kvt = [0, 2] if i == 0 else [1]
                plan = PLAN[i]

                def at(stage, j=0, J=1):
                    a = plan[stage]
                    bg.to(a + (plan[STAGES[STAGES.index(stage) + 1]] - a) * j / J)

                if i == 0:
                    v.memset(kT[:, :, LTOK:384], 0.0)
                    v.memset(vk[:, 2, :], 0.0).then_inc(S("kv_zero"), 1)
                at("kv")
                norm("kv" + X, kvt, (6, 8)[i])
                t_out("kv" + X, kvt, "kvn", free=U0["wq"] + 16 if i == 0 else U0["wqA"] + 16, tb=4)
                at("v")
                dve.wait_ge(S("k_ev"), 2 + i)
                heads_norm("kh" + X, kvt)
                at("n1")
                dve.wait_ge(S("turned"), AT["kh" + X][3] + len(kvt))
                norm("n1" + X, [i], 9 + i)
                t_out("n1" + X, [i], "mix1", free=U0["v" + X] + 8, tb=4)
                at("qh")
                dve.wait_ge(S("q_ev"), i + 1)
                heads_norm("qh" + X, [i])
                stick(i, lambda p: at("stick", p, 8))
                at("f1")
                dve.wait_ge(S("w_used"), U0["o" + X] + 8)
                v.tensor_tensor(hh(i), hh(i), ps2(0), ALU.add).then_inc(S("wo_h"), 1)
                dve.wait_ge(S("ld_f1"), 16)
                norm("f1" + X, [i], 11 + i, gain=bcF[:, :])
                at("topk")
                dve.wait_ge(S("sc1_ev"), i + 1)
                topk(1, i, lambda n: at("topk", n, TOPK_STEPS))
                bg.to(SLOTS)

            def stick(i, tick):
                nk = 2 + i
                W = nk * 128
                valid = cc("valid", 384)[:, 384 - W:384].unsqueeze(1).to_broadcast([128, 2, W])

                def logits(p):
                    n = 8 * i + p
                    z_, t_ = st[:, p % 2, 0, 0:2 * W], st[:, p % 2, 1, 0:2 * W]
                    dve.wait_ge(S("z_pe"), n + 1)
                    if n >= 2:
                        dve.wait_ge(S("o_pe"), n - 1)
                    v.scalar_tensor_tensor(z_.rearrange("p (r w) -> p r w", r=2), ps[:, 0:2, 0:W], 0.125, valid,
                                           ALU.mult, ALU.add).then_inc(S("z_sb"), 1)
                    dve.wait_ge(S("z_sb"), n + 1)
                    v.scalar_tensor_tensor(t_, z_, -1.0, z_, ALU.mult, ALU.min).then_inc(S("tmin"), 1)

                logits(0)
                for p in range(8):
                    n = 8 * i + p
                    tick(p)
                    z_, t_ = st[:, p % 2, 0, 0:2 * W], st[:, p % 2, 1, 0:2 * W]
                    dve.wait_ge(S("ln"), n + 1)
                    v.scalar_tensor_tensor(t_, z_, 0.0, t_, ALU.max, ALU.add).then_inc(S("sp"), 1)
                    if p < 7:
                        logits(p + 1)
                    dve.wait_ge(S("c_pe"), n + 1)
                    v.tensor_tensor(z_.rearrange("p (r k n) -> p r k n", r=2, k=nk),
                                    z_.rearrange("p (r k n) -> p r k n", r=2, k=nk),
                                    ps2(2)[:, 0:2 * W].rearrange("p (k r n) -> p r k n", r=2, k=nk), ALU.subtract)\
                        .then_inc(S("dd"), 1)

            front(0, Beside(straight(1, b_base)))
            flush(1, b_base, SLOTS)
            (_, a_base), (_, b_base) = gathers(1)
            front(1, Beside(straight(0, a_base)))
            flush(0, a_base, SLOTS)
            slots_loop(1, b_base)

            dve.wait_ge(S("vsum"), 16 + 4 * SLOTS)
            norm("n2", [0, 1], 13)
            t_out("n2", [0, 1], "gmix", free=U0["wqB"] + 16)

            def x_low(k):
                for t in range(2):
                    e = slice(t * 128, (t + 1) * 128)
                    dve.wait_ge(S("x_high"), 2 * k + t + 1)
                    v.tensor_tensor(xL[:, :, e], xT[:, :, e], xH[:, :, e], ALU.subtract)\
                        .then_inc(S("x_low"), 1)

            x_low(0)
            dve.wait_ge(S("ld_m"), 80)
            norm("nm", [0, 1], 15, src=lambda t: mrg[:, t, :])
            dve.wait_ge(S("trev_pe"), 1)
            v.tensor_tensor(pw[0:8, 0, 0:384], ps[0:8, 6, 0:384], cs2c[0:8, CS2["future"]:CS2["future"] + 384],
                            ALU.add).then_inc(S("trev_sb"), 1)
            for t in range(2):
                dve.wait_ge(S("sg"), t + 1)
                v.tensor_tensor(vtok[:, 2, t, :], ps[:, 4 + t, :], vtok[:, 2, t, :], ALU.mult).then_inc(S("iv_ev"), 1)
            t_out("nm", [0, 1], "gmem", dst=memT)

            def c2(name, a=0, n=256):
                return cs2c[:, CS2[name] + a:CS2[name] + a + n]

            for j in range(8):
                x_ = qkT[:, 8 + j, :]
                k_ = "q" if j < 4 else "k"
                tmp = oh2[:, (j % 2) * 256:(j % 2) * 256 + 256]
                dve.wait_ge(S("sw_pe"), j + 1)
                v.tensor_tensor(tmp, ps[:, j % 2, 0:256], c2("sin" + k_), ALU.mult).then_inc(S("rot_ps"), 1)
                link(v.tensor_tensor(x_, x_, c2("cos" + k_), ALU.mult))
                v.tensor_tensor(x_, x_, tmp, ALU.add).then_inc(S("rot"), 1)
            for hd in range(4):
                dve.wait_ge(S("rs_pe"), hd + 1)
                v.tensor_tensor(mrg[:, hd // 2, (hd % 2) * 384:(hd % 2) * 384 + 384], ps[:, 2 + hd % 2, 0:384],
                                c2("decay", 384 * hd, 384), ALU.mult).then_inc(S("rs_sb"), 1)
            dve.wait_ge(S("ry_pe"), 4)
            y3 = hn[:, 0, :].rearrange("p (g e) -> p g e", e=128)
            q3 = hn[:, 1, :].rearrange("p (g e) -> p g e", e=128)
            mu = tsb[:, 8:16]
            var = tsb[:, 16:24]
            link(v.tensor_copy(hn[:, 0, :], ps2(6)))
            v.tensor_reduce(mu, y3, AX, ALU.add).then_inc(S("ry_ps"), 1)
            dve.wait_ge(S("ry_ps"), 1)
            link(v.tensor_scalar(mu, mu, -1.0 / 128, None, ALU.mult))
            link(v.tensor_tensor(y3, y3, mu.unsqueeze(2).to_broadcast([128, 8, 128]), ALU.add))
            link(v.tensor_tensor(q3, y3, y3, ALU.mult))
            link(v.tensor_reduce(var, q3, AX, ALU.add))
            rstd("ry", var, var, 0, 128)
            link(v.tensor_tensor(y3, y3, var.unsqueeze(2).to_broadcast([128, 8, 128]), ALU.mult))
            y4 = hn[:, 0, :].rearrange("p (t d) -> p t d", t=2)
            link(v.tensor_tensor(y4, y4, bcG[:, :].unsqueeze(1).to_broadcast([128, 2, 512]), ALU.mult))
            for t in range(2):
                v.tensor_tensor(y4[:, t, :], y4[:, t, :], vtok[:, 2, t, :], ALU.mult).then_inc(S("x_ready"), 1)

            dve.wait_ge(S("bias"), 1)

            def soft_l(n):
                p_ = pw[:, n % 2, :]
                col = 8 * (n % 2)
                dve.wait_ge(S("ss_pe"), n + 1)
                if n >= 2:
                    dve.wait_ge(S("pt_pe"), n - 1)
                if n < 8:
                    v.scalar_tensor_tensor(p_[:, 0:128], ps[:, n % 2, 0:128], 0.125, biasT[:, n, 128:256],
                                           ALU.mult, ALU.add)
                    v.scalar_tensor_tensor(p_[:, 128:384], ps[:, n % 2, 128:384], 0.125, biasT[:, n, :],
                                           ALU.mult, ALU.add).then_inc(S("ss_ps"), 1)
                    dve.wait_ge(S("ss_ps"), n + 1)
                    v.tensor_reduce(nmx[:, col:col + 1], p_[:, 0:128], AX, ALU.max, negate=True)
                    v.tensor_reduce(nmx[:, col + 1:col + 2], p_[:, 128:384], AX, ALU.max, negate=True)\
                        .then_inc(S("nmx"), 1)
                else:
                    link(v.tensor_reduce(nmx[:, col:col + 2], ps[:, n % 2, :].rearrange("p (t m) -> p t m", t=2),
                                         AX, ALU.max, negate=True))
                    v.tensor_scalar(nmx[:, col:col + 2], nmx[:, col:col + 2], RET_DK ** -0.5, None, ALU.mult)\
                        .then_inc(S("nmx"), 1)

            def soft_n(n):
                p_ = pw[:, n % 2, :]
                col = 8 * (n % 2)
                dve.wait_ge(S("pe_"), 2 * n + 2)
                i = v.reciprocal(nmx[:, col + 4:col + 6], nmx[:, col + 2:col + 4])
                if n >= 8:
                    i.then_inc(S("ss_ps"), 1)
                    dve.wait_ge(S("ss_ps"), n + 1)
                else:
                    link(i)
                for t, (a, b) in enumerate([(0, 128), (128, 384)] if n < 8 else [(0, 256), (256, 512)]):
                    i = v.tensor_scalar(p_[:, a:b], p_[:, a:b], nmx[:, col + 4 + t:col + 5 + t], None, ALU.mult)
                i.then_inc(S("pn"), 1)

            soft_l(0)
            for n in range(12):
                if n < 11:
                    soft_l(n + 1)
                soft_n(n)
            for k in range(3):
                dve.wait_ge(S("w_used"), U0["br"] + 4 * k + 4)
                dve.wait_ge(S("z_sig"), k + 1)
                for t in range(2):
                    P2 = ps2(4 * (k % 2) + 2 * t)
                    if k == 0:
                        v.tensor_tensor(mrg[:, t, :], P2, zs[:, k, t, :], ALU.mult).then_inc(S("br0_ps"), 1)
                    else:
                        v.tensor_tensor(zs[:, k, t, :], P2, zs[:, k, t, :], ALU.mult).then_inc(S(f"br{k}_ps"), 1)
                        dve.wait_ge(S(f"br{k}_ps"), t + 1)
                        i = v.tensor_tensor(mrg[:, t, :], mrg[:, t, :], zs[:, k, t, :], ALU.add)
                        if k == 2:
                            i.then_inc(S("x_ready"), 1)
                        else:
                            link(i)
                if k == 0:
                    dve.wait_ge(S("br0_ps"), 2)
            add_h(U0["out"] + 8, "out_h", [0, 1])
            norm("n3", [0, 1], 17)
            t_out("n3", [0, 1], "gffn")
            x_low(1)

            def a_low(j):
                dve.wait_ge(S("a_high"), j + 1)
                v.tensor_tensor(aL[:, j, :], aT[:, j % 2, :], aH[:, j, :], ALU.subtract)\
                    .then_inc(S("a_low"), 1)

            v.memset(up_in[:, :, :, 0:2], 0.0).then_inc(S("padded"), 1)
            for j in range(FFC):
                for k in range(2):
                    x_ = up_in[:, j % 2, k, :]
                    y_ = up_cv[:, j % 2, k, :]
                    m = k * FFC + j
                    w_ = [colc[:, COL["convw"] + 44 * i + m:COL["convw"] + 44 * i + m + 1] for i in range(3)]
                    dve.wait_ge(S("up_ev"), 2 * j + k + 1)
                    link(v.tensor_scalar(y_, x_[:, 0:256], w_[0], gcol("convb", m), ALU.mult, ALU.add))
                    link(v.scalar_tensor_tensor(y_, x_[:, 1:257], w_[1], y_, ALU.mult, ALU.add))
                    v.scalar_tensor_tensor(y_, x_[:, 2:258], w_[2], y_, ALU.mult, ALU.add).then_inc(S("cv"), 1)
                dve.wait_ge(S("gate"), j + 1)
                dve.wait_ge(S("cv"), 2 * j + 2)
                v.tensor_tensor(aT[:, j % 2, :], up_cv[:, j % 2, 0, :], up_cv[:, j % 2, 1, :], ALU.mult)\
                    .then_inc(S("a_T"), 1)
                if j:
                    a_low(j - 1)
            a_low(FFC - 1)
            add_h(U0["down"] + 22, "down_h", [0, 1])
            rstd("n4", ss[:, 19:21], rs[:, 19:21], 2, D)
            dve.wait_ge(S("ld_g"), 16)
            for t in range(2):
                v.scalar_tensor_tensor(hn[:, t, :], h[:, t, :], rs[:, 19 + t:20 + t], bcL, ALU.mult, ALU.mult)\
                    .then_inc(S("fin"), 1)


def _t(w):
    J = w.shape[1] // 128
    return w.reshape(8, 128, J, 128).transpose(2, 1, 0, 3).reshape(J, 128, 1024)


def _n(w):
    return w.reshape(-1, 128, 1024)


def _n2(w):
    return w.reshape(4, 2, 128, 512).transpose(0, 2, 1, 3).reshape(4, 128, 1024)


def _pack_units(a):
    w_in, w_up = a["w_in_2"][0], a["w_up_2"][0]
    o = [0, 512, 1024, 1536, 2048, 2560, 3072, 3584, 4096, 5120, 6144, 7168]
    qa, ka, va, qr, kr, vr, gr, qm, za, zr, zm = [w_in[:, o[i]:o[i + 1]] for i in range(11)]
    up = np.stack([_t(w_up[:, :DFF]), _t(w_up[:, DFF:])], axis=1).reshape(-1, 128, 1024)
    keys = [a["peer_keys"][l].reshape(2, 8, 128, 128).transpose(0, 3, 1, 2).reshape(2, 128, 1024) for l in range(2)]
    kv, wq = a["w_kv"], a["peer_wq"]
    front = [_n(kv[:, :D]), _n(kv[:, D:]), _n(a["w_q"][0]), _n(a["w_o"][0]), _t(wq[1]), keys[1]]
    parts = [
        a["pool_w"][0].reshape(2, 2, 2, 128, 256).transpose(0, 3, 1, 2, 4).reshape(2, 128, 1024),
        _t(wq[0]), keys[0], *front, *front,
        _t(qa), _t(ka), _t(qr), _t(kr), _t(qm), _n2(va), _n2(vr), _n2(gr),
        _t(a["w_mem_kv_2"][0][:, :512]), _n2(a["w_mem_kv_2"][0][:, 512:]),
        *[_n2(z[:, o_:o_ + 512]) for z in (za, zr, zm) for o_ in (0, 512)],
        _n(a["w_br_attn_2"][0]), _n(a["w_br_ret_2"][0]), _n(a["w_br_mem_2"][0]), _n(a["w_out_2"][0]), up,
        _n(a["w_down_2"][0])]
    return np.ascontiguousarray(np.concatenate(parts, axis=0))


def _cols(v):
    return v.reshape(-1, 128).T


def _pack_cols(a):
    two = lambda g: np.concatenate([g, g]).reshape(128, 1)
    cw = a["conv_w_2"][0]
    return np.ascontiguousarray(np.concatenate(
        [_cols(a["norm_mix"][0]), _cols(a["norm_mix"][1]), _cols(a["kv_norm"]), _cols(a["g_mix_2"][0]),
         _cols(a["g_mem_2"][0]), _cols(a["g_ffn_2"][0]), two(a["k_norm"]), two(a["q_norm"][0]),
         _cols(a["conv_b_2"][0]), _cols(cw[0]), _cols(cw[1]), _cols(cw[2])], axis=1))


def _constants():
    f = np.float32
    i = np.arange(128)
    valid = np.zeros((128, 384), f)
    future = np.where(i[:, None] < i[None, :], 0.0, NEG)
    valid[:, 128:256] = future
    valid[META:, 256:384] = NEG
    c1 = [np.eye(128), (i[:, None] >= i[None, :]), np.ones((128, 128)), np.tile(np.arange(16), (128, 1)),
          (i[:, None] % META == np.arange(META)[None, :]), valid]
    cst = np.concatenate([np.asarray(x, f) for x in c1], axis=1)

    half = RET_DK // 2
    swap = np.roll(np.eye(128), half, axis=1)
    inv = f(10000.0) ** (-np.arange(half, dtype=f) / f(half))
    ang = (np.arange(SEQ, dtype=f)[None, :] * inv[:, None]).astype(f)
    cos = np.concatenate([np.cos(ang), np.cos(ang)]).astype(f)
    sin = np.concatenate([-np.sin(ang), np.sin(ang)]).astype(f)
    scale = f(RET_DK ** -0.5)
    decay = np.zeros((128, 4, 384))
    for hd in range(4):
        lg = np.log1p(-2.0 ** (-5.0 - hd))
        for a, (j0, i0, n) in {0: (0, 0, 256), 256: (128, 128, 128)}.items():
            diff = (i0 + np.arange(n))[None, :] - (j0 + i)[:, None]
            decay[:, hd, a:a + n] = np.where(diff >= 0, np.exp(lg * np.maximum(diff, 0)), 0.0)
    dist = 255 - np.arange(384)
    d = np.maximum(dist, 1).astype(f)
    large = 16 + (np.log(d / f(16)) / f(np.log(2048 / 16)) * f(16)).astype(np.int32)
    bucket = np.where(dist < 16, np.maximum(dist, 0), np.minimum(large, 31))
    hot = np.zeros((128, 384))
    hot[bucket, np.arange(384)] = 1.0
    fut = np.zeros((128, 384))
    fut[:, dist < 0] = NEG
    cs2 = np.concatenate([np.asarray(x, f) for x in
                          [swap, np.eye(128)[::-1], cos, sin, cos * scale, sin * scale, decay.reshape(128, -1), hot, fut]], axis=1)

    order = np.concatenate([np.arange(META, LTOK), np.arange(META)])
    pool = np.zeros((4, LTOK, LTOK))
    for g, w in enumerate((2, 4, 8, 16)):
        for t in range(LTOK):
            lo = max(0, t - w + 1)
            pool[g, lo:t + 1, t] = 1.0 / min(t + 1, w)
            pool[g, t, t] -= 1.0
    pool = pool[:, order][:, :, order]
    poolm = np.zeros((128, 4, 3, LTOK), f)
    for s, (c0, P) in enumerate(TILES):
        poolm[0:P, :, s, :] = pool[:, c0:c0 + P, :].transpose(1, 0, 2)
    return cst, cs2, poolm.reshape(128, -1)


def kernel(**inputs):
    import concourse.bacc as bacc
    from concourse.bass_utils import run_bass_kernel_spmd

    a = {k: np.asarray(v) for k, v in inputs.items()}
    cst, cs2, poolm = _constants()
    bc = np.zeros((5, D), np.float32)
    bc[0], bc[1], bc[2] = a["norm_ffn"][0], a["norm_ffn"][1], a["pool_scale"][0]
    bc[3, 0:512], bc[4] = a["ret_gn_gain_2"][0], a["g_final_2"]
    arrays = {
        "xin": a["x"][0], "metain": a["meta_tokens"], "units": _pack_units(a), "cols": _pack_cols(a),
        "cst": cst, "cs2": cs2, "poolm": poolm, "bc_rows": bc,
        "peer_u": a["peer_u"].reshape(2 * EXPERTS, D), "peer_v": a["peer_v"].reshape(2 * EXPERTS, D),
        "mem": a["mem_2"][0], "rel": a["rel_bias_2"]}
    arrays = {k: np.ascontiguousarray(v) for k, v in arrays.items()}
    nc = bacc.Bacc("TRN2", target_bir_lowering=False, num_devices=1)
    args = [nc.dram_tensor("in_" + k, v.shape, mybir.dt.from_np(v.dtype), kind="ExternalInput").ap()
            for k, v in arrays.items()]
    args.append(nc.dram_tensor("result", (SEQ, D), mybir.dt.float32, kind="ExternalOutput").ap())
    program(nc, *args)
    r = run_bass_kernel_spmd(nc, [{"in_" + k: v for k, v in arrays.items()}], core_ids=[0])
    return r.results[0]["result"].reshape(1, SEQ, D)
```
